# Optimizing a Trainium2 kernel written in Bass

```python
import math
import jax, jax.numpy as jnp
from jax import lax
import numpy as np

D_MODEL = 1024
BATCH = 1
SEQ = 1024
DEPTH = 1
DEC_BATCH = 8
DEC_SEQ = 4
PAST_LEN = 1024
PAGE_SIZE = 128

SWA_HEADS = 8
SWA_KV_HEADS = 2
SWA_HEAD_DIM = 64
SWA_GROUP = SWA_HEADS // SWA_KV_HEADS
SWA_WIDTH = SWA_HEADS * SWA_HEAD_DIM
KV_WIDTH = SWA_KV_HEADS * SWA_HEAD_DIM
WINDOW = 128
SWA_SCALE = SWA_HEAD_DIM ** -0.5
CHUNK = 128
CHUNK_GROUPS = 4
CHUNK_GROUP_DIM = 128
CHUNK_WIDTH = CHUNK_GROUPS * CHUNK_GROUP_DIM
MEM_LEN = 256
MEM_HEADS = 4
MEM_HEAD_DIM = 128
MEM_WIDTH = MEM_HEADS * MEM_HEAD_DIM
MEM_SCALE = MEM_HEAD_DIM ** -0.5
N_BRANCH = 3
BRANCH_WIDTH = 512
IN_WIDTH = SWA_WIDTH + 2 * KV_WIDTH + 2 * CHUNK_WIDTH + MEM_WIDTH + N_BRANCH * D_MODEL
PEER_HEADS = 8
PEER_N_KEYS = 128
PEER_N_EXPERTS = PEER_N_KEYS * PEER_N_KEYS
PEER_QUERY_DIM = 256
PEER_HALF = PEER_QUERY_DIM // 2
PEER_TOPK = 16
PEER_BLOCK = 128

EPS = 1e-6
NEG = -1e30

kernel_name = 'gated_chunkmlp_swa_mem_peer_step'

def rmsnorm(x, g):
    xf = x.astype(jnp.float32)
    xf = xf * lax.rsqrt(jnp.mean(xf * xf, axis=-1, keepdims=True) + EPS)
    return xf.astype(x.dtype) * g

def alibi_slopes():
    h = jnp.arange(1, SWA_HEADS + 1, dtype=jnp.float32)
    return jnp.exp2(-8.0 * h / SWA_HEADS).reshape(SWA_KV_HEADS, SWA_GROUP)

def sink_softmax(scores, sinks):
    m = jnp.maximum(jnp.max(scores, axis=-1, keepdims=True), sinks)
    e = jnp.exp(scores - m)
    return e / (jnp.sum(e, axis=-1, keepdims=True) + jnp.exp(sinks - m))

def in_proj(xn, p):
    B, T, _ = xn.shape
    proj = xn @ p['w_in']
    o1 = SWA_WIDTH
    o2 = o1 + KV_WIDTH
    o3 = o2 + KV_WIDTH
    o4 = o3 + 2 * CHUNK_WIDTH
    o5 = o4 + MEM_WIDTH
    q, k, v, uv, qm, gl = jnp.split(proj, [o1, o2, o3, o4, o5], axis=-1)
    u, vc = jnp.split(jax.nn.gelu(uv, approximate=False), 2, axis=-1)
    vc = rmsnorm(vc, p['chunk_norm_g'])
    return (q.reshape(B, T, SWA_KV_HEADS, SWA_GROUP, SWA_HEAD_DIM),
            k.reshape(B, T, SWA_KV_HEADS, SWA_HEAD_DIM),
            v.reshape(B, T, SWA_KV_HEADS, SWA_HEAD_DIM),
            u.reshape(B, T, CHUNK_GROUPS, CHUNK_GROUP_DIM),
            vc.reshape(B, T, CHUNK_GROUPS, CHUNK_GROUP_DIM),
            qm.reshape(B, T, MEM_HEADS, MEM_HEAD_DIM),
            gl.reshape(B, T, N_BRANCH, D_MODEL))

def swa_prompt(q, k, v, sinks):
    B, S = q.shape[:2]
    nb = S // WINDOW
    qb = q.reshape(B, nb, WINDOW, SWA_KV_HEADS, SWA_GROUP, SWA_HEAD_DIM)

    def band(t):
        tp = jnp.pad(t, ((0, 0), (WINDOW, 0), (0, 0), (0, 0)))
        tp = tp.reshape(B, nb + 1, WINDOW, SWA_KV_HEADS, SWA_HEAD_DIM)
        return jnp.concatenate([tp[:, :-1], tp[:, 1:]], axis=2)

    kb, vb = band(k), band(v)
    s = jnp.einsum('bnqkgd,bnskd->bnkgqs', qb, kb).astype(jnp.float32) * SWA_SCALE
    r = jnp.arange(WINDOW)
    c = jnp.arange(2 * WINDOW)
    dist = WINDOW + r[:, None] - c[None, :]
    key_pos = jnp.arange(nb)[:, None] * WINDOW - WINDOW + c[None, :]
    valid = ((dist >= 0) & (dist <= WINDOW))[None] & (key_pos >= 0)[:, None, :]
    s = s - alibi_slopes()[:, :, None, None] * dist.astype(jnp.float32)
    s = jnp.where(valid[None, :, None, None], s, NEG)
    w = sink_softmax(s, sinks.astype(jnp.float32).reshape(SWA_KV_HEADS, SWA_GROUP)[:, :, None, None])
    o = jnp.einsum('bnkgqs,bnskd->bnqkgd', w.astype(vb.dtype), vb)
    return o.reshape(B, S, SWA_WIDTH)

def swa_sample(q, k, v, ck, cv, sinks):
    Bd, T = q.shape[:2]
    kk = jnp.concatenate([ck, k], axis=1)
    vv = jnp.concatenate([cv, v], axis=1)
    s = jnp.einsum('btkgd,bskd->bkgts', q, kk).astype(jnp.float32) * SWA_SCALE
    dist = (WINDOW + jnp.arange(T))[:, None] - jnp.arange(WINDOW + T)[None, :]
    valid = (dist >= 0) & (dist <= WINDOW)
    s = s - alibi_slopes()[:, :, None, None] * dist.astype(jnp.float32)
    s = jnp.where(valid, s, NEG)
    w = sink_softmax(s, sinks.astype(jnp.float32).reshape(SWA_KV_HEADS, SWA_GROUP)[:, :, None, None])
    o = jnp.einsum('bkgts,bskd->btkgd', w.astype(vv.dtype), vv).reshape(Bd, T, SWA_WIDTH)
    return o, kk[:, T:], vv[:, T:]

def spatial_gate(u, v, ws, bs):
    L = u.shape[2]
    w = jnp.tril(ws[:, :L, :L])
    s = jnp.einsum('gts,bnsgc->bntgc', w, v) + bs[:, :L].T[None, None, :, :, None]
    return u * s

def mem_kv(mem, p):
    B, M, _ = mem.shape
    kv = rmsnorm(mem, p['mem_norm_g']) @ p['w_mem_kv']
    k, v = jnp.split(kv, 2, axis=-1)
    return (k.reshape(B, M, MEM_HEADS, MEM_HEAD_DIM), v.reshape(B, M, MEM_HEADS, MEM_HEAD_DIM))

def mem_attn(q, k, v):
    B, T = q.shape[:2]
    s = jnp.einsum('bthd,bmhd->bhtm', q, k).astype(jnp.float32) * MEM_SCALE
    w = jax.nn.softmax(s, axis=-1)
    return jnp.einsum('bhtm,bmhd->bthd', w.astype(v.dtype), v).reshape(B, T, MEM_WIDTH)

def peer(xn, p):
    B, T, D = xn.shape
    n = B * T
    nblk = -(-n // PEER_BLOCK)
    flat = jnp.pad(xn.reshape(n, D), ((0, nblk * PEER_BLOCK - n), (0, 0))).reshape(nblk, PEER_BLOCK, D)
    wq, sub, pu, pv = p['peer_wq'], p['peer_subkeys'], p['peer_u'], p['peer_v']

    def one(xb):
        t = xb.shape[0]
        q = (xb @ wq).reshape(t, PEER_HEADS, 2, PEER_HALF)
        s = jnp.einsum('thpd,pkd->thpk', q, sub).astype(jnp.float32)
        sv, si = lax.top_k(s, PEER_TOPK)
        cand = (sv[:, :, 0, :, None] + sv[:, :, 1, None, :]).reshape(t, PEER_HEADS, PEER_TOPK * PEER_TOPK)
        cv, ci = lax.top_k(cand, PEER_TOPK)
        e = (jnp.take_along_axis(si[:, :, 0], ci // PEER_TOPK, axis=-1) * PEER_N_KEYS
             + jnp.take_along_axis(si[:, :, 1], ci % PEER_TOPK, axis=-1))
        g = jax.nn.softmax(cv, axis=-1)
        a = jax.nn.gelu(jnp.einsum('td,thkd->thk', xb, pu[e]), approximate=False)
        return jnp.einsum('thk,thkd->td', g.astype(xb.dtype) * a, pv[e])

    out = lax.map(one, flat).reshape(nblk * PEER_BLOCK, D)[:n]
    return out.reshape(B, T, D)

def merge_and_channel(x, a_swa, a_chunk, a_mem, gl, p):
    br = jnp.stack([a_swa, a_chunk, a_mem], axis=2)
    proj = jnp.einsum('btjc,jcd->btjd', br, p['w_branch_out'])
    gate = jax.nn.sigmoid(gl + p['b_gate'])
    h = x + jnp.sum(gate * proj, axis=2) @ p['w_out']
    return h + peer(rmsnorm(h, p['norm2_g']), p)

def layer_prompt(x, mem, p):
    B, S, _ = x.shape
    q, k, v, u, vc, qm, gl = in_proj(rmsnorm(x, p['norm1_g']), p)
    a_swa = swa_prompt(q, k, v, p['swa_sinks'])
    nc = S // CHUNK
    a_chunk = spatial_gate(u.reshape(B, nc, CHUNK, CHUNK_GROUPS, CHUNK_GROUP_DIM),
                           vc.reshape(B, nc, CHUNK, CHUNK_GROUPS, CHUNK_GROUP_DIM),
                           p['chunk_ws'], p['chunk_bs']).reshape(B, S, CHUNK_WIDTH)
    mk, mv = mem_kv(mem, p)
    a_mem = mem_attn(qm, mk, mv)
    y = merge_and_channel(x, a_swa, a_chunk, a_mem, gl, p)
    return y, k[:, -WINDOW:], v[:, -WINDOW:], mk, mv

def layer_sample(x, ck, cv, cmk, cmv, p):
    Bd, T, _ = x.shape
    q, k, v, u, vc, qm, gl = in_proj(rmsnorm(x, p['norm1_g']), p)
    a_swa, nk, nv = swa_sample(q, k, v, ck, cv, p['swa_sinks'])
    a_chunk = spatial_gate(u[:, None], vc[:, None], p['chunk_ws'], p['chunk_bs'])[:, 0].reshape(Bd, T, CHUNK_WIDTH)
    a_mem = mem_attn(qm, cmk, cmv)
    y = merge_and_channel(x, a_swa, a_chunk, a_mem, gl, p)
    return y, nk, nv, vc

def setup_inputs(seed: int = 0) -> dict:
    key = jax.random.key(seed)
    ks = jax.random.split(key, 24)
    nrm = jax.random.normal
    f32 = jnp.float32
    return {
        'x_prompt': nrm(ks[0], (BATCH, SEQ, D_MODEL), f32),
        'x_sample': nrm(ks[1], (DEC_BATCH, DEC_SEQ, D_MODEL), f32),
        'cache_swa_k': nrm(ks[2], (DEPTH, DEC_BATCH, WINDOW, SWA_KV_HEADS, SWA_HEAD_DIM), f32),
        'cache_swa_v': nrm(ks[3], (DEPTH, DEC_BATCH, WINDOW, SWA_KV_HEADS, SWA_HEAD_DIM), f32),
        'cache_mem_k': nrm(ks[4], (DEPTH, DEC_BATCH, MEM_LEN, MEM_HEADS, MEM_HEAD_DIM), f32),
        'cache_mem_v': nrm(ks[5], (DEPTH, DEC_BATCH, MEM_LEN, MEM_HEADS, MEM_HEAD_DIM), f32),
        'mem_prompt': nrm(ks[6], (BATCH, MEM_LEN, D_MODEL), f32),
        'norm1_g': 1.0 + 0.05 * nrm(ks[7], (DEPTH, D_MODEL), f32),
        'w_in': nrm(ks[8], (DEPTH, D_MODEL, IN_WIDTH), f32) * D_MODEL ** -0.5,
        'b_gate': 0.01 * nrm(ks[9], (DEPTH, N_BRANCH, D_MODEL), f32),
        'swa_sinks': 0.5 * nrm(ks[10], (DEPTH, SWA_HEADS), f32),
        'chunk_norm_g': 1.0 + 0.05 * nrm(ks[11], (DEPTH, CHUNK_WIDTH), f32),
        'chunk_ws': nrm(ks[12], (DEPTH, CHUNK_GROUPS, CHUNK, CHUNK), f32) * CHUNK ** -0.5,
        'chunk_bs': 1.0 + 0.1 * nrm(ks[13], (DEPTH, CHUNK_GROUPS, CHUNK), f32),
        'mem_norm_g': 1.0 + 0.05 * nrm(ks[14], (DEPTH, D_MODEL), f32),
        'w_mem_kv': nrm(ks[15], (DEPTH, D_MODEL, 2 * MEM_WIDTH), f32) * D_MODEL ** -0.5,
        'w_branch_out': nrm(ks[16], (DEPTH, N_BRANCH, BRANCH_WIDTH, D_MODEL), f32) * BRANCH_WIDTH ** -0.5,
        'w_out': nrm(ks[17], (DEPTH, D_MODEL, D_MODEL), f32) * D_MODEL ** -0.5,
        'norm2_g': 1.0 + 0.05 * nrm(ks[18], (DEPTH, D_MODEL), f32),
        'peer_wq': nrm(ks[19], (DEPTH, D_MODEL, PEER_HEADS * PEER_QUERY_DIM), f32) * D_MODEL ** -0.5,
        'peer_subkeys': nrm(ks[20], (DEPTH, 2, PEER_N_KEYS, PEER_HALF), f32) * PEER_HALF ** -0.5,
        'peer_u': nrm(ks[21], (DEPTH, PEER_N_EXPERTS, D_MODEL), f32) * D_MODEL ** -0.5,
        'peer_v': nrm(ks[22], (DEPTH, PEER_N_EXPERTS, D_MODEL), f32) * D_MODEL ** -0.5,
        'final_norm_g': 1.0 + 0.05 * nrm(ks[23], (D_MODEL,), f32),
    }

def reference(x_prompt, x_sample, cache_swa_k, cache_swa_v, cache_mem_k, cache_mem_v, mem_prompt,
              norm1_g, w_in, b_gate, swa_sinks, chunk_norm_g, chunk_ws, chunk_bs, mem_norm_g, w_mem_kv,
              w_branch_out, w_out, norm2_g, peer_wq, peer_subkeys, peer_u, peer_v, final_norm_g):
    hp, hs = x_prompt, x_sample
    kp_l, vp_l, mkp_l, mvp_l, ks_l, vs_l, cv_l = [], [], [], [], [], [], []
    for l in range(DEPTH):
        p = {'norm1_g': norm1_g[l], 'w_in': w_in[l], 'b_gate': b_gate[l], 'swa_sinks': swa_sinks[l],
             'chunk_norm_g': chunk_norm_g[l], 'chunk_ws': chunk_ws[l], 'chunk_bs': chunk_bs[l],
             'mem_norm_g': mem_norm_g[l], 'w_mem_kv': w_mem_kv[l], 'w_branch_out': w_branch_out[l],
             'w_out': w_out[l], 'norm2_g': norm2_g[l], 'peer_wq': peer_wq[l],
             'peer_subkeys': peer_subkeys[l], 'peer_u': peer_u[l], 'peer_v': peer_v[l]}
        hp, kp, vp, mkp, mvp = layer_prompt(hp, mem_prompt, p)
        hs, ksn, vsn, cvs = layer_sample(hs, cache_swa_k[l], cache_swa_v[l], cache_mem_k[l], cache_mem_v[l], p)
        kp_l.append(kp)
        vp_l.append(vp)
        mkp_l.append(mkp)
        mvp_l.append(mvp)
        ks_l.append(ksn)
        vs_l.append(vsn)
        cv_l.append(cvs)
    y_prompt = rmsnorm(hp, final_norm_g)
    y_sample = rmsnorm(hs, final_norm_g)
    return (y_prompt, y_sample, jnp.stack(kp_l), jnp.stack(vp_l), jnp.stack(mkp_l), jnp.stack(mvp_l),
            jnp.stack(ks_l), jnp.stack(vs_l), jnp.stack(cv_l))


_drawn_inputs = setup_inputs


def setup_inputs(seed=0):
    import zlib

    import numpy as np

    out = dict(_drawn_inputs(seed))
    spreads = {}
    factors = {'b_gate': 8.0,
     'swa_sinks': 3.959,
     'norm2_g': 8.0,
     'peer_wq': 4.011,
     'peer_subkeys': 4.015,
     'peer_u': 4.52,
     'peer_v': 4.025}
    for name, (base, spread) in spreads.items():
        noise = np.random.default_rng([zlib.crc32(name.encode()), seed]).standard_normal(out[name].shape)
        drawn = base * np.exp(spread * noise) if base else spread * noise
        out[name] = __import__('jax').numpy.asarray(drawn.astype(out[name].dtype))
    for name, factor in factors.items():
        out[name] = (out[name] * factor).astype(out[name].dtype)
    return out
```

```python
from contextlib import ExitStack, contextmanager

import numpy as np

import concourse.bass as bass
from concourse import mybir

F32, U32, BF16 = mybir.dt.float32, mybir.dt.uint32, mybir.dt.bfloat16
ALU = mybir.AluOpType
ACT = mybir.ActivationFunctionType
AX = mybir.AxisListType

P = 128
D = 1024
DC = D // P
PROMPT = 1024
B, T = 8, 4
SAMPLE = B * T
TOKENS = PROMPT + SAMPLE
PTILES = PROMPT // P
TILES = PTILES + 1
PADDED = TILES * P
THIRD = TOKENS // 3
HD = 64
KV = 2
GQ = 4
HEADS = KV * GQ
KVW = KV * HD
WINDOW = 128
SWA_SCALE = HD ** -0.5
CG = 4
CW = CG * P
MEM = 256
MT = MEM // P
MH = 4
MW = MH * P
MEM_SCALE = P ** -0.5
NBR = 3
BC = 4
EPS = 1e-6
NEG = -1e30
PH = 8
K = 16
NK = 128
EXPERTS = NK * NK
PAIRS = PH // 2
SLOTS = PH * K
NB = 4
OPEN = 8
PER_PAIR = (SLOTS // NB - OPEN) // PAIRS
BATCHES = SLOTS // NB
STAGES = 2 + 2 * PAIRS
ARENA = 52400
LOWEST = -3.0e38

FQ, FM, FK, FU = 0, GQ, GQ + MH, GQ + MH + 1
FEATS = FU + CG


class Steps:

    def __init__(self, eng, sem):
        self.eng, self.sem, self.base, self.n = eng, sem, 0, 0
        self.last = None

    def add(self, ins, signal=None, after=None):
        if signal is not None:
            self.last = (signal, after)
            return ins.then_inc(signal, 1)
        self.last = None
        self.n += 1
        return ins.then_inc(self.sem, 1)

    def settle(self):
        if self.last:
            assert self.last[1] is not None
            self.eng.wait_ge(*self.last)
        elif not isinstance(self.base, int) or self.base + self.n:
            self.eng.wait_ge(self.sem, self.base + self.n)

    @contextmanager
    def loop(self, first, end, per):
        with self.eng.Fori(first, end) as i:
            start, outer = self.n, self.base
            self.base, self.last = outer + i * per - first * per, None
            yield i
            assert self.n - start == per, (self.n - start, per)
            self.base, self.last = outer, None
        self.n = start + (end - first) * per


def build(nc, t):
    ctx = ExitStack()
    with ctx:
        def sem(name):
            return ctx.enter_context(nc.semaphore(name))

        ps = ctx.enter_context(nc.psum_tensor("ps", [P, 8, 512], F32))

        def keep(name, shape, dt=F32):
            return ctx.enter_context(nc.sbuf_tensor(f"{name}_sb", [P, *shape], dt))

        ident = keep("ident", [P])
        nothing = keep("nothing", [512], BF16)
        norm1_col, mem_norm_col = keep("norm1_col", [DC]), keep("mem_norm_col", [DC])
        eps = keep("eps", [1])
        stat = keep("stat", [16])
        iota16 = keep("iota16", [K])
        arena = keep("arena", [ARENA])

        class Region:

            def __init__(self, at=0):
                self.at = at

            def take(self, *shape, dt=F32):
                n = int(np.prod(shape)) // (2 if dt == BF16 else 1)
                a = arena[:, self.at:self.at + n]
                self.at += n
                assert self.at <= ARENA, self.at
                if dt != F32:
                    a = a.bitcast(dt)
                names = "abcd"[:len(shape)]
                if len(shape) > 1:
                    kw = {names[k]: shape[k] for k in range(1, len(shape))}
                    a = a.rearrange(f"p ({' '.join(names)}) -> p {' '.join(names)}", **kw)
                return a

        r = Region()
        xnT = r.take(DC, PADDED)
        feats_at = r.at
        feats = r.take(FEATS, PADDED)
        spT = r.take(CG, PADDED)
        v_nat = r.take(TILES, KVW)
        mkT = r.take(MH, MEM)
        mv = r.take(MT, MW)
        w_ring = r.take(NBR, DC + BC, P)
        swa_bias = r.take(HEADS, 2 * P)
        smp_bias = r.take(KV, P + SAMPLE)
        chunk_g = r.take(CW)
        chunk_b = r.take(CG, P)
        chunk_b_smp = r.take(CG, SAMPLE)
        ws_T = r.take(CG, P)
        ws_T_smp = r.take(CG, SAMPLE)
        gate_b = r.take(DC * NBR)
        sinks = r.take(HEADS)
        smp_sinks = r.take(KV)
        knat = r.take(2, KVW)
        row = r.take(8, HEADS)
        temps_at = r.at
        a = Region(feats_at)
        w_vvc = a.take(DC, KVW + CW)
        w_mem = a.take(DC, 2 * MW)
        assert a.at <= feats_at + FEATS * PADDED
        a = Region(temps_at)
        x_t = a.take(D)
        xs = a.take(D)
        squares = a.take(D)
        xn_tile = a.take(DC, P)
        vc_gelu = a.take(CW)
        vc_n = a.take(CW)
        vc_squares = a.take(CW)
        mk_nat = a.take(MT, MW)
        c = Region(temps_at)
        qs = c.take(FK, P)
        ks = c.take(2 * P)
        vs = c.take(2, KVW)
        sc = c.take(HEADS, 2 * P)
        scT = c.take(KV, 2, GQ, P)
        msc = c.take(MH, MEM)
        mscT = c.take(MH, MT, P)
        s = Region(temps_at)
        kcT = s.take(B, P)
        cv = s.take(B, KVW)
        smp_sT = s.take(KV, P)
        smp_snT = s.take(KV, P)
        smp_s = s.take(KV, P + SAMPLE)
        smp_pT = s.take(KV, P)
        smp_pnT = s.take(KV, P)
        smp_mT = s.take(MT, P)
        smp_m = s.take(MEM)
        smp_mpT = s.take(MT, P)
        d = Region(temps_at)
        sig = d.take(TOKENS)
        prod = d.take(TOKENS)
        merged = d.take(PADDED)
        e = Region()
        w_out = e.take(DC, D)
        w_q = e.take(DC, PH * 2 * P)
        subT = e.take(2, NK)
        u_ring = e.take(2, NB, D)
        v_ring = e.take(NB, D)
        m_tile = e.take(DC, P)
        h_next, h_cur = e.take(D), e.take(D)
        n2_next, n2_cur = e.take(D), e.take(D)
        n2T = e.take(DC, P)
        dump, u_dump = e.take(D, dt=BF16), e.take(D)
        y = e.take(D)
        norm2_g, final_g = e.take(D), e.take(D)
        q_nat = e.take(4 * P)
        qT = e.take(4, P)
        rest = e.take(4, NK)
        sv = e.take(4, K)
        si = e.take(4, K, dt=U32)
        sif = e.take(4, K)
        cand = e.take(2, K * K)
        cand2 = rest.rearrange("p (h k) n -> p h (k n)", h=2)
        cv16 = e.take(2, K)
        ci16 = e.take(2, K, dt=U32)
        hilo = e.take(2, 2, K, dt=U32)
        hilof = e.take(2, 2, K)
        match = cand.rearrange("p h (k a) -> p h k a", k=K)
        picked = e.take(2, 2, K)
        shifted = e.take(2, K)
        raised = e.take(2, K)
        g_next, g_cur = e.take(SLOTS), e.take(SLOTS)
        i_next, i_cur = e.take(SLOTS, dt=U32), e.take(SLOTS, dt=U32)
        stage_open = e.take(OPEN * NB, dt=U32)
        stage_pair = e.take(2, PER_PAIR // 2 * NB, dt=U32)
        act4, gelu4, c4 = e.take(2, NB), e.take(2, NB), e.take(2, NB)
        diag = e.take(2, NB, P)
        norm = e.take(8)

        act_, dve_, pool_ = sem("act_steps"), sem("dve_steps"), sem("pool_steps")
        passed = sem("waits_passed")
        consts_in, cols_in = sem("consts_in"), sem("cols_in")
        made = sem("made")
        x_in, mean_sq, rstd, scaled, xT_mm, xn_ready, xn_kept = (sem(n) for n in (
            "x_in", "mean_sq", "rstd", "scaled", "xT_mm", "xn_ready", "xn_kept"))
        v_mm, vc_mm, v_out, vc_out, vc_sq, vc_rstd, vc_ready, sp_mm, sp_out = (sem(n) for n in (
            "v_mm", "vc_mm", "v_out", "vc_out", "vc_sq", "vc_rstd", "vc_ready", "sp_mm", "sp_out"))
        w_a_in, w_mem_in, mkv_mm, mkv_out, mkT_mm, mkT_out = (sem(n) for n in (
            "w_a_in", "w_mem_in", "mkv_mm", "mkv_out", "mkT_mm", "mkT_out"))
        wb_in = [sem(f"wb_in{n}") for n in range(2)]
        b_mm, b_out, chunk_out, knat_mm, knat_out = (sem(n) for n in (
            "b_mm", "b_out", "chunk_out", "knat_mm", "knat_out"))
        c_in, s_mm, s_taken, m_ready, e_ready, p_ready, pT_mm, pT_out, pv_mm, swa_out = (sem(n) for n in (
            "c_in", "s_mm", "s_taken", "m_ready", "e_ready", "p_ready", "pT_mm", "pT_out", "pv_mm", "swa_out"))
        ms_mm, mm_ready, me_ready, mp_ready, mpT_mm, mpT_out, mpv_mm, mem_out = (sem(n) for n in (
            "ms_mm", "mm_ready", "me_ready", "mp_ready", "mpT_mm", "mpT_out", "mpv_mm", "mem_out"))
        smp_in, smp_pe, smp_act, smp_dve = sem("smp_in"), sem("smp_pe"), sem("smp_act"), sem("smp_dve")
        smp_kv_in = [sem(f"smp_kv_in{n}") for n in range(2)]
        smp_kv_used = sem("smp_kv_used")
        wd_in = [sem(f"wd_in{n}") for n in range(NBR)]
        d_mm, d_sig, d_mul, merged_ready, merged_out = (sem(n) for n in (
            "d_mm", "d_sig", "d_mul", "merged_ready", "merged_out"))
        we_in, m_in, h_in, h_mm, h_sum, root, n2_ready, n2T_mm, n2T_out = (sem(n) for n in (
            "we_in", "m_in", "h_in", "h_mm", "h_sum", "root", "n2_ready", "n2T_mm", "n2T_out"))
        q_mm, q_out, qT_mm, qT_out, key_mm, keys_taken, shifted_ready, raised_ready = (sem(n) for n in (
            "q_mm", "q_out", "qT_mm", "qT_out", "key_mm", "keys_taken", "shifted_ready", "raised_ready"))
        moved, staged, dots, gelus, c_ready, diags, v_used = (sem(n) for n in (
            "moved", "staged", "dots", "gelus", "c_ready", "diags", "v_used"))
        u_in = [[sem(f"u_in{n}{j}") for j in range(NB)] for n in range(2)]
        v_in = [sem(f"v_in{j}") for j in range(NB)]
        acc_mm, acc_taken, y_root, y_ready, y_out = (sem(n) for n in (
            "acc_mm", "acc_taken", "y_root", "y_ready", "y_out"))
        stored, stored_k = sem("stored"), sem("stored_k")

        def cols(n):
            return bass.ds(n * P, P)

        def alone(eng):
            eng.sem_inc(passed, 1)

        def wide(a, *shape):
            return a.unsqueeze(a.ndim).broadcast_to([a.shape[0], *shape])

        LOADS = ["swa_bias", "smp_bias", "chunk_g", "chunk_b", "chunk_b_smp", "ws_T", "ws_T_smp",
                 "gate_b", "sinks", "smp_sinks"]
        where = dict(swa_bias=swa_bias, smp_bias=smp_bias, chunk_g=chunk_g, chunk_b=chunk_b,
                     ws_T=ws_T, gate_b=gate_b, sinks=sinks, smp_sinks=smp_sinks,
                     chunk_b_smp=chunk_b_smp, ws_T_smp=ws_T_smp[0:SAMPLE])
        block = ctx.enter_context(nc.Block())

        @block.sync
        def _(sp):
            def send(out, in_, s):
                return sp.dma_start(out, in_).then_inc(s, 16)

            send(x_t[:, :], t["x"][0:P, :], x_in)
            send(ident[:, :], t["ident"], cols_in)
            send(norm1_col[:, :], t["norm1_col"], cols_in)
            send(mem_norm_col[:, :], t["mem_norm_col"], cols_in)
            send(iota16[:, :], t["iota16"], cols_in)
            send(w_vvc[:, :, :], t["w_vvc"], w_a_in)
            for name in LOADS:
                send(where[name], t[name], consts_in)
            send(w_mem[:, :, :], t["w_mem"], w_mem_in)
            with sp.Fori(1, TILES) as i:
                sp.wait_ge(mean_sq, i)
                sp.wait_ge(scaled, i)
                send(x_t[:, :], t["x"][cols(i), :], x_in)
            for m in range(MT):
                sp.wait_ge(mean_sq, TILES + m)
                sp.wait_ge(scaled, TILES + m)
                send(x_t[:, :], t["mem"][m * P:(m + 1) * P, :], x_in)
            sp.wait_ge(vc_ready, TILES)
            send(t["vc_out"], vc_n[0:SAMPLE, :], stored)
            sp.wait_ge(v_out, TILES)
            send(t["v_prompt"], v_nat[:, PTILES - 1, :], stored)
            send(t["v_sample_new"], v_nat[0:SAMPLE, PTILES, :], stored)
            for m in range(MT):
                sp.wait_ge(mkv_out, 2 * m + 2)
                send(t["mk_out"][m * P:(m + 1) * P, :], mk_nat[:, m, :], stored)
                send(t["mv_out"][m * P:(m + 1) * P, :], mv[:, m, :], stored)
            for name in ("k", "v"):
                send(t[f"{name}_sample_old"], t[f"{name}_cache_rows"][:, T:WINDOW, :], stored_k)

            def load_b(n, slot):
                send(w_ring[:, slot, 0:DC, :], t["w_b"][bass.ds(n, 1)].rearrange("a p c m -> p (a c) m"), wb_in[slot])

            load_b(0, 0)
            load_b(1, 1)
            with sp.Fori(1, 4) as i:
                for slot in range(2):
                    sp.wait_ge(b_mm, 6 * i + 3 * slot - 3)
                    load_b(2 * i + slot, slot)
            sp.wait_ge(b_mm, 3 * (FK - 1))
            load_b(FK, 0)
            with sp.Fori(0, 2) as i:
                for k in range(2):
                    sp.wait_ge(b_mm, 6 * i + 3 * (FU - 1 + k))
                    load_b(2 * i + FU + k, (FU + k) % 2)
            sp.wait_ge(knat_out, 1)
            send(t["k_prompt"], knat[:, 0, :], stored_k)
            send(t["k_sample_new"], knat[0:SAMPLE, 1, :], stored_k)

            sp.wait_ge(mem_out, PTILES)
            sp.wait_ge(swa_out, PTILES)
            sp.wait_ge(mpv_mm, PTILES)
            send(kcT[:, :, :], t["k_cache_T"], smp_in)
            send(cv[:, :, :], t["v_cache"], smp_in)
            for n in range(2 * B):
                if n >= 2:
                    sp.wait_ge(smp_kv_used, n - 1)
                src = t["mk_cache_T"] if n < B else t["mv_cache"]
                send(w_ring[:, n % 2, 0:DC, :].rearrange("p c m -> p (c m)"), src[n % B], smp_kv_in[n % 2])

            def load_d(i, j):
                send(w_ring[:, j, :, :], t["w_d"][bass.ds(3 * i + j, 1)].rearrange("a p c m -> p (a c) m"), wd_in[j])

            sp.wait_ge(smp_kv_used, 2 * B)
            for j in range(NBR):
                load_d(0, j)
            with sp.Fori(1, DC) as i:
                for j in range(NBR):
                    sp.wait_ge(d_mm, 9 * i + (3 * j - 6))
                    load_d(i, j)
                sp.wait_ge(merged_ready, i)
                send(t["m_scratch"][bass.ds(i - 1, 1)].rearrange("a p n -> (a p) n"), merged[:, :], merged_out)
            sp.wait_ge(merged_ready, DC)
            send(t["m_scratch"][DC - 1], merged[:, :], merged_out)

            sp.wait_ge(d_mm, 3 * NBR * DC)
            sp.wait_ge(merged_out, 16 * DC)
            sp.wait_ge(stored, 16 * (3 + 2 * MT))
            sp.wait_ge(stored_k, 16 * 4)
            send(w_out[:, :, :], t["w_out"], we_in)
            send(w_q[:, :, :], t["w_q"], we_in)
            send(subT[:, :, :], t["subT"], we_in)
            send(norm2_g, t["norm2_g"], we_in)
            send(final_g, t["final_g"], we_in)

            def load_e(f):
                send(m_tile[:, :, :], t["m_scratch"][:, :, cols(f)].rearrange("c p n -> p c n"), m_in)
                send(h_next[:, :], t["x"][cols(f), :], h_in)

            load_e(0)
            with sp.Fori(0, PTILES) as i:
                sp.wait_ge(moved, i + 1)
                sp.wait_ge(h_mm, i + 1)
                load_e(i + 1)
                sp.wait_ge(y_ready, i + 1)
                send(t["y"][cols(i), :], y[:, :], y_out)
            sp.wait_ge(y_ready, TILES)
            send(t["y"][PROMPT:TOKENS, :], y[0:SAMPLE, :], y_out)
            sp.wait_ge(y_out, 16 * TILES)

        @block.tensor
        def _(pe):
            mm, tr = nc.tensor.matmul, nc.tensor.transpose
            xT = ps[:, 0:2, :].rearrange("p b (c n) -> p (b c) n", n=P)

            def transpose_x(n):
                pe.wait_ge(scaled, n + 1)
                pe.wait_ge(xn_ready, n)
                for c in range(DC):
                    last = tr(xT[:, c, :], xs[:, c * P:(c + 1) * P], ident[:, :])
                last.then_inc(xT_mm, 1)

            def tile_a(n, sample=False):
                transpose_x(n)
                pe.wait_ge(xn_ready, n + 1)
                pe.wait_ge(v_out, n)
                pe.wait_ge(vc_out, n)
                for c in range(DC):
                    last = mm(ps[:, 2, 0:KVW], xn_tile[:, c, :], w_vvc[:, c, 0:KVW], start=c == 0, stop=c == DC - 1)
                last.then_inc(v_mm, 1)
                for c in range(DC):
                    last = mm(ps[:, 3, :], xn_tile[:, c, :], w_vvc[:, c, KVW:KVW + CW], start=c == 0, stop=c == DC - 1)
                last.then_inc(vc_mm, 1)
                pe.wait_ge(vc_ready, n + 1)
                pe.wait_ge(sp_out, n)
                for g in range(CG):
                    if sample:
                        last = mm(ps[:, 4, g * SAMPLE:(g + 1) * SAMPLE], vc_n[0:SAMPLE, g * P:(g + 1) * P],
                                  ws_T_smp[0:SAMPLE, g, :], start=True, stop=True)
                    else:
                        last = mm(ps[:, 4, g * P:(g + 1) * P], vc_n[:, g * P:(g + 1) * P], ws_T[:, g, :],
                                  start=True, stop=True)
                last.then_inc(sp_mm, 1)

            pe.wait_ge(cols_in, 64)
            pe.wait_ge(w_a_in, 16)
            pe.wait_ge(made, 2)
            with pe.Fori(0, PTILES) as i:
                tile_a(i)
            tile_a(PTILES, sample=True)

            pe.wait_ge(w_mem_in, 16)
            for m in range(MT):
                transpose_x(TILES + m)
                pe.wait_ge(xn_ready, TILES + m + 1)
                pe.wait_ge(mkv_out, 2 * m)
                for half in range(2):
                    for c in range(DC):
                        last = mm(ps[:, 5 + half, :], xn_tile[:, c, :], w_mem[:, c, half * MW:(half + 1) * MW],
                                  start=c == 0, stop=c == DC - 1)
                    last.then_inc(mkv_mm, 1)
                pe.wait_ge(mkv_out, 2 * m + 1)
                pe.wait_ge(mkT_out, m)
                for h in range(MH):
                    last = tr(ps[:, 7, h * P:(h + 1) * P], mk_nat[:, m, h * P:(h + 1) * P], ident[:, :])
                last.then_inc(mkT_mm, 1)

            def block_b(n, slot, uses, first=False):
                pe.wait_ge(wb_in[slot], 16 * uses)
                for th in range(3):
                    if not first:
                        pe.wait_ge(b_out, 3 * n + (th - 2))
                    for c in range(DC):
                        last = mm(ps[:, 5 + th, 0:THIRD], w_ring[:, slot, c, :], xnT[:, c, th * THIRD:(th + 1) * THIRD],
                                  start=c == 0, stop=c == DC - 1)
                    last.then_inc(b_mm, 1)

            pe.wait_ge(xn_kept, TILES)
            pe.wait_ge(mkT_out, MT)
            pe.wait_ge(mkv_out, 2 * MT)
            block_b(0, 0, 1, first=True)
            block_b(1, 1, 1)
            with pe.Fori(1, 4) as i:
                for slot in range(2):
                    block_b(2 * i + slot, slot, i + 1)
            block_b(FK, 0, 5)
            with pe.Fori(0, 2) as i:
                for k in range(2):
                    slot = (FU + k) % 2
                    block_b(2 * i + FU + k, slot, i + (5 if slot else 6))
            pe.wait_ge(b_out, 3 * FEATS)
            tr(ps[:, 0, 0:KVW], feats[:, FK, PROMPT - P:PROMPT], ident[:, :])
            tr(ps[0:SAMPLE, 1, 0:KVW], feats[:, FK, PROMPT:TOKENS], ident[:, :]).then_inc(knat_mm, 1)
            pe.wait_ge(knat_out, 1)

            def tile_c(n, first=False):
                pe.wait_ge(c_in, 3 * n + 3)
                if not first:
                    pe.wait_ge(swa_out, n)
                    pe.wait_ge(mem_out, n)
                keys = slice(P, 2 * P) if first else slice(0, 2 * P)
                for kv in range(KV):
                    part = slice(kv * HD, (kv + 1) * HD)
                    for g in range(GQ):
                        at = (g % 2) * 2 * P
                        last = mm(ps[:, 2 * kv + g // 2, at + keys.start:at + keys.stop], qs[part, FQ + g, :],
                                  ks[part, keys], start=True, stop=True)
                last.then_inc(s_mm, 1)
                pe.wait_ge(s_taken, n + 1)
                for h in range(MH):
                    last = mm(ps[:, 1 + h // 2, (h % 2) * MEM:(h % 2 + 1) * MEM], qs[:, FM + h, :], mkT[:, h, :],
                              start=True, stop=True)
                last.then_inc(ms_mm, 1)
                pe.wait_ge(p_ready, n + 1)
                if not first:
                    pe.wait_ge(mpT_out, n)
                    pe.wait_ge(pT_out, 2 * n)
                halves = (1,) if first else (0, 1)
                for kv in range(KV):
                    for half in halves:
                        for g in range(GQ):
                            last = tr(ps[:, 4 + 2 * kv + half, g * P:(g + 1) * P],
                                      sc[:, kv * GQ + g, half * P:(half + 1) * P], ident[:, :])
                    last.then_inc(pT_mm, 1)
                pe.wait_ge(pT_out, 2 * n + 2)
                for kv in range(KV):
                    part = slice(kv * HD, (kv + 1) * HD)
                    for half in halves:
                        last = mm(ps[part, 0, :], vs[:, half, part], scT[:, kv, half, :, :].rearrange("p g n -> p (g n)"),
                                  start=half == halves[0], stop=half == 1)
                last.then_inc(pv_mm, 1)
                pe.wait_ge(mp_ready, n + 1)
                for h in range(MH):
                    for m in range(MT):
                        k = h * MT + m
                        last = tr(ps[:, 4 + k // 4, (k % 4) * P:(k % 4 + 1) * P], msc[:, h, m * P:(m + 1) * P], ident[:, :])
                last.then_inc(mpT_mm, 1)
                pe.wait_ge(mpT_out, n + 1)
                for h in range(MH):
                    for m in range(MT):
                        last = mm(ps[:, 3, h * P:(h + 1) * P], mv[:, m, h * P:(h + 1) * P], mscT[:, h, m, :],
                                  start=m == 0, stop=m == MT - 1)
                last.then_inc(mpv_mm, 1)

            tile_c(0, first=True)
            with pe.Fori(1, PTILES) as i:
                tile_c(i)

            pe.wait_ge(mem_out, PTILES)
            pe.wait_ge(swa_out, PTILES)
            pe.wait_ge(smp_in, 32)
            for kv in range(KV):
                part = slice(kv * HD, (kv + 1) * HD)
                for b in range(B):
                    q = feats[part, FQ:FQ + GQ, PROMPT + b * T:PROMPT + (b + 1) * T]
                    at = slice(b * GQ * T, (b + 1) * GQ * T)
                    mm(ps[:, kv, at], kcT[part, b, :], q, start=True, stop=True)
                    last = mm(ps[0:SAMPLE, 2 + kv, at], feats[part, FK, PROMPT:TOKENS], q, start=True, stop=True)
            last.then_inc(smp_pe, 1)
            pe.wait_ge(smp_act, 1)
            for kv in range(KV):
                at = kv * 2 * P
                tr(ps[:, 4, at:at + P], smp_sT[:, kv, :], ident[:, :])
                last = tr(ps[:, 4, at + P:at + P + SAMPLE], smp_snT[0:SAMPLE, kv, :], ident[0:SAMPLE, 0:SAMPLE])
            last.then_inc(smp_pe, 1)
            for b in range(B):
                pe.wait_ge(smp_kv_in[b % 2], 16 * (b // 2 + 1))
                km = w_ring[:, b % 2, 0:DC, :].rearrange("p c m -> p (c m)").rearrange("p (h m) -> p h m", h=MH)
                for h in range(MH):
                    for m in range(MT):
                        at = m * P + (b * MH + h) * T
                        last = mm(ps[:, 5, at:at + T], km[:, h, m * P:(m + 1) * P],
                                  feats[:, FM + h, PROMPT + b * T:PROMPT + (b + 1) * T], start=True, stop=True)
                last.then_inc(smp_kv_used, 1)
            pe.wait_ge(smp_dve, 2)
            for kv in range(KV):
                tr(ps[:, 6, kv * P:(kv + 1) * P], smp_s[:, kv, 0:P], ident[:, :])
                last = tr(ps[0:SAMPLE, 7, kv * P:(kv + 1) * P], smp_s[:, kv, P:P + SAMPLE], ident[:, :])
            last.then_inc(smp_pe, 1)
            pe.wait_ge(smp_act, 3)
            for kv in range(KV):
                part = slice(kv * HD, (kv + 1) * HD)
                for b in range(B):
                    at = slice(b * GQ * T, (b + 1) * GQ * T)
                    mm(ps[part, 0, at], cv[:, b, part], smp_pT[:, kv, at], start=True, stop=False)
                    last = mm(ps[part, 0, at], v_nat[0:SAMPLE, PTILES, part], smp_pnT[0:SAMPLE, kv, at],
                              start=False, stop=True)
            last.then_inc(smp_pe, 1)
            pe.wait_ge(smp_act, 4)
            for m in range(MT):
                last = tr(ps[:, 1, m * P:(m + 1) * P], smp_mT[:, m, :], ident[:, :])
            last.then_inc(smp_pe, 1)
            pe.wait_ge(smp_dve, 5)
            for m in range(MT):
                last = tr(ps[:, 2, m * P:(m + 1) * P], smp_m[:, m * P:(m + 1) * P], ident[:, :])
            last.then_inc(smp_pe, 1)
            pe.wait_ge(smp_act, 6)
            for b in range(B):
                pe.wait_ge(smp_kv_in[b % 2], 16 * ((B + b) // 2 + 1))
                vm = w_ring[:, b % 2, 0:DC, :].rearrange("p c m -> p (c m)").rearrange("p (m w) -> p m w", m=MT)
                for h in range(MH):
                    at = slice((b * MH + h) * T, (b * MH + h + 1) * T)
                    for m in range(MT):
                        last = mm(ps[:, 3, at], vm[:, m, h * P:(h + 1) * P], smp_mpT[:, m, at],
                                  start=m == 0, stop=m == MT - 1)
                last.then_inc(smp_kv_used, 1)

            def unit(i, j, first=False):
                pe.wait_ge(wd_in[j], 16 * (i + 1))
                branch = feats[:, (FQ, FU, FM)[j]:(FQ, FU, FM)[j] + BC, :]
                for th in range(3):
                    part = slice(th * THIRD, (th + 1) * THIRD)
                    if not first:
                        pe.wait_ge(d_sig, 9 * i + (3 * j + th - 2))
                        pe.wait_ge(d_mul, 9 * i + (3 * j + th - 2))
                    for c in range(DC):
                        mm(ps[:, th, 0:THIRD], w_ring[:, j, c, :], xnT[:, c, part], start=c == 0, stop=c == DC - 1)
                    for c in range(BC):
                        last = mm(ps[:, 3 + th, 0:THIRD], w_ring[:, j, DC + c, :], branch[:, c, part],
                                  start=c == 0, stop=c == BC - 1)
                    last.then_inc(d_mm, 1)

            pe.wait_ge(smp_dve, 6)
            pe.wait_ge(chunk_out, CG)
            for j in range(NBR):
                unit(0, j, first=j == 0)
            with pe.Fori(1, DC) as i:
                for j in range(NBR):
                    unit(i, j)

            h_ps = ps[:, 4:6, :]
            n2T_ps = h_ps.rearrange("p b (c n) -> p (b c) n", n=P)

            def front_h(f, half):
                if half == 0:
                    pe.wait_ge(m_in, 16 * (f + 1))
                    pe.wait_ge(n2T_out, f)
                for c in range(DC):
                    last = mm(h_ps[:, half, :], m_tile[:, c, :], w_out[:, c, half * 512:(half + 1) * 512],
                              start=c == 0, stop=c == DC - 1)
                if half:
                    last.then_inc(h_mm, 1)

            def front_n2T(f):
                pe.wait_ge(n2_ready, f + 1)
                for c in range(DC):
                    last = tr(n2T_ps[:, c, :], n2_next[:, c * P:(c + 1) * P], ident[:, :])
                last.then_inc(n2T_mm, 1)

            def front_q(g, p):
                pe.wait_ge(keys_taken, g)
                for c in range(DC):
                    last = mm(ps[:, 6:7, :], n2T[:, c, :], w_q[:, c:c + 1, bass.ds(p * 4 * P, 4 * P)],
                              start=c == 0, stop=c == DC - 1)
                last.then_inc(q_mm, 1)

            def front_qT(g):
                pe.wait_ge(q_out, g + 1)
                for k in range(4):
                    last = tr(ps[:, 7, k * P:(k + 1) * P], q_nat[:, k * P:(k + 1) * P], ident[:, :])
                last.then_inc(qT_mm, 1)

            def front_keys(g):
                pe.wait_ge(qT_out, g + 1)
                for k in range(4):
                    last = mm(ps[:, 6, k * NK:(k + 1) * NK], qT[:, k, :], subT[:, k % 2, :], start=True, stop=True)
                last.then_inc(key_mm, 1)

            def open_acc(n):
                pe.wait_ge(acc_taken, n)
                for half in range(2):
                    mm(ps[:, half, :], nothing[:, 0:P], nothing[:, :], start=True, stop=False, skip_group_check=True)

            def add_v(batch, b, R):
                for j in range(NB):
                    pe.wait_ge(v_in[j], 16 * batch + 16)
                    pe.wait_ge(diags, 4 * batch + (j + 1))
                    if R < P:
                        alone(pe)
                    for half in range(2):
                        last = mm(ps[0:R, half, :], diag[0:R, b % 2, j, 0:R], v_ring[0:R, j, half * 512:(half + 1) * 512],
                                  start=False, stop=False, skip_group_check=True)
                    last.then_inc(v_used, 1)

            def tile_e(n, f, R=P):
                open_acc(n)
                for b in range(OPEN):
                    if b:
                        add_v(32 * n + (b - 1), b - 1, R)
                    if f is not None:
                        if b < 2:
                            front_h(f, b)
                        elif b == 4:
                            front_n2T(f)
                with pe.Fori(0, PAIRS) as p:
                    for b in range(PER_PAIR):
                        if f is not None and b == 0:
                            front_q(4 * f + p, p)
                        add_v(32 * n + PER_PAIR * p + (OPEN + b - 1), (b - 1) % 2, R)
                        if f is not None and b == 1:
                            front_qT(4 * f + p)
                        if f is not None and b == 2:
                            front_keys(4 * f + p)
                add_v(32 * n + (BATCHES - 1), BATCHES - 1, R)
                for half in range(2):
                    last = mm(ps[:, half, :], nothing[:, 0:P], nothing[:, :], start=False, stop=True, skip_group_check=True)
                last.then_inc(acc_mm, 1)

            pe.wait_ge(we_in, 16 * 5)
            pe.wait_ge(d_sig, 3 * NBR * DC)
            pe.wait_ge(d_mul, 3 * NBR * DC)
            front_h(0, 0)
            front_h(0, 1)
            front_n2T(0)
            pe.wait_ge(n2T_out, 1)
            with pe.Fori(0, PAIRS) as p:
                front_q(p, p)
                front_qT(p)
                front_keys(p)
            with pe.Fori(0, PTILES) as i:
                tile_e(i, i + 1)
            tile_e(PTILES, None, R=SAMPLE)

        @block.scalar
        def _(act):
            fn = nc.scalar.activation

            def mean_square(n):
                act.wait_ge(x_in, 16 * n + 16)
                act.wait_ge(rstd, n)
                fn(squares[:, :], x_t[:, :], ACT.Square, scale=D ** -0.5, accum_out=stat[:, 0:1]).then_inc(mean_sq, 1)
                act.wait_ge(mean_sq, n + 1)

            def tile_a(n):
                mean_square(n)
                act.wait_ge(v_mm, n + 1)
                alone(act)
                fn(v_nat[:, bass.ds(n, 1), :], ps[:, 2:3, 0:KVW], ACT.Copy).then_inc(v_out, 1)
                act.wait_ge(vc_mm, n + 1)
                act.wait_ge(vc_ready, n)
                fn(vc_gelu[:, :], ps[:, 3, :], ACT.Gelu).then_inc(vc_out, 1)
                act.wait_ge(vc_out, n + 1)
                act.wait_ge(vc_rstd, n)
                fn(vc_squares[:, :], vc_gelu[:, :], ACT.Square, accum_out=stat[:, 4:5]).then_inc(vc_sq, 1)
                act.wait_ge(vc_sq, n + 1)

            with act.Fori(0, TILES) as i:
                tile_a(i)
            for m in range(MT):
                mean_square(TILES + m)
                act.wait_ge(mkv_mm, 2 * m + 1)
                fn(mk_nat[:, m, :], ps[:, 5, :], ACT.Copy).then_inc(mkv_out, 1)
                act.wait_ge(mkv_mm, 2 * m + 2)
                fn(mv[:, m, :], ps[:, 6, :], ACT.Copy).then_inc(mkv_out, 1)

            def block_b(n, func):
                for th in range(3):
                    act.wait_ge(b_mm, 3 * n + (th + 1))
                    alone(act)
                    fn(feats[:, bass.ds(n, 1), th * THIRD:(th + 1) * THIRD], ps[:, 5 + th:6 + th, 0:THIRD], func)\
                        .then_inc(b_out, 1)

            with act.Fori(0, FU) as i:
                block_b(i, ACT.Copy)
            with act.Fori(0, CG) as i:
                block_b(i + FU, ACT.Gelu)

            act.wait_ge(xn_ready, TILES + MT)

            def tile_c(n, first=False):
                keys = slice(P, 2 * P) if first else slice(0, 2 * P)
                act.wait_ge(m_ready, n + 1)
                for h in range(HEADS):
                    fn(sc[:, h, keys], sc[:, h, keys], ACT.Exp, bias=row[:, 1, h:h + 1], accum_out=row[:, 3, h:h + 1])
                fn(row[:, 4, :], row[:, 2, :], ACT.Exp).then_inc(e_ready, 1)
                act.wait_ge(mm_ready, n + 1)
                if not first:
                    act.wait_ge(mpT_mm, n)
                for h in range(MH):
                    last = fn(msc[:, h, :], ps[:, 1 + h // 2, (h % 2) * MEM:(h % 2 + 1) * MEM], ACT.Exp,
                              bias=row[:, 5, h:h + 1], scale=MEM_SCALE, accum_out=row[:, 6, h:h + 1])
                last.then_inc(me_ready, 1)
                for kv in range(KV):
                    act.wait_ge(pT_mm, 2 * n + (kv + 1))
                    if not first:
                        act.wait_ge(pv_mm, n)
                    lo = 1 if first else 0
                    fn(scT[:, kv, lo:2, :, :].rearrange("p a g n -> p a (g n)"), ps[:, 4 + 2 * kv + lo:6 + 2 * kv, :],
                       ACT.Copy).then_inc(pT_out, 1)
                act.wait_ge(mpT_mm, n + 1)
                if not first:
                    act.wait_ge(mpv_mm, n)
                fn(mscT[:, :, :, :].rearrange("p h m n -> p (h m n)"), ps[:, 4:6, :].rearrange("p a n -> p (a n)"),
                   ACT.Copy).then_inc(mpT_out, 1)

            tile_c(0, first=True)
            with act.Fori(1, PTILES) as i:
                tile_c(i)

            act.wait_ge(mpv_mm, PTILES)
            act.wait_ge(smp_pe, 1)
            fn(smp_sT[:, :, :], ps[:, 0:2, 0:P], ACT.Copy)
            fn(smp_snT[0:SAMPLE, :, :], ps[0:SAMPLE, 2:4, 0:P], ACT.Copy).then_inc(smp_act, 1)
            act.wait_ge(smp_dve, 1)
            for kv in range(KV):
                fn(smp_s[:, kv, :], smp_s[:, kv, :], ACT.Exp, bias=row[:, 1, kv:kv + 1], accum_out=row[:, 3, kv:kv + 1])
            fn(row[:, 4, 0:KV], row[:, 2, 0:KV], ACT.Exp).then_inc(smp_act, 1)
            act.wait_ge(smp_pe, 3)
            fn(smp_pT[:, :, :].rearrange("p a n -> p (a n)"), ps[:, 6, 0:KV * P], ACT.Copy)
            fn(smp_pnT[0:SAMPLE, :, :].rearrange("p a n -> p (a n)"), ps[0:SAMPLE, 7, 0:KV * P], ACT.Copy)\
                .then_inc(smp_act, 1)
            act.wait_ge(smp_kv_used, B)
            fn(smp_mT[:, :, :].rearrange("p a n -> p (a n)"), ps[:, 5, 0:MEM], ACT.Copy).then_inc(smp_act, 1)
            act.wait_ge(smp_dve, 4)
            fn(smp_m[:, :], ps[:, 1, 0:MEM], ACT.Exp, bias=row[:, 5, 0:1], scale=MEM_SCALE,
               accum_out=row[:, 6, 0:1]).then_inc(smp_act, 1)
            act.wait_ge(smp_pe, 6)
            fn(smp_mpT[:, :, :].rearrange("p a n -> p (a n)"), ps[:, 2, 0:MEM], ACT.Copy).then_inc(smp_act, 1)

            def unit(i, j, first=False):
                for th in range(3):
                    act.wait_ge(d_mm, 9 * i + (3 * j + th + 1))
                    if not first:
                        act.wait_ge(d_mul, 9 * i + (3 * j + th - 2))
                    alone(act)
                    fn(sig[:, th * THIRD:(th + 1) * THIRD], ps[:, th, 0:THIRD], ACT.Sigmoid,
                       bias=gate_b[:, bass.ds(3 * i + j, 1)]).then_inc(d_sig, 1)

            act.wait_ge(smp_kv_used, 2 * B)
            for j in range(NBR):
                unit(0, j, first=j == 0)
            with act.Fori(1, DC) as i:
                for j in range(NBR):
                    unit(i, j)

            A = Steps(act, act_)

            def square_root(a, R, signal):
                A.add(fn(dump[0:R, :], a[0:R, :], ACT.Square, scale=D ** -0.5, accum_out=norm[0:R, 0:1]))
                A.settle()
                A.add(fn(norm[0:R, 1:2], norm[0:R, 0:1], ACT.Sqrt, bias=eps[0:R, 0:1]), signal)

            def front_norm(f):
                act.wait_ge(h_sum, f + 1)
                square_root(h_next, P, root)

            def front_n2T(f):
                act.wait_ge(n2T_mm, f + 1)
                A.add(fn(n2T[:, :, :].rearrange("p c n -> p (c n)"), ps[:, 4:6, :].rearrange("p a n -> p (a n)"),
                         ACT.Copy), n2T_out)

            def front_q(g):
                act.wait_ge(q_mm, g + 1)
                A.add(fn(q_nat[:, :], ps[:, 6, :], ACT.Copy), q_out)

            def front_qT(g):
                act.wait_ge(qT_mm, g + 1)
                A.add(fn(qT[:, :, :].rearrange("p k n -> p (k n)"), ps[:, 7, :], ACT.Copy), qT_out)

            def front_exp(g):
                act.wait_ge(shifted_ready, g + 1)
                A.add(fn(raised[:, :, :].rearrange("p h k -> p (h k)"), shifted[:, :, :].rearrange("p h k -> p (h k)"),
                         ACT.Exp), raised_ready)

            def gelu(batch, b, R):
                act.wait_ge(dots, 4 * batch + 4)
                A.add(fn(gelu4[0:R, b % 2, :], act4[0:R, b % 2, :], ACT.Gelu), gelus)

            def make_diag(batch, b, R, opening):
                act.wait_ge(c_ready, batch + 1)
                act.wait_ge(v_used, 4 * batch if opening else 4 * batch - 4)
                for j in range(NB):
                    A.add(fn(diag[0:R, b % 2, j, 0:R], ident[0:R, 0:R], ACT.Copy, scale=c4[0:R, b % 2, j:j + 1]), diags)

            def tile_e(n, f, R=P):
                for b in range(OPEN):
                    gelu(32 * n + b, b, R)
                    if b:
                        make_diag(32 * n + (b - 1), b - 1, R, b == 1)
                    if f is not None:
                        if b == 2:
                            front_norm(f)
                        elif b == 4:
                            front_n2T(f)
                with act.Fori(0, PAIRS) as p:
                    for b in range(PER_PAIR):
                        gelu(32 * n + PER_PAIR * p + (OPEN + b), b, R)
                        make_diag(32 * n + PER_PAIR * p + (OPEN + b - 1), (b - 1) % 2, R, False)
                        if f is not None:
                            if b == 0:
                                front_q(4 * f + p)
                            elif b == 1:
                                front_qT(4 * f + p)
                            elif b == 4:
                                front_exp(4 * f + p)
                make_diag(32 * n + (BATCHES - 1), BATCHES - 1, R, False)
                act.wait_ge(acc_taken, n + 1)
                square_root(h_cur, R, y_root)

            act.wait_ge(we_in, 16 * 5)
            front_norm(0)
            front_n2T(0)
            with act.Fori(0, PAIRS) as p:
                front_q(p)
                front_qT(p)
                front_exp(p)
            with A.loop(0, PTILES, 2) as i:
                tile_e(i, i + 1)
            tile_e(PTILES, None, R=SAMPLE)

        @block.vector
        def _(dve):
            V = Steps(dve, dve_)
            v = nc.vector

            V.add(v.memset(nothing[:, :], 0.0))
            V.add(v.memset(eps[:, :], EPS))
            dve.wait_ge(cols_in, 64)
            dve.wait_ge(consts_in, 16 * len(LOADS))

            def xn(n, col, kept):
                dve.wait_ge(rstd, n + 1)
                dve.wait_ge(xT_mm, n)
                v.tensor_scalar(xs[:, :], x_t[:, :], stat[:, 2:3], None, ALU.mult).then_inc(scaled, 1)
                dve.wait_ge(xT_mm, n + 1)
                dve.wait_ge(xn_kept, kept)
                xT = ps[:, 0:2, :].rearrange("p b (c n) -> p (b c) n", n=P)
                v.tensor_tensor(xn_tile[:, :, :], xT, wide(col[:, :], DC, P), ALU.mult).then_inc(xn_ready, 1)

            def tile_a(n, sample=False):
                dve.wait_ge(vc_mm, n)
                xn(n, norm1_col, n)
                dve.wait_ge(vc_rstd, n + 1)
                dve.wait_ge(sp_mm, n)
                v.scalar_tensor_tensor(vc_n[:, :], vc_gelu[:, :], stat[:, 6:7], chunk_g, ALU.mult, ALU.mult)\
                    .then_inc(vc_ready, 1)
                dve.wait_ge(sp_mm, n + 1)
                if sample:
                    v.tensor_tensor(spT[:, :, PROMPT:TOKENS], ps[:, 4, 0:CG * SAMPLE].rearrange("p (g n) -> p g n", g=CG),
                                    chunk_b_smp[:, :, :], ALU.add).then_inc(sp_out, 1)
                else:
                    v.tensor_tensor(spT[:, :, cols(n)], ps[:, 4, :].rearrange("p (g n) -> p g n", g=CG),
                                    chunk_b[:, :, :], ALU.add).then_inc(sp_out, 1)

            with dve.Fori(0, PTILES) as i:
                tile_a(i)
            tile_a(PTILES, sample=True)
            for m in range(MT):
                if m:
                    dve.wait_ge(mkv_mm, 2 * m)
                else:
                    dve.wait_ge(vc_mm, TILES)
                xn(TILES + m, mem_norm_col, TILES)
                dve.wait_ge(mkT_mm, m + 1)
                v.tensor_copy(mkT[:, :, m * P:(m + 1) * P], ps[:, 7, :].rearrange("p (h n) -> p h n", h=MH))\
                    .then_inc(mkT_out, 1)

            dve.wait_ge(sp_out, TILES)
            with dve.Fori(0, CG) as i:
                dve.wait_ge(b_out, 3 * i + 3 * (FU + 1))
                v.tensor_tensor(feats[:, bass.ds(i + FU, 1), 0:TOKENS], feats[:, bass.ds(i + FU, 1), 0:TOKENS],
                                spT[:, bass.ds(i, 1), 0:TOKENS], ALU.mult).then_inc(chunk_out, 1)
            dve.wait_ge(knat_mm, 1)
            v.tensor_copy(knat[:, 0, :], ps[:, 0, 0:KVW])
            v.tensor_copy(knat[0:SAMPLE, 1, :], ps[0:SAMPLE, 1, 0:KVW]).then_inc(knat_out, 1)

            def tile_c(n, first=False):
                keys = slice(P, 2 * P) if first else slice(0, 2 * P)
                nk = P if first else 2 * P
                scores = ps[:, 0:4, :].rearrange("p b (g n) -> p (b g) n", g=2)[:, :, keys]
                dve.wait_ge(s_mm, n + 1)
                if not first:
                    dve.wait_ge(pT_mm, 2 * n)
                V.add(v.scalar_tensor_tensor(sc[:, :, keys], scores, SWA_SCALE, swa_bias[:, :, keys], ALU.mult, ALU.add), s_taken, n + 1)
                V.settle()
                V.add(v.tensor_reduce(row[:, 0, :], sc[:, :, keys], AX.X, ALU.max))
                V.settle()
                V.add(v.tensor_tensor(row[:, 0, :], row[:, 0, :], sinks, ALU.max))
                V.settle()
                V.add(v.tensor_scalar(row[:, 1, :], row[:, 0, :], -1.0, None, ALU.mult))
                V.add(v.tensor_tensor(row[:, 2, :], sinks, row[:, 0, :], ALU.subtract), m_ready)
                dve.wait_ge(ms_mm, n + 1)
                V.add(v.tensor_reduce(row[:, 7, 0:MH], ps[:, 1:3, :].rearrange("p b (g n) -> p (b g) n", g=2), AX.X, ALU.max))
                V.settle()
                V.add(v.tensor_scalar(row[:, 5, 0:MH], row[:, 7, 0:MH], -MEM_SCALE, None, ALU.mult), mm_ready)
                dve.wait_ge(e_ready, n + 1)
                V.add(v.tensor_tensor(row[:, 3, :], row[:, 3, :], row[:, 4, :], ALU.add))
                V.settle()
                V.add(v.reciprocal(row[:, 4, :], row[:, 3, :]))
                V.settle()
                V.add(v.tensor_tensor(sc[:, :, keys], sc[:, :, keys], wide(row[:, 4, :], HEADS, nk), ALU.mult), p_ready)
                dve.wait_ge(me_ready, n + 1)
                V.add(v.reciprocal(row[:, 7, 0:MH], row[:, 6, 0:MH]))
                V.settle()
                V.add(v.tensor_tensor(msc[:, :, :], msc[:, :, :], wide(row[:, 7, 0:MH], MH, MEM), ALU.mult), mp_ready)
                dve.wait_ge(pv_mm, n + 1)
                V.add(v.tensor_copy(feats[:, FQ:FQ + GQ, cols(n)], ps[:, 0, :].rearrange("p (g n) -> p g n", g=GQ)), swa_out)
                dve.wait_ge(mpv_mm, n + 1)
                V.add(v.tensor_copy(feats[:, FM:FM + MH, cols(n)], ps[:, 3, :].rearrange("p (h n) -> p h n", h=MH)), mem_out)

            tile_c(0, first=True)
            with V.loop(1, PTILES, 7) as i:
                tile_c(i)

            V.settle()
            dve.wait_ge(smp_pe, 2)
            V.add(v.scalar_tensor_tensor(smp_s[:, :, :], ps[:, 4, :].rearrange("p (k n) -> p k n", k=KV)[:, :, 0:P + SAMPLE],
                                         SWA_SCALE, smp_bias[:, :, :], ALU.mult, ALU.add))
            V.settle()
            V.add(v.tensor_reduce(row[:, 0, 0:KV], smp_s[:, :, :], AX.X, ALU.max))
            V.settle()
            V.add(v.tensor_tensor(row[:, 0, 0:KV], row[:, 0, 0:KV], smp_sinks, ALU.max))
            V.settle()
            V.add(v.tensor_scalar(row[:, 1, 0:KV], row[:, 0, 0:KV], -1.0, None, ALU.mult))
            V.add(v.tensor_tensor(row[:, 2, 0:KV], smp_sinks, row[:, 0, 0:KV], ALU.subtract), smp_dve)
            dve.wait_ge(smp_act, 2)
            V.add(v.tensor_tensor(row[:, 3, 0:KV], row[:, 3, 0:KV], row[:, 4, 0:KV], ALU.add))
            V.settle()
            V.add(v.reciprocal(row[:, 4, 0:KV], row[:, 3, 0:KV]))
            V.settle()
            V.add(v.tensor_tensor(smp_s[:, :, :], smp_s[:, :, :], wide(row[:, 4, 0:KV], KV, P + SAMPLE), ALU.mult), smp_dve)
            dve.wait_ge(smp_pe, 4)
            for g in range(GQ):
                V.add(v.tensor_copy(
                    feats[:, FQ + g, PROMPT:TOKENS].rearrange("p (b t) -> p b t", b=B),
                    ps[:, 0, 0:P].rearrange("p (b g t) -> p b g t", b=B, g=GQ)[:, :, g, :]),
                    smp_dve if g == GQ - 1 else None)
            dve.wait_ge(smp_pe, 5)
            V.add(v.tensor_reduce(row[:, 7, 0:1], ps[:, 1, 0:MEM], AX.X, ALU.max))
            V.settle()
            V.add(v.tensor_scalar(row[:, 5, 0:1], row[:, 7, 0:1], -MEM_SCALE, None, ALU.mult), smp_dve)
            dve.wait_ge(smp_act, 5)
            V.add(v.reciprocal(row[:, 7, 0:1], row[:, 6, 0:1]))
            V.settle()
            V.add(v.tensor_scalar(smp_m[:, :], smp_m[:, :], row[:, 7, 0:1], None, ALU.mult), smp_dve)
            dve.wait_ge(smp_kv_used, 2 * B)
            for h in range(MH):
                V.add(v.tensor_copy(
                    feats[:, FM + h, PROMPT:TOKENS].rearrange("p (b t) -> p b t", b=B),
                    ps[:, 3, 0:P].rearrange("p (b h t) -> p b h t", b=B, h=MH)[:, :, h, :]),
                    smp_dve if h == MH - 1 else None, 6)

            V.settle()
            V.add(v.memset(merged[:, TOKENS:PADDED], 0.0))
            V.settle()

            def unit(i, j, first=False):
                for th in range(3):
                    part = slice(th * THIRD, (th + 1) * THIRD)
                    dve.wait_ge(d_sig, 9 * i + (3 * j + th + 1))
                    if j == 0:
                        if th == 0 and not first:
                            dve.wait_ge(merged_out, 16 * i)
                        V.add(v.tensor_tensor(merged[:, part], ps[:, 3 + th, 0:THIRD], sig[:, part], ALU.mult), d_mul, 9 * i + (3 * j + th + 1))
                    else:
                        V.settle()
                        V.add(v.tensor_tensor(prod[:, part], ps[:, 3 + th, 0:THIRD], sig[:, part], ALU.mult), d_mul, 9 * i + (3 * j + th + 1))
                        V.settle()
                        V.add(v.tensor_tensor(merged[:, part], merged[:, part], prod[:, part], ALU.add),
                              merged_ready if j == NBR - 1 and th == 2 else None, i + 1)

            for j in range(NBR):
                unit(0, j, first=True)
            with V.loop(1, DC, 5) as i:
                for j in range(NBR):
                    unit(i, j)

            V.settle()
            dve.wait_ge(we_in, 16 * 5)

            def hold():
                V.settle()
                alone(dve)

            def inverse_root(R, scr):
                V.add(v.reciprocal(scr[0:R, 2:3], scr[0:R, 1:2]))
                V.add(v.tensor_scalar(scr[0:R, 3:4], scr[0:R, 0:1], EPS, None, ALU.add))
                V.settle()
                V.add(v.scalar_tensor_tensor(scr[0:R, 4:5], scr[0:R, 2:3], scr[0:R, 3:4], scr[0:R, 2:3], ALU.mult, ALU.mult))
                V.settle()
                V.add(v.tensor_scalar(scr[0:R, 5:6], scr[0:R, 4:5], -0.5, 1.5, ALU.mult, ALU.add))
                V.settle()
                V.add(v.tensor_tensor(scr[0:R, 6:7], scr[0:R, 2:3], scr[0:R, 5:6], ALU.mult))
                V.settle()

            def front_sum(f):
                dve.wait_ge(h_mm, f + 1)
                dve.wait_ge(h_in, 16 * f + 16)
                V.add(v.tensor_tensor(h_next[:, :], h_next[:, :], ps[:, 4:6, :].rearrange("p a n -> p (a n)"), ALU.add), h_sum)

            def front_norm(f):
                dve.wait_ge(root, f + 1)
                inverse_root(P, norm)
                V.add(v.scalar_tensor_tensor(n2_next[:, :], h_next[:, :], norm[:, 6:7], norm2_g, ALU.mult, ALU.mult), n2_ready)

            def keys_first(g):
                dve.wait_ge(key_mm, g + 1)
                hold()
                s4 = ps[:, 6, :].rearrange("p (k n) -> p k n", k=4)
                for k in range(4):
                    V.add(v.max(sv[:, k, 0:8], s4[:, k, :]))
                hold()
                for k in range(4):
                    V.add(v.max_index(si[:, k, 0:8], sv[:, k, 0:8], s4[:, k, :]))
                for k in range(4):
                    V.add(v.match_replace(rest[:, k, :], sv[:, k, 0:8], s4[:, k, :], LOWEST),
                          keys_taken if k == 3 else None, g + 1)

            def keys_second(g):
                hold()
                for k in range(4):
                    V.add(v.max(sv[:, k, 8:16], rest[:, k, :]))
                hold()
                for k in range(4):
                    V.add(v.max_index(si[:, k, 8:16], sv[:, k, 8:16], rest[:, k, :]))
                for h in range(2):
                    V.add(v.tensor_tensor(cand[:, h, :].rearrange("p (a b) -> p a b", a=K), wide(sv[:, 2 * h, :], K, K),
                                          sv[:, 2 * h + 1, :].unsqueeze(1).broadcast_to([P, K, K]), ALU.add))
                V.settle()
                V.add(v.tensor_copy(sif[:, :, :], si[:, :, :]))

            def pairs_best(g):
                hold()
                for h in range(2):
                    V.add(v.max(cv16[:, h, 0:8], cand[:, h, :]))
                hold()
                for h in range(2):
                    V.add(v.max_index(ci16[:, h, 0:8], cv16[:, h, 0:8], cand[:, h, :]))
                for h in range(2):
                    V.add(v.match_replace(cand2[:, h, :], cv16[:, h, 0:8], cand[:, h, :], LOWEST))
                hold()
                for h in range(2):
                    V.add(v.max(cv16[:, h, 8:16], cand2[:, h, :]))
                hold()
                for h in range(2):
                    V.add(v.max_index(ci16[:, h, 8:16], cv16[:, h, 8:16], cand2[:, h, :]))
                V.add(v.tensor_tensor(shifted[:, :, :], cv16[:, :, :], cv16[:, :, 0:1].broadcast_to([P, 2, K]), ALU.subtract), shifted_ready, g + 1)

            def experts(g, p):
                flat = "p h k -> p (h k)"
                V.settle()
                V.add(v.tensor_scalar(hilo[:, 0], ci16[:, :, :], 4, None, ALU.logical_shift_right))
                V.add(v.tensor_scalar(hilo[:, 1], ci16[:, :, :], 15, None, ALU.bitwise_and))
                V.settle()
                V.add(v.tensor_copy(hilof[:, :, :, :], hilo[:, :, :, :]))
                for half in range(2):
                    V.settle()
                    V.add(v.tensor_tensor(match[:, :, :, :].rearrange("p h k a -> p (h k) a"),
                                          wide(hilof[:, half].rearrange(flat), 2 * K, K),
                                          iota16[:, :].unsqueeze(1).broadcast_to([P, 2 * K, K]), ALU.is_equal))
                    V.settle()
                    number = sif[:, half:4:2, :]
                    V.add(v.tensor_tensor(match[:, :, :, :], match[:, :, :, :],
                                          number.unsqueeze(2).broadcast_to([P, 2, K, K]), ALU.mult))
                    V.settle()
                    V.add(v.tensor_reduce(picked[:, half].rearrange(flat), match[:, :, :, :].rearrange("p h k a -> p (h k) a"),
                                          AX.X, ALU.add))
                V.settle()
                V.add(v.scalar_tensor_tensor(i_next[:, bass.ds(2 * K * p, 2 * K)], picked[:, 0].rearrange(flat), float(NK),
                                             picked[:, 1].rearrange(flat), ALU.mult, ALU.add))
                dve.wait_ge(raised_ready, g + 1)
                V.add(v.tensor_reduce(stat[:, 8:10], raised[:, :, :], AX.X, ALU.add))
                V.settle()
                V.add(v.reciprocal(stat[:, 10:12], stat[:, 8:10]))
                V.settle()
                V.add(v.tensor_tensor(g_next[:, bass.ds(2 * K * p, 2 * K)].rearrange("p (h k) -> p h k", h=2), raised[:, :, :],
                                      wide(stat[:, 10:12], 2, K), ALU.mult))

            def move(n):
                V.settle()
                dve.wait_ge(y_ready, n)
                dve.wait_ge(staged, STAGES * n)
                V.add(v.tensor_copy(i_cur, i_next))
                V.add(v.tensor_copy(n2_cur, n2_next))
                V.add(v.tensor_copy(g_cur, g_next))
                V.add(v.tensor_copy(h_cur, h_next), moved, n + 1)
                V.settle()

            def dot(batch, b, R, opening):
                for j in range(NB):
                    dve.wait_ge(u_in[b % 2][j], 8 * batch + 16 - 8 * (b % 2))
                    if j or not opening:
                        dve.wait_ge(dots, 4 * batch + (j - 1))
                    V.add(v.scalar_tensor_tensor(product[j % 2][0:R, :], u_ring[0:R, b % 2, j, :], 1.0, n2_cur[0:R, :],
                                                 ALU.mult, ALU.mult, accum_out=act4[0:R, b % 2, j:j + 1]), dots)

            product = [u_dump, ps[:, 2:4, :].rearrange("p a n -> p (a n)")]

            def weigh(batch, at, b, R, opening):
                dve.wait_ge(gelus, batch + 1)
                dve.wait_ge(diags, 4 * batch if opening else 4 * batch - 4)
                V.add(v.tensor_tensor(c4[0:R, b % 2, :], gelu4[0:R, b % 2, :], g_cur[0:R, bass.ds(at, NB)], ALU.mult), c_ready, batch + 1)

            def tile_e(n, f, R=P):
                move(n)
                for b in range(OPEN):
                    dot(32 * n + b, b, R, b == 0)
                    if b:
                        weigh(32 * n + (b - 1), NB * (b - 1), b - 1, R, b == 1)
                    if f is not None:
                        if b == 2:
                            front_sum(f)
                        elif b == 3:
                            front_norm(f)
                per = PAIR_STEPS if f is not None else 0
                with V.loop(0, PAIRS, per) as p:
                    for b in range(PER_PAIR):
                        dot(32 * n + PER_PAIR * p + (OPEN + b), b, R, False)
                        weigh(32 * n + PER_PAIR * p + (OPEN + b - 1), NB * PER_PAIR * p + NB * (OPEN + b - 1), (b - 1) % 2, R, False)
                        if f is not None:
                            if b == 2:
                                keys_first(4 * f + p)
                            elif b == 3:
                                keys_second(4 * f + p)
                            elif b == 4:
                                pairs_best(4 * f + p)
                            elif b == 5:
                                experts(4 * f + p, p)
                weigh(32 * n + (BATCHES - 1), NB * (BATCHES - 1), BATCHES - 1, R, False)
                dve.wait_ge(acc_mm, n + 1)
                V.add(v.tensor_tensor(h_cur[0:R, :], h_cur[0:R, :], ps[0:R, 0:2, :].rearrange("p a n -> p (a n)"), ALU.add), acc_taken)
                dve.wait_ge(y_root, n + 1)
                inverse_root(R, norm)
                dve.wait_ge(y_out, 16 * n)
                V.add(v.scalar_tensor_tensor(y[0:R, :], h_cur[0:R, :], norm[0:R, 6:7], final_g[0:R, :], ALU.mult, ALU.mult), y_ready)

            PAIR_STEPS = 11 + 11 + 10 + 13
            front_sum(0)
            front_norm(0)
            with V.loop(0, PAIRS, PAIR_STEPS) as p:
                keys_first(p)
                keys_second(p)
                pairs_best(p)
                experts(p, p)
            tile_steps = 3 + 5 + PAIRS * PAIR_STEPS + 5
            with V.loop(0, PTILES, tile_steps) as i:
                tile_e(i, i + 1)
            tile_e(PTILES, None, R=SAMPLE)

        @block.gpsimd
        def _(pool):
            G = Steps(pool, pool_)
            g = nc.gpsimd

            pool.wait_ge(consts_in, 16 * len(LOADS))
            G.add(g.memset(stat[:, 3:4], -0.5))
            g.affine_select(out=ws_T[:, :, :], in_=ws_T[:, :, :], compare_op=ALU.is_ge, fill=0.0, base=0,
                            pattern=[[0, CG], [1, P]], channel_multiplier=-1).then_inc(made, 1)
            small = ws_T_smp[0:SAMPLE, :, :]
            g.affine_select(out=small, in_=small, compare_op=ALU.is_ge, fill=0.0, base=0,
                            pattern=[[0, CG], [1, SAMPLE]], channel_multiplier=-1).then_inc(made, 1)
            G.settle()

            def inverse_root(signal, taken, n, at, scale):
                pool.wait_ge(signal, n + 1)
                pool.wait_ge(taken, n)
                alone(pool)
                G.add(g.tensor_scalar(stat[:, at + 1:at + 2], stat[:, at:at + 1], scale, EPS, ALU.mult, ALU.add))
                G.settle()

            def rstd_x(n):
                inverse_root(mean_sq, scaled, n, 0, 1.0)
                g.tensor_tensor(stat[:, 2:3], stat[:, 1:2], stat[:, 3:4], ALU.pow).then_inc(rstd, 1)

            def tile_a(n):
                rstd_x(n)
                pool.wait_ge(xn_ready, n + 1)
                g.tensor_copy(xnT[:, :, cols(n)], xn_tile[:, :, :]).then_inc(xn_kept, 1)
                inverse_root(vc_sq, vc_ready, n, 4, 1.0 / CW)
                g.tensor_tensor(stat[:, 6:7], stat[:, 5:6], stat[:, 3:4], ALU.pow).then_inc(vc_rstd, 1)

            with G.loop(0, TILES, 2) as i:
                tile_a(i)
            for m in range(MT):
                rstd_x(TILES + m)

            pool.wait_ge(b_out, 3 * FU)
            pool.wait_ge(v_out, TILES)
            pool.wait_ge(xn_ready, TILES + MT)
            pool.wait_ge(mkT_mm, MT)
            pool.wait_ge(stored, 16 * (3 + 2 * MT))
            g.tensor_copy(qs[:, :, :], feats[:, 0:FK, 0:P]).then_inc(c_in, 1)
            g.tensor_copy(ks[:, P:2 * P], feats[:, FK, 0:P]).then_inc(c_in, 1)
            g.tensor_copy(vs[:, 1, :], v_nat[:, 0, :]).then_inc(c_in, 1)
            with pool.Fori(1, PTILES) as i:
                pool.wait_ge(ms_mm, i)
                g.tensor_copy(qs[:, :, :], feats[:, 0:FK, cols(i)]).then_inc(c_in, 1)
                g.tensor_copy(ks.unsqueeze(1), feats[:, FK:FK + 1, bass.ds(i * P - P, 2 * P)]).then_inc(c_in, 1)
                pool.wait_ge(pv_mm, i)
                g.tensor_copy(vs[:, :, :], v_nat[:, bass.ds(i - 1, 2), :]).then_inc(c_in, 1)

            def rows(ring, table, index, R, s):
                g.indirect_dma_start(ring[0:R, :], None, t[table], bass.IndirectOffsetOnAxis(index[0:R, :], 0)).then_inc(s, 16)

            def gather_u(batch, b, index, R, opening):
                pool.wait_ge(dots, 4 * batch if opening else 4 * batch - 4)
                alone(pool)
                for j in range(NB):
                    rows(u_ring[:, b % 2, j, :], "peer_u", index[:, j:j + 1], R, u_in[b % 2][j])

            def gather_v(batch, index, R):
                pool.wait_ge(v_used, 4 * batch)
                alone(pool)
                for j in range(NB):
                    rows(v_ring[:, j, :], "peer_v", index[:, j:j + 1], R, v_in[j])

            half = PER_PAIR // 2 * NB

            def tile_e(n, R=P):
                pool.wait_ge(moved, n + 1)
                alone(pool)
                g.tensor_copy(stage_open, i_cur[:, 0:OPEN * NB]).then_inc(staged, 1)
                pool.wait_ge(staged, STAGES * n + 1)
                for b in range(OPEN):
                    gather_u(32 * n + b, b, stage_open[:, NB * b:NB * b + NB], R, b == 0)
                    if b:
                        gather_v(32 * n + (b - 1), stage_open[:, NB * (b - 1):NB * b], R)
                last = stage_open[:, NB * (OPEN - 1):NB * OPEN]
                g.tensor_copy(stage_pair[:, 1, half - NB:half], last).then_inc(staged, 1)
                pool.wait_ge(staged, STAGES * n + 2)
                alone(pool)
                with pool.Fori(0, PAIRS) as p:
                    for b in range(PER_PAIR):
                        h, k = divmod(b, PER_PAIR // 2)
                        batch = 32 * n + PER_PAIR * p + (OPEN + b)
                        if k == 0:
                            g.tensor_copy(stage_pair[:, h, :], i_cur[:, bass.ds(PER_PAIR * NB * p + OPEN * NB + half * h, half)])\
                                .then_inc(staged, 1)
                            pool.wait_ge(staged, STAGES * n + 2 * p + (3 + h))
                        gather_u(batch, b, stage_pair[:, h, NB * k:NB * k + NB], R, False)
                        hp, kp = divmod((b - 1) % PER_PAIR, PER_PAIR // 2)
                        gather_v(batch - 1, stage_pair[:, hp, NB * kp:NB * kp + NB], R)
                gather_v(32 * n + (BATCHES - 1), stage_pair[:, 1, half - NB:half], R)

            with pool.Fori(0, PTILES) as i:
                tile_e(i)
            tile_e(PTILES, R=SAMPLE)


def _position_constants():
    slopes = np.exp2(-8.0 * np.arange(1, HEADS + 1, dtype=np.float32) / HEADS).astype(np.float32)
    r, c = np.arange(WINDOW)[:, None], np.arange(2 * WINDOW)[None, :]
    dist = WINDOW + r - c
    valid = (dist >= 0) & (dist <= WINDOW)
    prompt = np.where(valid[:, None, :], -slopes[None, :, None] * dist[:, None, :].astype(np.float32), np.float32(NEG))
    b, g, t = (x.ravel()[:, None] for x in np.meshgrid(np.arange(B), np.arange(GQ), np.arange(T), indexing="ij"))
    sb, st = (x.ravel()[None, :] for x in np.meshgrid(np.arange(B), np.arange(T), indexing="ij"))
    dist = np.concatenate([WINDOW + t - np.arange(WINDOW)[None, :], t - st], 1)
    valid = (dist >= 0) & (dist <= WINDOW) & np.concatenate([np.ones((P, WINDOW), bool), sb == b], 1)
    sample = np.stack([np.where(valid, -slopes[kv * GQ + g] * dist.astype(np.float32), np.float32(NEG))
                       for kv in range(KV)], 1)
    return prompt.astype(np.float32), sample.astype(np.float32)


def kernel(x_prompt, x_sample, cache_swa_k, cache_swa_v, cache_mem_k, cache_mem_v, mem_prompt,
           norm1_g, w_in, b_gate, swa_sinks, chunk_norm_g, chunk_ws, chunk_bs, mem_norm_g, w_mem_kv,
           w_branch_out, w_out, norm2_g, peer_wq, peer_subkeys, peer_u, peer_v, final_norm_g):
    import concourse.bacc as bacc
    from concourse.bass_utils import run_bass_kernel_spmd

    A = np.asarray
    f32 = np.float32

    def on_all(v):
        v = A(v).reshape(1, -1)
        return np.ascontiguousarray(np.broadcast_to(v, (P, v.shape[1])))

    def chunked(w):
        w = A(w)
        return np.ascontiguousarray(w.reshape(-1, P, w.shape[1]).transpose(1, 0, 2))

    def blocks(w):
        w = A(w)
        return w.reshape(-1, P, w.shape[1] // P, P).transpose(2, 1, 0, 3)

    qw = HEADS * HD
    o = np.cumsum([0, qw, KVW, KVW, CW, CW, MW, NBR * D])
    w = A(w_in)[0]
    w_q, w_k, w_v, w_u, w_vc, w_mq, w_g = (w[:, o[n]:o[n + 1]] for n in range(7))
    w_q = w_q.reshape(D, KV, GQ, HD).transpose(0, 2, 1, 3).reshape(D, qw)
    w_b = np.concatenate([blocks(x) for x in (w_q, w_mq, w_k, w_u)], 0)
    br = A(w_branch_out)[0]
    br = np.stack([br[0].reshape(KV, GQ, HD, D).transpose(1, 0, 2, 3).reshape(qw, D), br[1], br[2]], 0)
    gates = np.stack([blocks(w_g[:, j * D:(j + 1) * D]) for j in range(NBR)], 1)
    outs = np.stack([blocks(br[j]) for j in range(NBR)], 1)
    w_d = np.concatenate([gates, outs], 3).reshape(DC * NBR, P, DC + BC, P)
    ws = A(chunk_ws)[0]
    ws_smp = np.zeros((SAMPLE, CG, SAMPLE), f32)
    for b in range(B):
        ws_smp[b * T:(b + 1) * T, :, b * T:(b + 1) * T] = ws[:, :T, :T].transpose(2, 0, 1)
    bs = A(chunk_bs)[0]
    xp = np.zeros((PADDED, D), f32)
    xp[:PROMPT] = A(x_prompt)[0]
    xp[PROMPT:TOKENS] = A(x_sample).reshape(SAMPLE, D)
    sinks = A(swa_sinks)[0]
    kc, vc = A(cache_swa_k)[0].reshape(B, WINDOW, KVW), A(cache_swa_v)[0].reshape(B, WINDOW, KVW)
    mk, mv = A(cache_mem_k)[0], A(cache_mem_v)[0].reshape(B, MT, P, MW)
    prompt_bias, sample_bias = _position_constants()
    arrays = dict(
        x=xp, mem=A(mem_prompt)[0], ident=np.eye(P, dtype=f32), iota16=on_all(np.arange(K, dtype=f32)),
        norm1_col=A(norm1_g)[0].reshape(DC, P).T, mem_norm_col=A(mem_norm_g)[0].reshape(DC, P).T,
        w_vvc=chunked(np.concatenate([w_v, w_vc], 1)), w_mem=chunked(A(w_mem_kv)[0]),
        swa_bias=prompt_bias, smp_bias=sample_bias, chunk_g=on_all(chunk_norm_g),
        chunk_b=on_all(bs).reshape(P, CG, P), chunk_b_smp=on_all(np.tile(bs[:, None, :T], (1, B, 1))).reshape(P, CG, SAMPLE),
        ws_T=ws.transpose(2, 0, 1), ws_T_smp=ws_smp,
        gate_b=A(b_gate)[0].reshape(NBR, DC, P).transpose(2, 1, 0).reshape(P, DC * NBR),
        sinks=on_all(sinks),
        smp_sinks=np.tile(np.repeat(sinks.reshape(KV, GQ), T, axis=1), (1, B)).T,
        k_cache_T=kc.transpose(2, 0, 1), v_cache=vc.transpose(1, 0, 2), k_cache_rows=kc, v_cache_rows=vc,
        mk_cache_T=mk.transpose(0, 3, 2, 1).reshape(B, P, MH * MEM),
        mv_cache=mv.transpose(0, 2, 1, 3).reshape(B, P, MT * MW),
        w_b=w_b, w_d=w_d, w_out=chunked(A(w_out)[0]), w_q=chunked(A(peer_wq)[0]),
        subT=A(peer_subkeys)[0].transpose(2, 0, 1), norm2_g=on_all(norm2_g), final_g=on_all(final_norm_g),
        peer_u=A(peer_u)[0], peer_v=A(peer_v)[0],
    )
    outputs = dict(
        y=(TOKENS, D), k_prompt=(WINDOW, KVW), v_prompt=(WINDOW, KVW), mk_out=(MEM, MW), mv_out=(MEM, MW),
        k_sample_old=(B, WINDOW - T, KVW), v_sample_old=(B, WINDOW - T, KVW),
        k_sample_new=(SAMPLE, KVW), v_sample_new=(SAMPLE, KVW), vc_out=(SAMPLE, CW),
    )
    nc = bacc.Bacc("TRN2", target_bir_lowering=False, num_devices=1)
    tensors = {}
    for name, a in arrays.items():
        arrays[name] = np.ascontiguousarray(a)
        assert a.dtype == f32, name
        tensors[name] = nc.dram_tensor(name, a.shape, F32, kind="ExternalInput").ap()
    for name, shape in outputs.items():
        tensors[name] = nc.dram_tensor(name, shape, F32, kind="ExternalOutput").ap()
    tensors["m_scratch"] = nc.dram_tensor("m_scratch", (DC, P, PADDED), F32, kind="Internal").ap()
    build(nc, tensors)
    r = run_bass_kernel_spmd(nc, [arrays], core_ids=[0]).results[0]

    def rolled(name):
        new = r[f"{name}_sample_new"].reshape(B, T, KVW)
        return np.concatenate([r[f"{name}_sample_old"], new], 1).reshape(1, B, WINDOW, KV, HD)

    return (r["y"][:PROMPT].reshape(1, PROMPT, D), r["y"][PROMPT:].reshape(B, T, D),
            r["k_prompt"].reshape(1, 1, WINDOW, KV, HD), r["v_prompt"].reshape(1, 1, WINDOW, KV, HD),
            r["mk_out"].reshape(1, 1, MEM, MH, P), r["mv_out"].reshape(1, 1, MEM, MH, P),
            rolled("k"), rolled("v"), r["vc_out"].reshape(1, B, T, CG, P))
```

```python
from contextlib import ExitStack, contextmanager

import numpy as np

import concourse.bass as bass
from concourse import mybir

F32, U32, BF16 = mybir.dt.float32, mybir.dt.uint32, mybir.dt.bfloat16
ALU = mybir.AluOpType
ACT = mybir.ActivationFunctionType
AX = mybir.AxisListType

P = 128
D = 1024
DC = D // P
PROMPT = 1024
B, T = 8, 4
SAMPLE = B * T
TOKENS = PROMPT + SAMPLE
PTILES = PROMPT // P
TILES = PTILES + 1
PADDED = TILES * P
THIRD = TOKENS // 3
HD = 64
KV = 2
GQ = 4
HEADS = KV * GQ
KVW = KV * HD
WINDOW = 128
SWA_SCALE = HD ** -0.5
CG = 4
CW = CG * P
MEM = 256
MT = MEM // P
MH = 4
MW = MH * P
MEM_SCALE = P ** -0.5
NBR = 3
BC = 4
EPS = 1e-6
NEG = -1e30
PH = 8
K = 16
NK = 128
EXPERTS = NK * NK
PAIRS = PH // 2
SLOTS = PH * K
NB = 4
OPEN = 8
PER_PAIR = (SLOTS // NB - OPEN) // PAIRS
BATCHES = SLOTS // NB
STAGES = 2 + 2 * PAIRS
ARENA = 52400
LOWEST = -3.0e38

FQ, FM, FK, FU = 0, GQ, GQ + MH, GQ + MH + 1
FEATS = FU + CG


class Steps:

    def __init__(self, eng, sem):
        self.eng, self.sem, self.base, self.n = eng, sem, 0, 0
        self.last = None

    def add(self, ins, signal=None, after=None):
        if signal is not None:
            self.last = (signal, after)
            return ins.then_inc(signal, 1)
        self.last = None
        self.n += 1
        return ins.then_inc(self.sem, 1)

    def settle(self):
        if self.last:
            assert self.last[1] is not None
            self.eng.wait_ge(*self.last)
        elif not isinstance(self.base, int) or self.base + self.n:
            self.eng.wait_ge(self.sem, self.base + self.n)

    @contextmanager
    def loop(self, first, end, per):
        with self.eng.Fori(first, end) as i:
            start, outer = self.n, self.base
            self.base, self.last = outer + i * per - first * per, None
            yield i
            assert self.n - start == per, (self.n - start, per)
            self.base, self.last = outer, None
        self.n = start + (end - first) * per


def build(nc, t):
    ctx = ExitStack()
    with ctx:
        def sem(name):
            return ctx.enter_context(nc.semaphore(name))

        ps = ctx.enter_context(nc.psum_tensor("ps", [P, 8, 512], F32))

        def keep(name, shape, dt=F32):
            return ctx.enter_context(nc.sbuf_tensor(f"{name}_sb", [P, *shape], dt))

        ident = keep("ident", [P])
        nothing = keep("nothing", [512], BF16)
        norm1_col, mem_norm_col = keep("norm1_col", [DC]), keep("mem_norm_col", [DC])
        eps = keep("eps", [1])
        stat = keep("stat", [16])
        iota16 = keep("iota16", [K])
        arena = keep("arena", [ARENA])

        class Region:

            def __init__(self, at=0):
                self.at = at

            def take(self, *shape, dt=F32):
                n = int(np.prod(shape)) // (2 if dt == BF16 else 1)
                a = arena[:, self.at:self.at + n]
                self.at += n
                assert self.at <= ARENA, self.at
                if dt != F32:
                    a = a.bitcast(dt)
                names = "abcd"[:len(shape)]
                if len(shape) > 1:
                    kw = {names[k]: shape[k] for k in range(1, len(shape))}
                    a = a.rearrange(f"p ({' '.join(names)}) -> p {' '.join(names)}", **kw)
                return a

        r = Region()
        xnT = r.take(DC, PADDED)
        feats_at = r.at
        feats = r.take(FEATS, PADDED)
        spT = r.take(CG, PADDED)
        v_nat = r.take(TILES, KVW)
        mkT = r.take(MH, MEM)
        mv = r.take(MT, MW)
        w_ring = r.take(NBR, DC + BC, P)
        swa_bias = r.take(HEADS, 2 * P)
        smp_bias = r.take(KV, P + SAMPLE)
        chunk_g = r.take(CW)
        chunk_b = r.take(CG, P)
        chunk_b_smp = r.take(CG, SAMPLE)
        ws_T = r.take(CG, P)
        ws_T_smp = r.take(CG, SAMPLE)
        gate_b = r.take(DC * NBR)
        sinks = r.take(HEADS)
        smp_sinks = r.take(KV)
        knat = r.take(2, KVW)
        row = r.take(8, HEADS)
        temps_at = r.at
        a = Region(feats_at)
        w_vvc = a.take(DC, KVW + CW)
        w_mem = a.take(DC, 2 * MW)
        assert a.at <= feats_at + FEATS * PADDED
        a = Region(temps_at)
        x_t = a.take(D)
        xs = a.take(D)
        squares = a.take(D)
        xn_tile = a.take(DC, P)
        vc_gelu = a.take(CW)
        vc_n = a.take(CW)
        vc_squares = a.take(CW)
        mk_nat = a.take(MT, MW)
        c = Region(temps_at)
        qs = c.take(FK, P)
        ks = c.take(2 * P)
        vs = c.take(2, KVW)
        sc = c.take(HEADS, 2 * P)
        scT = c.take(KV, 2, GQ, P)
        msc = c.take(MH, MEM)
        mscT = c.take(MH, MT, P)
        s = Region(temps_at)
        kcT = s.take(B, P)
        cv = s.take(B, KVW)
        smp_sT = s.take(KV, P)
        smp_snT = s.take(KV, P)
        smp_s = s.take(KV, P + SAMPLE)
        smp_pT = s.take(KV, P)
        smp_pnT = s.take(KV, P)
        smp_mT = s.take(MT, P)
        smp_m = s.take(MEM)
        smp_mpT = s.take(MT, P)
        d = Region(temps_at)
        sig = d.take(TOKENS)
        prod = d.take(TOKENS)
        merged = d.take(PADDED)
        e = Region()
        w_out = e.take(DC, D)
        w_q = e.take(DC, PH * 2 * P)
        subT = e.take(2, NK)
        u_ring = e.take(2, NB, D)
        v_ring = e.take(NB, D)
        m_tile = e.take(DC, P)
        h_next, h_cur = e.take(D), e.take(D)
        n2_next, n2_cur = e.take(D), e.take(D)
        n2T = e.take(DC, P)
        dump, u_dump = e.take(D, dt=BF16), e.take(D)
        y = e.take(D)
        norm2_g, final_g = e.take(D), e.take(D)
        q_nat = e.take(4 * P)
        qT = e.take(4, P)
        rest = e.take(4, NK)
        sv = e.take(4, K)
        si = e.take(4, K, dt=U32)
        sif = e.take(4, K)
        cand = e.take(2, K * K)
        cand2 = rest.rearrange("p (h k) n -> p h (k n)", h=2)
        cv16 = e.take(2, K)
        ci16 = e.take(2, K, dt=U32)
        hilo = e.take(2, 2, K, dt=U32)
        hilof = e.take(2, 2, K)
        match = cand.rearrange("p h (k a) -> p h k a", k=K)
        picked = e.take(2, 2, K)
        shifted = e.take(2, K)
        raised = e.take(2, K)
        g_next, g_cur = e.take(SLOTS), e.take(SLOTS)
        i_next, i_cur = e.take(SLOTS, dt=U32), e.take(SLOTS, dt=U32)
        stage_open = e.take(OPEN * NB, dt=U32)
        stage_pair = e.take(2, PER_PAIR // 2 * NB, dt=U32)
        act4, gelu4, c4 = e.take(2, NB), e.take(2, NB), e.take(2, NB)
        diag = e.take(2, NB, P)
        norm = e.take(8)

        act_, dve_, pool_ = sem("act_steps"), sem("dve_steps"), sem("pool_steps")
        passed = sem("waits_passed")
        consts_in, cols_in = sem("consts_in"), sem("cols_in")
        made = sem("made")
        x_in, mean_sq, rstd, scaled, xT_mm, xn_ready, xn_kept = (sem(n) for n in (
            "x_in", "mean_sq", "rstd", "scaled", "xT_mm", "xn_ready", "xn_kept"))
        v_mm, vc_mm, v_out, vc_out, vc_sq, vc_rstd, vc_ready, sp_mm, sp_out = (sem(n) for n in (
            "v_mm", "vc_mm", "v_out", "vc_out", "vc_sq", "vc_rstd", "vc_ready", "sp_mm", "sp_out"))
        w_a_in, w_mem_in, mkv_mm, mkv_out, mkT_mm, mkT_out = (sem(n) for n in (
            "w_a_in", "w_mem_in", "mkv_mm", "mkv_out", "mkT_mm", "mkT_out"))
        wb_in = [sem(f"wb_in{n}") for n in range(2)]
        b_mm, b_out, chunk_out, knat_mm, knat_out = (sem(n) for n in (
            "b_mm", "b_out", "chunk_out", "knat_mm", "knat_out"))
        c_in, s_mm, s_taken, m_ready, e_ready, p_ready, pT_mm, pT_out, pv_mm, swa_out = (sem(n) for n in (
            "c_in", "s_mm", "s_taken", "m_ready", "e_ready", "p_ready", "pT_mm", "pT_out", "pv_mm", "swa_out"))
        ms_mm, mm_ready, me_ready, mp_ready, mpT_mm, mpT_out, mpv_mm, mem_out = (sem(n) for n in (
            "ms_mm", "mm_ready", "me_ready", "mp_ready", "mpT_mm", "mpT_out", "mpv_mm", "mem_out"))
        smp_in, smp_pe, smp_act, smp_dve = sem("smp_in"), sem("smp_pe"), sem("smp_act"), sem("smp_dve")
        smp_kv_in = [sem(f"smp_kv_in{n}") for n in range(2)]
        smp_kv_used = sem("smp_kv_used")
        wd_in = [sem(f"wd_in{n}") for n in range(NBR)]
        d_mm, d_sig, d_mul, merged_ready, merged_out = (sem(n) for n in (
            "d_mm", "d_sig", "d_mul", "merged_ready", "merged_out"))
        we_in, m_in, h_in, h_mm, h_sum, root, n2_ready, n2T_mm, n2T_out = (sem(n) for n in (
            "we_in", "m_in", "h_in", "h_mm", "h_sum", "root", "n2_ready", "n2T_mm", "n2T_out"))
        q_mm, q_out, qT_mm, qT_out, key_mm, keys_taken, shifted_ready, raised_ready = (sem(n) for n in (
            "q_mm", "q_out", "qT_mm", "qT_out", "key_mm", "keys_taken", "shifted_ready", "raised_ready"))
        chosen, moved, h_moved, staged, dots, gelus, c_ready, diags, v_used = (sem(n) for n in (
            "chosen", "moved", "h_moved", "staged", "dots", "gelus", "c_ready", "diags", "v_used"))
        u_in = [[sem(f"u_in{n}{j}") for j in range(NB)] for n in range(2)]
        v_in = [sem(f"v_in{j}") for j in range(NB)]
        acc_mm, acc_taken, y_root, y_ready, y_out = (sem(n) for n in (
            "acc_mm", "acc_taken", "y_root", "y_ready", "y_out"))
        stored, stored_k = sem("stored"), sem("stored_k")

        def cols(n):
            return bass.ds(n * P, P)

        def alone(eng):
            eng.sem_inc(passed, 1)

        def need(eng, sem, value):
            if not isinstance(value, int) or value > 0:
                eng.wait_ge(sem, value)

        def wide(a, *shape):
            return a.unsqueeze(a.ndim).broadcast_to([a.shape[0], *shape])

        LOADS = ["swa_bias", "smp_bias", "chunk_g", "chunk_b", "chunk_b_smp", "ws_T", "ws_T_smp",
                 "gate_b", "sinks", "smp_sinks"]
        where = dict(swa_bias=swa_bias, smp_bias=smp_bias, chunk_g=chunk_g, chunk_b=chunk_b,
                     ws_T=ws_T, gate_b=gate_b, sinks=sinks, smp_sinks=smp_sinks,
                     chunk_b_smp=chunk_b_smp, ws_T_smp=ws_T_smp[0:SAMPLE])
        block = ctx.enter_context(nc.Block())

        @block.sync
        def _(sp):
            def send(out, in_, s):
                return sp.dma_start(out, in_).then_inc(s, 16)

            send(x_t[:, :], t["x"][0:P, :], x_in)
            send(ident[:, :], t["ident"], cols_in)
            send(norm1_col[:, :], t["norm1_col"], cols_in)
            send(mem_norm_col[:, :], t["mem_norm_col"], cols_in)
            send(iota16[:, :], t["iota16"], cols_in)
            send(w_vvc[:, :, :], t["w_vvc"], w_a_in)
            for name in LOADS:
                send(where[name], t[name], consts_in)
            send(w_mem[:, :, :], t["w_mem"], w_mem_in)
            with sp.Fori(1, TILES) as i:
                sp.wait_ge(mean_sq, i)
                sp.wait_ge(scaled, i)
                send(x_t[:, :], t["x"][cols(i), :], x_in)
            for m in range(MT):
                sp.wait_ge(mean_sq, TILES + m)
                sp.wait_ge(scaled, TILES + m)
                send(x_t[:, :], t["mem"][m * P:(m + 1) * P, :], x_in)
            sp.wait_ge(vc_ready, TILES)
            send(t["vc_out"], vc_n[0:SAMPLE, :], stored)
            sp.wait_ge(v_out, TILES)
            send(t["v_prompt"], v_nat[:, PTILES - 1, :], stored)
            send(t["v_sample_new"], v_nat[0:SAMPLE, PTILES, :], stored)
            for m in range(MT):
                sp.wait_ge(mkv_out, 2 * m + 2)
                send(t["mk_out"][m * P:(m + 1) * P, :], mk_nat[:, m, :], stored)
                send(t["mv_out"][m * P:(m + 1) * P, :], mv[:, m, :], stored)
            for name in ("k", "v"):
                send(t[f"{name}_sample_old"], t[f"{name}_cache_rows"][:, T:WINDOW, :], stored_k)

            def load_b(n, slot):
                send(w_ring[:, slot, 0:DC, :], t["w_b"][bass.ds(n, 1)].rearrange("a p c m -> p (a c) m"), wb_in[slot])

            load_b(0, 0)
            load_b(1, 1)
            with sp.Fori(1, 4) as i:
                for slot in range(2):
                    sp.wait_ge(b_mm, 6 * i + 3 * slot - 3)
                    load_b(2 * i + slot, slot)
            sp.wait_ge(b_mm, 3 * (FK - 1))
            load_b(FK, 0)
            with sp.Fori(0, 2) as i:
                for k in range(2):
                    sp.wait_ge(b_mm, 6 * i + 3 * (FU - 1 + k))
                    load_b(2 * i + FU + k, (FU + k) % 2)
            sp.wait_ge(knat_out, 1)
            send(t["k_prompt"], knat[:, 0, :], stored_k)
            send(t["k_sample_new"], knat[0:SAMPLE, 1, :], stored_k)

            sp.wait_ge(mem_out, PTILES)
            sp.wait_ge(swa_out, PTILES)
            sp.wait_ge(mpv_mm, PTILES)
            send(kcT[:, :, :], t["k_cache_T"], smp_in)
            send(cv[:, :, :], t["v_cache"], smp_in)
            for n in range(2 * B):
                if n >= 2:
                    sp.wait_ge(smp_kv_used, n - 1)
                src = t["mk_cache_T"] if n < B else t["mv_cache"]
                send(w_ring[:, n % 2, 0:DC, :].rearrange("p c m -> p (c m)"), src[n % B], smp_kv_in[n % 2])

            def load_d(i, j):
                send(w_ring[:, j, :, :], t["w_d"][bass.ds(3 * i + j, 1)].rearrange("a p c m -> p (a c) m"), wd_in[j])

            sp.wait_ge(smp_kv_used, 2 * B)
            for j in range(NBR):
                load_d(0, j)
            with sp.Fori(1, DC) as i:
                for j in range(NBR):
                    sp.wait_ge(d_mm, 9 * i + (3 * j - 6))
                    load_d(i, j)
                sp.wait_ge(merged_ready, i)
                send(t["m_scratch"][bass.ds(i - 1, 1)].rearrange("a p n -> (a p) n"), merged[:, :], merged_out)
            sp.wait_ge(merged_ready, DC)
            send(t["m_scratch"][DC - 1], merged[:, :], merged_out)

            sp.wait_ge(d_mm, 3 * NBR * DC)
            sp.wait_ge(merged_out, 16 * DC)
            sp.wait_ge(stored, 16 * (3 + 2 * MT))
            sp.wait_ge(stored_k, 16 * 4)
            send(w_out[:, :, :], t["w_out"], we_in)
            send(w_q[:, :, :], t["w_q"], we_in)
            send(subT[:, :, :], t["subT"], we_in)
            send(norm2_g, t["norm2_g"], we_in)
            send(final_g, t["final_g"], we_in)

            def load_m(f):
                send(m_tile[:, :, :], t["m_scratch"][:, :, cols(f)].rearrange("c p n -> p c n"), m_in)

            def load_h(f):
                send(h_next[:, :], t["x"][cols(f), :], h_in)

            load_m(0)
            load_h(0)
            sp.wait_ge(h_mm, 1)
            load_m(1)
            sp.wait_ge(h_moved, 1)
            load_h(1)
            sp.wait_ge(h_mm, 2)
            load_m(2)
            with sp.Fori(1, PTILES - 1) as i:
                sp.wait_ge(y_ready, i)
                send(t["y"][cols(i - 1), :], y[:, :], y_out)
                sp.wait_ge(h_moved, i + 1)
                load_h(i + 1)
                sp.wait_ge(h_mm, i + 2)
                load_m(i + 2)
            sp.wait_ge(y_ready, PTILES - 1)
            send(t["y"][cols(PTILES - 2), :], y[:, :], y_out)
            sp.wait_ge(h_moved, PTILES)
            load_h(PTILES)
            sp.wait_ge(y_ready, PTILES)
            send(t["y"][cols(PTILES - 1), :], y[:, :], y_out)
            sp.wait_ge(y_ready, TILES)
            send(t["y"][PROMPT:TOKENS, :], y[0:SAMPLE, :], y_out)
            sp.wait_ge(y_out, 16 * TILES)

        @block.tensor
        def _(pe):
            mm, tr = nc.tensor.matmul, nc.tensor.transpose
            xT = ps[:, 0:2, :].rearrange("p b (c n) -> p (b c) n", n=P)

            def transpose_x(n):
                pe.wait_ge(scaled, n + 1)
                pe.wait_ge(xn_ready, n)
                for c in range(DC):
                    last = tr(xT[:, c, :], xs[:, c * P:(c + 1) * P], ident[:, :])
                last.then_inc(xT_mm, 1)

            def tile_a(n, sample=False):
                transpose_x(n)
                pe.wait_ge(xn_ready, n + 1)
                pe.wait_ge(v_out, n)
                pe.wait_ge(vc_out, n)
                for c in range(DC):
                    last = mm(ps[:, 2, 0:KVW], xn_tile[:, c, :], w_vvc[:, c, 0:KVW], start=c == 0, stop=c == DC - 1)
                last.then_inc(v_mm, 1)
                for c in range(DC):
                    last = mm(ps[:, 3, :], xn_tile[:, c, :], w_vvc[:, c, KVW:KVW + CW], start=c == 0, stop=c == DC - 1)
                last.then_inc(vc_mm, 1)
                pe.wait_ge(vc_ready, n + 1)
                pe.wait_ge(sp_out, n)
                for g in range(CG):
                    if sample:
                        last = mm(ps[:, 4, g * SAMPLE:(g + 1) * SAMPLE], vc_n[0:SAMPLE, g * P:(g + 1) * P],
                                  ws_T_smp[0:SAMPLE, g, :], start=True, stop=True)
                    else:
                        last = mm(ps[:, 4, g * P:(g + 1) * P], vc_n[:, g * P:(g + 1) * P], ws_T[:, g, :],
                                  start=True, stop=True)
                last.then_inc(sp_mm, 1)

            pe.wait_ge(cols_in, 64)
            pe.wait_ge(w_a_in, 16)
            pe.wait_ge(made, 2)
            with pe.Fori(0, PTILES) as i:
                tile_a(i)
            tile_a(PTILES, sample=True)

            pe.wait_ge(w_mem_in, 16)
            for m in range(MT):
                transpose_x(TILES + m)
                pe.wait_ge(xn_ready, TILES + m + 1)
                pe.wait_ge(mkv_out, 2 * m)
                for half in range(2):
                    for c in range(DC):
                        last = mm(ps[:, 5 + half, :], xn_tile[:, c, :], w_mem[:, c, half * MW:(half + 1) * MW],
                                  start=c == 0, stop=c == DC - 1)
                    last.then_inc(mkv_mm, 1)
                pe.wait_ge(mkv_out, 2 * m + 1)
                pe.wait_ge(mkT_out, m)
                for h in range(MH):
                    last = tr(ps[:, 7, h * P:(h + 1) * P], mk_nat[:, m, h * P:(h + 1) * P], ident[:, :])
                last.then_inc(mkT_mm, 1)

            def block_b(n, slot, uses, first=False):
                pe.wait_ge(wb_in[slot], 16 * uses)
                for th in range(3):
                    if not first:
                        pe.wait_ge(b_out, 3 * n + (th - 2))
                    for c in range(DC):
                        last = mm(ps[:, 5 + th, 0:THIRD], w_ring[:, slot, c, :], xnT[:, c, th * THIRD:(th + 1) * THIRD],
                                  start=c == 0, stop=c == DC - 1)
                    last.then_inc(b_mm, 1)

            pe.wait_ge(xn_kept, TILES)
            pe.wait_ge(mkT_out, MT)
            pe.wait_ge(mkv_out, 2 * MT)
            block_b(0, 0, 1, first=True)
            block_b(1, 1, 1)
            with pe.Fori(1, 4) as i:
                for slot in range(2):
                    block_b(2 * i + slot, slot, i + 1)
            block_b(FK, 0, 5)
            with pe.Fori(0, 2) as i:
                for k in range(2):
                    slot = (FU + k) % 2
                    block_b(2 * i + FU + k, slot, i + (5 if slot else 6))
            pe.wait_ge(b_out, 3 * FEATS)
            tr(ps[:, 0, 0:KVW], feats[:, FK, PROMPT - P:PROMPT], ident[:, :])
            tr(ps[0:SAMPLE, 1, 0:KVW], feats[:, FK, PROMPT:TOKENS], ident[:, :]).then_inc(knat_mm, 1)
            pe.wait_ge(knat_out, 1)

            def tile_c(n, first=False):
                pe.wait_ge(c_in, 3 * n + 3)
                if not first:
                    pe.wait_ge(swa_out, n)
                    pe.wait_ge(mem_out, n)
                keys = slice(P, 2 * P) if first else slice(0, 2 * P)
                for kv in range(KV):
                    part = slice(kv * HD, (kv + 1) * HD)
                    for g in range(GQ):
                        at = (g % 2) * 2 * P
                        last = mm(ps[:, 2 * kv + g // 2, at + keys.start:at + keys.stop], qs[part, FQ + g, :],
                                  ks[part, keys], start=True, stop=True)
                last.then_inc(s_mm, 1)
                pe.wait_ge(s_taken, n + 1)
                for h in range(MH):
                    last = mm(ps[:, 1 + h // 2, (h % 2) * MEM:(h % 2 + 1) * MEM], qs[:, FM + h, :], mkT[:, h, :],
                              start=True, stop=True)
                last.then_inc(ms_mm, 1)
                pe.wait_ge(p_ready, n + 1)
                if not first:
                    pe.wait_ge(mpT_out, n)
                    pe.wait_ge(pT_out, 2 * n)
                halves = (1,) if first else (0, 1)
                for kv in range(KV):
                    for half in halves:
                        for g in range(GQ):
                            last = tr(ps[:, 4 + 2 * kv + half, g * P:(g + 1) * P],
                                      sc[:, kv * GQ + g, half * P:(half + 1) * P], ident[:, :])
                    last.then_inc(pT_mm, 1)
                pe.wait_ge(pT_out, 2 * n + 2)
                for kv in range(KV):
                    part = slice(kv * HD, (kv + 1) * HD)
                    for half in halves:
                        last = mm(ps[part, 0, :], vs[:, half, part], scT[:, kv, half, :, :].rearrange("p g n -> p (g n)"),
                                  start=half == halves[0], stop=half == 1)
                last.then_inc(pv_mm, 1)
                pe.wait_ge(mp_ready, n + 1)
                for h in range(MH):
                    for m in range(MT):
                        k = h * MT + m
                        last = tr(ps[:, 4 + k // 4, (k % 4) * P:(k % 4 + 1) * P], msc[:, h, m * P:(m + 1) * P], ident[:, :])
                last.then_inc(mpT_mm, 1)
                pe.wait_ge(mpT_out, n + 1)
                for h in range(MH):
                    for m in range(MT):
                        last = mm(ps[:, 3, h * P:(h + 1) * P], mv[:, m, h * P:(h + 1) * P], mscT[:, h, m, :],
                                  start=m == 0, stop=m == MT - 1)
                last.then_inc(mpv_mm, 1)

            tile_c(0, first=True)
            with pe.Fori(1, PTILES) as i:
                tile_c(i)

            pe.wait_ge(mem_out, PTILES)
            pe.wait_ge(swa_out, PTILES)
            pe.wait_ge(smp_in, 32)
            for kv in range(KV):
                part = slice(kv * HD, (kv + 1) * HD)
                for b in range(B):
                    q = feats[part, FQ:FQ + GQ, PROMPT + b * T:PROMPT + (b + 1) * T]
                    at = slice(b * GQ * T, (b + 1) * GQ * T)
                    mm(ps[:, kv, at], kcT[part, b, :], q, start=True, stop=True)
                    last = mm(ps[0:SAMPLE, 2 + kv, at], feats[part, FK, PROMPT:TOKENS], q, start=True, stop=True)
            last.then_inc(smp_pe, 1)
            pe.wait_ge(smp_act, 1)
            for kv in range(KV):
                at = kv * 2 * P
                tr(ps[:, 4, at:at + P], smp_sT[:, kv, :], ident[:, :])
                last = tr(ps[:, 4, at + P:at + P + SAMPLE], smp_snT[0:SAMPLE, kv, :], ident[0:SAMPLE, 0:SAMPLE])
            last.then_inc(smp_pe, 1)
            for b in range(B):
                pe.wait_ge(smp_kv_in[b % 2], 16 * (b // 2 + 1))
                km = w_ring[:, b % 2, 0:DC, :].rearrange("p c m -> p (c m)").rearrange("p (h m) -> p h m", h=MH)
                for h in range(MH):
                    for m in range(MT):
                        at = m * P + (b * MH + h) * T
                        last = mm(ps[:, 5, at:at + T], km[:, h, m * P:(m + 1) * P],
                                  feats[:, FM + h, PROMPT + b * T:PROMPT + (b + 1) * T], start=True, stop=True)
                last.then_inc(smp_kv_used, 1)
            pe.wait_ge(smp_dve, 2)
            for kv in range(KV):
                tr(ps[:, 6, kv * P:(kv + 1) * P], smp_s[:, kv, 0:P], ident[:, :])
                last = tr(ps[0:SAMPLE, 7, kv * P:(kv + 1) * P], smp_s[:, kv, P:P + SAMPLE], ident[:, :])
            last.then_inc(smp_pe, 1)
            pe.wait_ge(smp_act, 3)
            for kv in range(KV):
                part = slice(kv * HD, (kv + 1) * HD)
                for b in range(B):
                    at = slice(b * GQ * T, (b + 1) * GQ * T)
                    mm(ps[part, 0, at], cv[:, b, part], smp_pT[:, kv, at], start=True, stop=False)
                    last = mm(ps[part, 0, at], v_nat[0:SAMPLE, PTILES, part], smp_pnT[0:SAMPLE, kv, at],
                              start=False, stop=True)
            last.then_inc(smp_pe, 1)
            pe.wait_ge(smp_act, 4)
            for m in range(MT):
                last = tr(ps[:, 1, m * P:(m + 1) * P], smp_mT[:, m, :], ident[:, :])
            last.then_inc(smp_pe, 1)
            pe.wait_ge(smp_dve, 5)
            for m in range(MT):
                last = tr(ps[:, 2, m * P:(m + 1) * P], smp_m[:, m * P:(m + 1) * P], ident[:, :])
            last.then_inc(smp_pe, 1)
            pe.wait_ge(smp_act, 6)
            for b in range(B):
                pe.wait_ge(smp_kv_in[b % 2], 16 * ((B + b) // 2 + 1))
                vm = w_ring[:, b % 2, 0:DC, :].rearrange("p c m -> p (c m)").rearrange("p (m w) -> p m w", m=MT)
                for h in range(MH):
                    at = slice((b * MH + h) * T, (b * MH + h + 1) * T)
                    for m in range(MT):
                        last = mm(ps[:, 3, at], vm[:, m, h * P:(h + 1) * P], smp_mpT[:, m, at],
                                  start=m == 0, stop=m == MT - 1)
                last.then_inc(smp_kv_used, 1)

            def unit(i, j, first=False):
                pe.wait_ge(wd_in[j], 16 * (i + 1))
                branch = feats[:, (FQ, FU, FM)[j]:(FQ, FU, FM)[j] + BC, :]
                for th in range(3):
                    part = slice(th * THIRD, (th + 1) * THIRD)
                    if not first:
                        pe.wait_ge(d_sig, 9 * i + (3 * j + th - 2))
                        pe.wait_ge(d_mul, 9 * i + (3 * j + th - 2))
                    for c in range(DC):
                        mm(ps[:, th, 0:THIRD], w_ring[:, j, c, :], xnT[:, c, part], start=c == 0, stop=c == DC - 1)
                    for c in range(BC):
                        last = mm(ps[:, 3 + th, 0:THIRD], w_ring[:, j, DC + c, :], branch[:, c, part],
                                  start=c == 0, stop=c == BC - 1)
                    last.then_inc(d_mm, 1)

            pe.wait_ge(smp_dve, 6)
            pe.wait_ge(chunk_out, CG)
            for j in range(NBR):
                unit(0, j, first=j == 0)
            with pe.Fori(1, DC) as i:
                for j in range(NBR):
                    unit(i, j)

            h_ps = ps[:, 4:6, :]
            n2T_ps = h_ps.rearrange("p b (c n) -> p (b c) n", n=P)

            def front_h(f, part):
                half, at = divmod(part, 2)
                if part == 0:
                    pe.wait_ge(m_in, 16 * (f + 1))
                    need(pe, n2T_out, f)
                for c in range(DC // 2 * at, DC // 2 * (at + 1)):
                    last = mm(h_ps[:, half, :], m_tile[:, c, :], w_out[:, c, half * 512:(half + 1) * 512],
                              start=c == 0, stop=c == DC - 1)
                if part == 3:
                    last.then_inc(h_mm, 1)

            def front_n2T(f):
                pe.wait_ge(n2_ready, f + 1)
                for c in range(DC):
                    last = tr(n2T_ps[:, c, :], n2_next[:, c * P:(c + 1) * P], ident[:, :])
                last.then_inc(n2T_mm, 1)

            def front_q(f, p, part):
                if part == 0:
                    need(pe, keys_taken, PAIRS * f + p)
                    pe.wait_ge(n2T_out, f + 1)
                for c in range(DC // 2 * part, DC // 2 * (part + 1)):
                    last = mm(ps[:, 6:7, :], n2T[:, c, :], w_q[:, c:c + 1, bass.ds(p * 4 * P, 4 * P)],
                              start=c == 0, stop=c == DC - 1)
                if part:
                    last.then_inc(q_mm, 1)

            def front_qT(g):
                pe.wait_ge(q_out, g + 1)
                for k in range(4):
                    last = tr(ps[:, 7, k * P:(k + 1) * P], q_nat[:, k * P:(k + 1) * P], ident[:, :])
                last.then_inc(qT_mm, 1)

            def front_keys(g):
                pe.wait_ge(qT_out, g + 1)
                for k in range(4):
                    last = mm(ps[:, 6, k * NK:(k + 1) * NK], qT[:, k, :], subT[:, k % 2, :], start=True, stop=True)
                last.then_inc(key_mm, 1)

            def open_acc(n):
                need(pe, acc_taken, n)
                for half in range(2):
                    mm(ps[:, half, :], nothing[:, 0:P], nothing[:, :], start=True, stop=False, skip_group_check=True)

            def add_v(batch, b, R, slots=range(NB)):
                for j in slots:
                    pe.wait_ge(v_in[j], 16 * batch + 16)
                    pe.wait_ge(diags, 4 * batch + (j + 1))
                    if R < P:
                        alone(pe)
                    for half in range(2):
                        last = mm(ps[0:R, half, :], diag[0:R, b % 2, j, 0:R], v_ring[0:R, j, half * 512:(half + 1) * 512],
                                  start=False, stop=False, skip_group_check=True)
                    last.then_inc(v_used, 1)

            def close_acc(n, R=P):
                add_v(BATCHES * n + (BATCHES - 1), BATCHES - 1, R)
                for half in range(2):
                    last = mm(ps[:, half, :], nothing[:, 0:P], nothing[:, :], start=False, stop=True, skip_group_check=True)
                last.then_inc(acc_mm, 1)

            def tile_e(n, f, R=P, follows=True):
                for b in range(OPEN):
                    if b == 0 and follows:
                        close_acc(n - 1)
                    if b == 1:
                        open_acc(n)
                    if b:
                        add_v(BATCHES * n + (b - 1), b - 1, R)
                    if f is not None:
                        if b < 4:
                            front_h(f, b)
                        elif b == 6:
                            front_n2T(f)
                with pe.Fori(0, PAIRS) as p:
                    for b in range(PER_PAIR):
                        add_v(BATCHES * n + PER_PAIR * p + (OPEN + b - 1), (b - 1) % 2, R, (0, 1))
                        if f is not None:
                            if b == 0:
                                front_q(f, p, 0)
                            elif b == 1:
                                front_qT(4 * f + p)
                            elif b == 2:
                                front_keys(4 * f + p)
                        add_v(BATCHES * n + PER_PAIR * p + (OPEN + b - 1), (b - 1) % 2, R, (2, 3))
                        if f is not None and b == 0:
                            front_q(f, p, 1)

            def first_keys(p):
                front_q(0, p, 0)
                front_q(0, p, 1)
                front_qT(p)
                front_keys(p)

            pe.wait_ge(we_in, 16 * 5)
            pe.wait_ge(d_sig, 3 * NBR * DC)
            pe.wait_ge(d_mul, 3 * NBR * DC)
            for part in range(4):
                front_h(0, part)
            front_n2T(0)
            first_keys(0)
            with pe.Fori(1, PAIRS) as p:
                first_keys(p)
            tile_e(0, 1, follows=False)
            with pe.Fori(1, PTILES) as i:
                tile_e(i, i + 1)
            tile_e(PTILES, None, R=SAMPLE)
            close_acc(PTILES, R=SAMPLE)

        @block.scalar
        def _(act):
            fn = nc.scalar.activation

            def mean_square(n):
                act.wait_ge(x_in, 16 * n + 16)
                act.wait_ge(rstd, n)
                fn(squares[:, :], x_t[:, :], ACT.Square, scale=D ** -0.5, accum_out=stat[:, 0:1]).then_inc(mean_sq, 1)
                act.wait_ge(mean_sq, n + 1)

            def tile_a(n):
                mean_square(n)
                act.wait_ge(v_mm, n + 1)
                alone(act)
                fn(v_nat[:, bass.ds(n, 1), :], ps[:, 2:3, 0:KVW], ACT.Copy).then_inc(v_out, 1)
                act.wait_ge(vc_mm, n + 1)
                act.wait_ge(vc_ready, n)
                fn(vc_gelu[:, :], ps[:, 3, :], ACT.Gelu).then_inc(vc_out, 1)
                act.wait_ge(vc_out, n + 1)
                act.wait_ge(vc_rstd, n)
                fn(vc_squares[:, :], vc_gelu[:, :], ACT.Square, accum_out=stat[:, 4:5]).then_inc(vc_sq, 1)
                act.wait_ge(vc_sq, n + 1)

            with act.Fori(0, TILES) as i:
                tile_a(i)
            for m in range(MT):
                mean_square(TILES + m)
                act.wait_ge(mkv_mm, 2 * m + 1)
                fn(mk_nat[:, m, :], ps[:, 5, :], ACT.Copy).then_inc(mkv_out, 1)
                act.wait_ge(mkv_mm, 2 * m + 2)
                fn(mv[:, m, :], ps[:, 6, :], ACT.Copy).then_inc(mkv_out, 1)

            def block_b(n, func):
                for th in range(3):
                    act.wait_ge(b_mm, 3 * n + (th + 1))
                    alone(act)
                    fn(feats[:, bass.ds(n, 1), th * THIRD:(th + 1) * THIRD], ps[:, 5 + th:6 + th, 0:THIRD], func)\
                        .then_inc(b_out, 1)

            with act.Fori(0, FU) as i:
                block_b(i, ACT.Copy)
            with act.Fori(0, CG) as i:
                block_b(i + FU, ACT.Gelu)

            act.wait_ge(xn_ready, TILES + MT)

            def tile_c(n, first=False):
                keys = slice(P, 2 * P) if first else slice(0, 2 * P)
                act.wait_ge(m_ready, n + 1)
                for h in range(HEADS):
                    fn(sc[:, h, keys], sc[:, h, keys], ACT.Exp, bias=row[:, 1, h:h + 1], accum_out=row[:, 3, h:h + 1])
                fn(row[:, 4, :], row[:, 2, :], ACT.Exp).then_inc(e_ready, 1)
                act.wait_ge(mm_ready, n + 1)
                if not first:
                    act.wait_ge(mpT_mm, n)
                for h in range(MH):
                    last = fn(msc[:, h, :], ps[:, 1 + h // 2, (h % 2) * MEM:(h % 2 + 1) * MEM], ACT.Exp,
                              bias=row[:, 5, h:h + 1], scale=MEM_SCALE, accum_out=row[:, 6, h:h + 1])
                last.then_inc(me_ready, 1)
                for kv in range(KV):
                    act.wait_ge(pT_mm, 2 * n + (kv + 1))
                    if not first:
                        act.wait_ge(pv_mm, n)
                    lo = 1 if first else 0
                    fn(scT[:, kv, lo:2, :, :].rearrange("p a g n -> p a (g n)"), ps[:, 4 + 2 * kv + lo:6 + 2 * kv, :],
                       ACT.Copy).then_inc(pT_out, 1)
                act.wait_ge(mpT_mm, n + 1)
                if not first:
                    act.wait_ge(mpv_mm, n)
                fn(mscT[:, :, :, :].rearrange("p h m n -> p (h m n)"), ps[:, 4:6, :].rearrange("p a n -> p (a n)"),
                   ACT.Copy).then_inc(mpT_out, 1)

            tile_c(0, first=True)
            with act.Fori(1, PTILES) as i:
                tile_c(i)

            act.wait_ge(mpv_mm, PTILES)
            act.wait_ge(smp_pe, 1)
            fn(smp_sT[:, :, :], ps[:, 0:2, 0:P], ACT.Copy)
            fn(smp_snT[0:SAMPLE, :, :], ps[0:SAMPLE, 2:4, 0:P], ACT.Copy).then_inc(smp_act, 1)
            act.wait_ge(smp_dve, 1)
            for kv in range(KV):
                fn(smp_s[:, kv, :], smp_s[:, kv, :], ACT.Exp, bias=row[:, 1, kv:kv + 1], accum_out=row[:, 3, kv:kv + 1])
            fn(row[:, 4, 0:KV], row[:, 2, 0:KV], ACT.Exp).then_inc(smp_act, 1)
            act.wait_ge(smp_pe, 3)
            fn(smp_pT[:, :, :].rearrange("p a n -> p (a n)"), ps[:, 6, 0:KV * P], ACT.Copy)
            fn(smp_pnT[0:SAMPLE, :, :].rearrange("p a n -> p (a n)"), ps[0:SAMPLE, 7, 0:KV * P], ACT.Copy)\
                .then_inc(smp_act, 1)
            act.wait_ge(smp_kv_used, B)
            fn(smp_mT[:, :, :].rearrange("p a n -> p (a n)"), ps[:, 5, 0:MEM], ACT.Copy).then_inc(smp_act, 1)
            act.wait_ge(smp_dve, 4)
            fn(smp_m[:, :], ps[:, 1, 0:MEM], ACT.Exp, bias=row[:, 5, 0:1], scale=MEM_SCALE,
               accum_out=row[:, 6, 0:1]).then_inc(smp_act, 1)
            act.wait_ge(smp_pe, 6)
            fn(smp_mpT[:, :, :].rearrange("p a n -> p (a n)"), ps[:, 2, 0:MEM], ACT.Copy).then_inc(smp_act, 1)

            def unit(i, j, first=False):
                for th in range(3):
                    act.wait_ge(d_mm, 9 * i + (3 * j + th + 1))
                    if not first:
                        act.wait_ge(d_mul, 9 * i + (3 * j + th - 2))
                    alone(act)
                    fn(sig[:, th * THIRD:(th + 1) * THIRD], ps[:, th, 0:THIRD], ACT.Sigmoid,
                       bias=gate_b[:, bass.ds(3 * i + j, 1)]).then_inc(d_sig, 1)

            act.wait_ge(smp_kv_used, 2 * B)
            for j in range(NBR):
                unit(0, j, first=j == 0)
            with act.Fori(1, DC) as i:
                for j in range(NBR):
                    unit(i, j)

            A = Steps(act, act_)

            def square_root(a, R, signal):
                A.add(fn(dump[0:R, :], a[0:R, :], ACT.Square, scale=D ** -0.5, accum_out=norm[0:R, 0:1]))
                A.settle()
                A.add(fn(norm[0:R, 1:2], norm[0:R, 0:1], ACT.Sqrt, bias=eps[0:R, 0:1]), signal)

            def front_norm(f):
                act.wait_ge(h_sum, f + 1)
                square_root(h_next, P, root)

            def front_n2T(f):
                act.wait_ge(n2T_mm, f + 1)
                A.add(fn(n2T[:, :, :].rearrange("p c n -> p (c n)"), ps[:, 4:6, :].rearrange("p a n -> p (a n)"),
                         ACT.Copy), n2T_out)

            def front_q(g):
                act.wait_ge(q_mm, g + 1)
                A.add(fn(q_nat[:, :], ps[:, 6, :], ACT.Copy), q_out)

            def front_qT(g):
                act.wait_ge(qT_mm, g + 1)
                A.add(fn(qT[:, :, :].rearrange("p k n -> p (k n)"), ps[:, 7, :], ACT.Copy), qT_out)

            def front_exp(g):
                act.wait_ge(shifted_ready, g + 1)
                A.add(fn(raised[:, :, :].rearrange("p h k -> p (h k)"), shifted[:, :, :].rearrange("p h k -> p (h k)"),
                         ACT.Exp), raised_ready)

            def gelu(batch, b, R):
                act.wait_ge(dots, 4 * batch + 4)
                A.add(fn(gelu4[0:R, b % 2, :], act4[0:R, b % 2, :], ACT.Gelu), gelus)

            def make_diag(batch, b, R):
                act.wait_ge(c_ready, batch + 1)
                need(act, v_used, 4 * batch - 4)
                for j in range(NB):
                    A.add(fn(diag[0:R, b % 2, j, 0:R], ident[0:R, 0:R], ACT.Copy, scale=c4[0:R, b % 2, j:j + 1]), diags)

            def final_root(n, R=P):
                act.wait_ge(acc_taken, n + 1)
                square_root(h_cur, R, y_root)

            def tile_e(n, f, R=P, follows=True):
                for b in range(OPEN):
                    if b:
                        make_diag(BATCHES * n + (b - 1), b - 1, R)
                    elif follows:
                        make_diag(BATCHES * n - 1, BATCHES - 1, P)
                    if b == 1 and follows:
                        final_root(n - 1)
                    gelu(BATCHES * n + b, b, R)
                    if f is not None:
                        if b == 4:
                            front_norm(f)
                        elif b == 6:
                            front_n2T(f)
                with act.Fori(0, PAIRS) as p:
                    for b in range(PER_PAIR):
                        if f is not None:
                            if b == 1:
                                front_q(4 * f + p)
                            elif b == 2:
                                front_qT(4 * f + p)
                            elif b == 5:
                                front_exp(4 * f + p)
                        make_diag(BATCHES * n + PER_PAIR * p + (OPEN + b - 1), (b - 1) % 2, R)
                        gelu(BATCHES * n + PER_PAIR * p + (OPEN + b), b, R)

            def first_keys(p):
                front_q(p)
                front_qT(p)
                front_exp(p)

            act.wait_ge(we_in, 16 * 5)
            front_norm(0)
            front_n2T(0)
            first_keys(0)
            with act.Fori(1, PAIRS) as p:
                first_keys(p)
            tile_e(0, 1, follows=False)
            with A.loop(1, PTILES, 2) as i:
                tile_e(i, i + 1)
            tile_e(PTILES, None, R=SAMPLE)
            make_diag(BATCHES * TILES - 1, BATCHES - 1, SAMPLE)
            final_root(PTILES, SAMPLE)

        @block.vector
        def _(dve):
            V = Steps(dve, dve_)
            v = nc.vector

            V.add(v.memset(nothing[:, :], 0.0))
            V.add(v.memset(eps[:, :], EPS))
            dve.wait_ge(cols_in, 64)
            dve.wait_ge(consts_in, 16 * len(LOADS))

            def xn(n, col, kept):
                dve.wait_ge(rstd, n + 1)
                dve.wait_ge(xT_mm, n)
                v.tensor_scalar(xs[:, :], x_t[:, :], stat[:, 2:3], None, ALU.mult).then_inc(scaled, 1)
                dve.wait_ge(xT_mm, n + 1)
                dve.wait_ge(xn_kept, kept)
                xT = ps[:, 0:2, :].rearrange("p b (c n) -> p (b c) n", n=P)
                v.tensor_tensor(xn_tile[:, :, :], xT, wide(col[:, :], DC, P), ALU.mult).then_inc(xn_ready, 1)

            def tile_a(n, sample=False):
                dve.wait_ge(vc_mm, n)
                xn(n, norm1_col, n)
                dve.wait_ge(vc_rstd, n + 1)
                dve.wait_ge(sp_mm, n)
                v.scalar_tensor_tensor(vc_n[:, :], vc_gelu[:, :], stat[:, 6:7], chunk_g, ALU.mult, ALU.mult)\
                    .then_inc(vc_ready, 1)
                dve.wait_ge(sp_mm, n + 1)
                if sample:
                    v.tensor_tensor(spT[:, :, PROMPT:TOKENS], ps[:, 4, 0:CG * SAMPLE].rearrange("p (g n) -> p g n", g=CG),
                                    chunk_b_smp[:, :, :], ALU.add).then_inc(sp_out, 1)
                else:
                    v.tensor_tensor(spT[:, :, cols(n)], ps[:, 4, :].rearrange("p (g n) -> p g n", g=CG),
                                    chunk_b[:, :, :], ALU.add).then_inc(sp_out, 1)

            with dve.Fori(0, PTILES) as i:
                tile_a(i)
            tile_a(PTILES, sample=True)
            for m in range(MT):
                if m:
                    dve.wait_ge(mkv_mm, 2 * m)
                else:
                    dve.wait_ge(vc_mm, TILES)
                xn(TILES + m, mem_norm_col, TILES)
                dve.wait_ge(mkT_mm, m + 1)
                v.tensor_copy(mkT[:, :, m * P:(m + 1) * P], ps[:, 7, :].rearrange("p (h n) -> p h n", h=MH))\
                    .then_inc(mkT_out, 1)

            dve.wait_ge(sp_out, TILES)
            with dve.Fori(0, CG) as i:
                dve.wait_ge(b_out, 3 * i + 3 * (FU + 1))
                v.tensor_tensor(feats[:, bass.ds(i + FU, 1), 0:TOKENS], feats[:, bass.ds(i + FU, 1), 0:TOKENS],
                                spT[:, bass.ds(i, 1), 0:TOKENS], ALU.mult).then_inc(chunk_out, 1)
            dve.wait_ge(knat_mm, 1)
            v.tensor_copy(knat[:, 0, :], ps[:, 0, 0:KVW])
            v.tensor_copy(knat[0:SAMPLE, 1, :], ps[0:SAMPLE, 1, 0:KVW]).then_inc(knat_out, 1)

            def tile_c(n, first=False):
                keys = slice(P, 2 * P) if first else slice(0, 2 * P)
                nk = P if first else 2 * P
                scores = ps[:, 0:4, :].rearrange("p b (g n) -> p (b g) n", g=2)[:, :, keys]
                dve.wait_ge(s_mm, n + 1)
                if not first:
                    dve.wait_ge(pT_mm, 2 * n)
                V.add(v.scalar_tensor_tensor(sc[:, :, keys], scores, SWA_SCALE, swa_bias[:, :, keys], ALU.mult, ALU.add), s_taken, n + 1)
                V.settle()
                V.add(v.tensor_reduce(row[:, 0, :], sc[:, :, keys], AX.X, ALU.max))
                V.settle()
                V.add(v.tensor_tensor(row[:, 0, :], row[:, 0, :], sinks, ALU.max))
                V.settle()
                V.add(v.tensor_scalar(row[:, 1, :], row[:, 0, :], -1.0, None, ALU.mult))
                V.add(v.tensor_tensor(row[:, 2, :], sinks, row[:, 0, :], ALU.subtract), m_ready)
                dve.wait_ge(ms_mm, n + 1)
                V.add(v.tensor_reduce(row[:, 7, 0:MH], ps[:, 1:3, :].rearrange("p b (g n) -> p (b g) n", g=2), AX.X, ALU.max))
                V.settle()
                V.add(v.tensor_scalar(row[:, 5, 0:MH], row[:, 7, 0:MH], -MEM_SCALE, None, ALU.mult), mm_ready)
                dve.wait_ge(e_ready, n + 1)
                V.add(v.tensor_tensor(row[:, 3, :], row[:, 3, :], row[:, 4, :], ALU.add))
                V.settle()
                V.add(v.reciprocal(row[:, 4, :], row[:, 3, :]))
                V.settle()
                V.add(v.tensor_tensor(sc[:, :, keys], sc[:, :, keys], wide(row[:, 4, :], HEADS, nk), ALU.mult), p_ready)
                dve.wait_ge(me_ready, n + 1)
                V.add(v.reciprocal(row[:, 7, 0:MH], row[:, 6, 0:MH]))
                V.settle()
                V.add(v.tensor_tensor(msc[:, :, :], msc[:, :, :], wide(row[:, 7, 0:MH], MH, MEM), ALU.mult), mp_ready)
                dve.wait_ge(pv_mm, n + 1)
                V.add(v.tensor_copy(feats[:, FQ:FQ + GQ, cols(n)], ps[:, 0, :].rearrange("p (g n) -> p g n", g=GQ)), swa_out)
                dve.wait_ge(mpv_mm, n + 1)
                V.add(v.tensor_copy(feats[:, FM:FM + MH, cols(n)], ps[:, 3, :].rearrange("p (h n) -> p h n", h=MH)), mem_out)

            tile_c(0, first=True)
            with V.loop(1, PTILES, 7) as i:
                tile_c(i)

            V.settle()
            dve.wait_ge(smp_pe, 2)
            V.add(v.scalar_tensor_tensor(smp_s[:, :, :], ps[:, 4, :].rearrange("p (k n) -> p k n", k=KV)[:, :, 0:P + SAMPLE],
                                         SWA_SCALE, smp_bias[:, :, :], ALU.mult, ALU.add))
            V.settle()
            V.add(v.tensor_reduce(row[:, 0, 0:KV], smp_s[:, :, :], AX.X, ALU.max))
            V.settle()
            V.add(v.tensor_tensor(row[:, 0, 0:KV], row[:, 0, 0:KV], smp_sinks, ALU.max))
            V.settle()
            V.add(v.tensor_scalar(row[:, 1, 0:KV], row[:, 0, 0:KV], -1.0, None, ALU.mult))
            V.add(v.tensor_tensor(row[:, 2, 0:KV], smp_sinks, row[:, 0, 0:KV], ALU.subtract), smp_dve)
            dve.wait_ge(smp_act, 2)
            V.add(v.tensor_tensor(row[:, 3, 0:KV], row[:, 3, 0:KV], row[:, 4, 0:KV], ALU.add))
            V.settle()
            V.add(v.reciprocal(row[:, 4, 0:KV], row[:, 3, 0:KV]))
            V.settle()
            V.add(v.tensor_tensor(smp_s[:, :, :], smp_s[:, :, :], wide(row[:, 4, 0:KV], KV, P + SAMPLE), ALU.mult), smp_dve)
            dve.wait_ge(smp_pe, 4)
            for g in range(GQ):
                V.add(v.tensor_copy(
                    feats[:, FQ + g, PROMPT:TOKENS].rearrange("p (b t) -> p b t", b=B),
                    ps[:, 0, 0:P].rearrange("p (b g t) -> p b g t", b=B, g=GQ)[:, :, g, :]),
                    smp_dve if g == GQ - 1 else None)
            dve.wait_ge(smp_pe, 5)
            V.add(v.tensor_reduce(row[:, 7, 0:1], ps[:, 1, 0:MEM], AX.X, ALU.max))
            V.settle()
            V.add(v.tensor_scalar(row[:, 5, 0:1], row[:, 7, 0:1], -MEM_SCALE, None, ALU.mult), smp_dve)
            dve.wait_ge(smp_act, 5)
            V.add(v.reciprocal(row[:, 7, 0:1], row[:, 6, 0:1]))
            V.settle()
            V.add(v.tensor_scalar(smp_m[:, :], smp_m[:, :], row[:, 7, 0:1], None, ALU.mult), smp_dve)
            dve.wait_ge(smp_kv_used, 2 * B)
            for h in range(MH):
                V.add(v.tensor_copy(
                    feats[:, FM + h, PROMPT:TOKENS].rearrange("p (b t) -> p b t", b=B),
                    ps[:, 3, 0:P].rearrange("p (b h t) -> p b h t", b=B, h=MH)[:, :, h, :]),
                    smp_dve if h == MH - 1 else None, 6)

            V.settle()
            V.add(v.memset(merged[:, TOKENS:PADDED], 0.0))
            V.settle()

            def unit(i, j, first=False):
                for th in range(3):
                    part = slice(th * THIRD, (th + 1) * THIRD)
                    dve.wait_ge(d_sig, 9 * i + (3 * j + th + 1))
                    if j == 0:
                        if th == 0 and not first:
                            dve.wait_ge(merged_out, 16 * i)
                        V.add(v.tensor_tensor(merged[:, part], ps[:, 3 + th, 0:THIRD], sig[:, part], ALU.mult), d_mul, 9 * i + (3 * j + th + 1))
                    else:
                        V.settle()
                        V.add(v.tensor_tensor(prod[:, part], ps[:, 3 + th, 0:THIRD], sig[:, part], ALU.mult), d_mul, 9 * i + (3 * j + th + 1))
                        V.settle()
                        V.add(v.tensor_tensor(merged[:, part], merged[:, part], prod[:, part], ALU.add),
                              merged_ready if j == NBR - 1 and th == 2 else None, i + 1)

            for j in range(NBR):
                unit(0, j, first=True)
            with V.loop(1, DC, 5) as i:
                for j in range(NBR):
                    unit(i, j)

            V.settle()
            dve.wait_ge(we_in, 16 * 5)

            def hold():
                V.settle()
                alone(dve)

            def inverse_root(R, scr):
                V.add(v.reciprocal(scr[0:R, 2:3], scr[0:R, 1:2]))
                V.add(v.tensor_scalar(scr[0:R, 3:4], scr[0:R, 0:1], EPS, None, ALU.add))
                V.settle()
                V.add(v.scalar_tensor_tensor(scr[0:R, 4:5], scr[0:R, 2:3], scr[0:R, 3:4], scr[0:R, 2:3], ALU.mult, ALU.mult))
                V.settle()
                V.add(v.tensor_scalar(scr[0:R, 5:6], scr[0:R, 4:5], -0.5, 1.5, ALU.mult, ALU.add))
                V.settle()
                V.add(v.tensor_tensor(scr[0:R, 6:7], scr[0:R, 2:3], scr[0:R, 5:6], ALU.mult))
                V.settle()

            def front_sum(f):
                dve.wait_ge(h_mm, f + 1)
                dve.wait_ge(h_in, 16 * f + 16)
                V.add(v.tensor_tensor(h_next[:, :], h_next[:, :], ps[:, 4:6, :].rearrange("p a n -> p (a n)"), ALU.add), h_sum, f + 1)

            def front_norm(f):
                dve.wait_ge(root, f + 1)
                inverse_root(P, norm)
                V.add(v.scalar_tensor_tensor(n2_next[:, :], h_next[:, :], norm[:, 6:7], norm2_g, ALU.mult, ALU.mult), n2_ready, f + 1)

            def keys_first(g):
                dve.wait_ge(key_mm, g + 1)
                hold()
                s4 = ps[:, 6, :].rearrange("p (k n) -> p k n", k=4)
                for k in range(4):
                    V.add(v.max(sv[:, k, 0:8], s4[:, k, :]))
                hold()
                for k in range(4):
                    V.add(v.max_index(si[:, k, 0:8], sv[:, k, 0:8], s4[:, k, :]))
                for k in range(4):
                    V.add(v.match_replace(rest[:, k, :], sv[:, k, 0:8], s4[:, k, :], LOWEST),
                          keys_taken if k == 3 else None, g + 1)

            def keys_second(g):
                hold()
                for k in range(4):
                    V.add(v.max(sv[:, k, 8:16], rest[:, k, :]))
                hold()
                for k in range(4):
                    V.add(v.max_index(si[:, k, 8:16], sv[:, k, 8:16], rest[:, k, :]))
                for h in range(2):
                    V.add(v.tensor_tensor(cand[:, h, :].rearrange("p (a b) -> p a b", a=K), wide(sv[:, 2 * h, :], K, K),
                                          sv[:, 2 * h + 1, :].unsqueeze(1).broadcast_to([P, K, K]), ALU.add))
                V.settle()
                V.add(v.tensor_copy(sif[:, :, :], si[:, :, :]))

            def pairs_best(g):
                hold()
                for h in range(2):
                    V.add(v.max(cv16[:, h, 0:8], cand[:, h, :]))
                hold()
                for h in range(2):
                    V.add(v.max_index(ci16[:, h, 0:8], cv16[:, h, 0:8], cand[:, h, :]))
                for h in range(2):
                    V.add(v.match_replace(cand2[:, h, :], cv16[:, h, 0:8], cand[:, h, :], LOWEST))
                hold()
                for h in range(2):
                    V.add(v.max(cv16[:, h, 8:16], cand2[:, h, :]))
                hold()
                for h in range(2):
                    V.add(v.max_index(ci16[:, h, 8:16], cv16[:, h, 8:16], cand2[:, h, :]))
                V.add(v.tensor_tensor(shifted[:, :, :], cv16[:, :, :], cv16[:, :, 0:1].broadcast_to([P, 2, K]), ALU.subtract), shifted_ready, g + 1)

            def experts(f, p):
                g = PAIRS * f + p
                flat = "p h k -> p (h k)"
                V.settle()
                V.add(v.tensor_scalar(hilo[:, 0], ci16[:, :, :], 4, None, ALU.logical_shift_right))
                V.add(v.tensor_scalar(hilo[:, 1], ci16[:, :, :], 15, None, ALU.bitwise_and))
                V.settle()
                V.add(v.tensor_copy(hilof[:, :, :, :], hilo[:, :, :, :]))
                for half in range(2):
                    V.settle()
                    V.add(v.tensor_tensor(match[:, :, :, :].rearrange("p h k a -> p (h k) a"),
                                          wide(hilof[:, half].rearrange(flat), 2 * K, K),
                                          iota16[:, :].unsqueeze(1).broadcast_to([P, 2 * K, K]), ALU.is_equal))
                    V.settle()
                    number = sif[:, half:4:2, :]
                    V.add(v.tensor_tensor(match[:, :, :, :], match[:, :, :, :],
                                          number.unsqueeze(2).broadcast_to([P, 2, K, K]), ALU.mult))
                    V.settle()
                    V.add(v.tensor_reduce(picked[:, half].rearrange(flat), match[:, :, :, :].rearrange("p h k a -> p (h k) a"),
                                          AX.X, ALU.add))
                V.settle()
                need(dve, staged, STAGES * (f - 1) + 1)
                V.add(v.scalar_tensor_tensor(i_next[:, bass.ds(2 * K * p, 2 * K)], picked[:, 0].rearrange(flat), float(NK),
                                             picked[:, 1].rearrange(flat), ALU.mult, ALU.add), chosen, g + 1)
                dve.wait_ge(raised_ready, g + 1)
                V.add(v.tensor_reduce(stat[:, 8:10], raised[:, :, :], AX.X, ALU.add))
                V.settle()
                V.add(v.reciprocal(stat[:, 10:12], stat[:, 8:10]))
                V.settle()
                V.add(v.tensor_tensor(g_next[:, bass.ds(2 * K * p, 2 * K)].rearrange("p (h k) -> p h k", h=2), raised[:, :, :],
                                      wide(stat[:, 10:12], 2, K), ALU.mult))

            def move_n2():
                V.settle()
                V.add(v.tensor_copy(n2_cur, n2_next))
                V.settle()

            def move_choice(n):
                V.settle()
                need(dve, staged, STAGES * n)
                V.add(v.tensor_copy(i_cur, i_next))
                V.add(v.tensor_copy(g_cur, g_next), moved, n + 1)

            def move_h(n):
                dve.wait_ge(moved, n + 1)
                V.add(v.tensor_copy(h_cur, h_next), h_moved, n + 1)

            def dot(batch, b, R, slots):
                for j in slots:
                    dve.wait_ge(u_in[b % 2][j], 8 * batch + 16 - 8 * (b % 2))
                    need(dve, dots, 4 * batch + (j - 1))
                    V.add(v.scalar_tensor_tensor(product[j % 2][0:R, :], u_ring[0:R, b % 2, j, :], 1.0, n2_cur[0:R, :],
                                                 ALU.mult, ALU.mult, accum_out=act4[0:R, b % 2, j:j + 1]), dots, 4 * batch + (j + 1))

            product = [u_dump, ps[:, 2:4, :].rearrange("p a n -> p (a n)")]

            def weigh(batch, at, b, R):
                dve.wait_ge(gelus, batch + 1)
                need(dve, diags, 4 * batch - 4)
                V.add(v.tensor_tensor(c4[0:R, b % 2, :], gelu4[0:R, b % 2, :], g_cur[0:R, bass.ds(at, NB)], ALU.mult), c_ready, batch + 1)

            def take_acc(n, R=P):
                dve.wait_ge(acc_mm, n + 1)
                dve.wait_ge(h_moved, n + 1)
                V.add(v.tensor_tensor(h_cur[0:R, :], h_cur[0:R, :], ps[0:R, 0:2, :].rearrange("p a n -> p (a n)"), ALU.add), acc_taken, n + 1)

            def final_norm(n, R=P):
                dve.wait_ge(y_root, n + 1)
                inverse_root(R, norm)
                need(dve, y_out, 16 * n)
                V.add(v.scalar_tensor_tensor(y[0:R, :], h_cur[0:R, :], norm[0:R, 6:7], final_g[0:R, :], ALU.mult, ALU.mult),
                      y_ready, n + 1)
                V.settle()

            def tile_e(n, f, R=P, follows=True):
                move_n2()
                for b in range(OPEN):
                    dot(BATCHES * n + b, b, R, (0, 1))
                    if b:
                        weigh(BATCHES * n + (b - 1), NB * (b - 1), b - 1, R)
                    else:
                        if follows:
                            weigh(BATCHES * n - 1, NB * (BATCHES - 1), BATCHES - 1, P)
                        move_choice(n)
                    if b == 1 and follows:
                        take_acc(n - 1)
                    dot(BATCHES * n + b, b, R, (2, 3))
                    if b == 2:
                        if follows:
                            final_norm(n - 1)
                        move_h(n)
                    if f is not None:
                        if b == 4:
                            front_sum(f)
                        elif b == 5:
                            front_norm(f)
                per = PAIR_STEPS if f is not None else 0
                with V.loop(0, PAIRS, per) as p:
                    for b in range(PER_PAIR):
                        dot(BATCHES * n + PER_PAIR * p + (OPEN + b), b, R, (0, 1))
                        weigh(BATCHES * n + PER_PAIR * p + (OPEN + b - 1), NB * PER_PAIR * p + NB * (OPEN + b - 1), (b - 1) % 2, R)
                        dot(BATCHES * n + PER_PAIR * p + (OPEN + b), b, R, (2, 3))
                        if f is not None:
                            if b == 2:
                                keys_first(PAIRS * f + p)
                            elif b == 3:
                                keys_second(PAIRS * f + p)
                            elif b == 4:
                                pairs_best(PAIRS * f + p)
                            elif b == 5:
                                experts(f, p)

            def first_keys(p):
                keys_first(p)
                keys_second(p)
                pairs_best(p)
                experts(0, p)

            PAIR_STEPS = 11 + 11 + 10 + 12
            front_sum(0)
            front_norm(0)
            first_keys(0)
            with V.loop(1, PAIRS, PAIR_STEPS) as p:
                first_keys(p)
            tile_e(0, 1, follows=False)
            tile_steps = 2 + 5 + 5 + PAIRS * PAIR_STEPS
            with V.loop(1, PTILES, tile_steps) as i:
                tile_e(i, i + 1)
            tile_e(PTILES, None, R=SAMPLE)
            weigh(BATCHES * TILES - 1, NB * (BATCHES - 1), BATCHES - 1, SAMPLE)
            take_acc(PTILES, SAMPLE)
            final_norm(PTILES, SAMPLE)

        @block.gpsimd
        def _(pool):
            G = Steps(pool, pool_)
            g = nc.gpsimd

            pool.wait_ge(consts_in, 16 * len(LOADS))
            G.add(g.memset(stat[:, 3:4], -0.5))
            g.affine_select(out=ws_T[:, :, :], in_=ws_T[:, :, :], compare_op=ALU.is_ge, fill=0.0, base=0,
                            pattern=[[0, CG], [1, P]], channel_multiplier=-1).then_inc(made, 1)
            small = ws_T_smp[0:SAMPLE, :, :]
            g.affine_select(out=small, in_=small, compare_op=ALU.is_ge, fill=0.0, base=0,
                            pattern=[[0, CG], [1, SAMPLE]], channel_multiplier=-1).then_inc(made, 1)
            G.settle()

            def inverse_root(signal, taken, n, at, scale):
                pool.wait_ge(signal, n + 1)
                pool.wait_ge(taken, n)
                alone(pool)
                G.add(g.tensor_scalar(stat[:, at + 1:at + 2], stat[:, at:at + 1], scale, EPS, ALU.mult, ALU.add))
                G.settle()

            def rstd_x(n):
                inverse_root(mean_sq, scaled, n, 0, 1.0)
                g.tensor_tensor(stat[:, 2:3], stat[:, 1:2], stat[:, 3:4], ALU.pow).then_inc(rstd, 1)

            def tile_a(n):
                rstd_x(n)
                pool.wait_ge(xn_ready, n + 1)
                g.tensor_copy(xnT[:, :, cols(n)], xn_tile[:, :, :]).then_inc(xn_kept, 1)
                inverse_root(vc_sq, vc_ready, n, 4, 1.0 / CW)
                g.tensor_tensor(stat[:, 6:7], stat[:, 5:6], stat[:, 3:4], ALU.pow).then_inc(vc_rstd, 1)

            with G.loop(0, TILES, 2) as i:
                tile_a(i)
            for m in range(MT):
                rstd_x(TILES + m)

            pool.wait_ge(b_out, 3 * FU)
            pool.wait_ge(v_out, TILES)
            pool.wait_ge(xn_ready, TILES + MT)
            pool.wait_ge(mkT_mm, MT)
            pool.wait_ge(stored, 16 * (3 + 2 * MT))
            g.tensor_copy(qs[:, :, :], feats[:, 0:FK, 0:P]).then_inc(c_in, 1)
            g.tensor_copy(ks[:, P:2 * P], feats[:, FK, 0:P]).then_inc(c_in, 1)
            g.tensor_copy(vs[:, 1, :], v_nat[:, 0, :]).then_inc(c_in, 1)
            with pool.Fori(1, PTILES) as i:
                pool.wait_ge(ms_mm, i)
                g.tensor_copy(qs[:, :, :], feats[:, 0:FK, cols(i)]).then_inc(c_in, 1)
                g.tensor_copy(ks.unsqueeze(1), feats[:, FK:FK + 1, bass.ds(i * P - P, 2 * P)]).then_inc(c_in, 1)
                pool.wait_ge(pv_mm, i)
                g.tensor_copy(vs[:, :, :], v_nat[:, bass.ds(i - 1, 2), :]).then_inc(c_in, 1)

            def rows(ring, table, index, R, s):
                g.indirect_dma_start(ring[0:R, :], None, t[table], bass.IndirectOffsetOnAxis(index[0:R, :], 0)).then_inc(s, 16)

            def gather_u(batch, b, h, index, R):
                need(pool, dots, 4 * batch + (2 * h - 6))
                alone(pool)
                for j in (2 * h, 2 * h + 1):
                    rows(u_ring[:, b % 2, j, :], "peer_u", index[:, j:j + 1], R, u_in[b % 2][j])

            def gather_v(batch, h, index, R):
                need(pool, v_used, 4 * batch + (2 * h - 2))
                alone(pool)
                for j in (2 * h, 2 * h + 1):
                    rows(v_ring[:, j, :], "peer_v", index[:, j:j + 1], R, v_in[j])

            half = PER_PAIR // 2 * NB
            final = stage_pair[:, 1, half - NB:half]

            def tile_e(n, R=P, follows=True):
                pool.wait_ge(chosen, PAIRS * n + 1)
                alone(pool)
                g.tensor_copy(stage_open, i_next[:, 0:OPEN * NB]).then_inc(staged, 1)
                pool.wait_ge(staged, STAGES * n + 1)
                for b in range(OPEN):
                    for h in range(2):
                        gather_u(BATCHES * n + b, b, h, stage_open[:, NB * b:NB * b + NB], R)
                        if b:
                            gather_v(BATCHES * n + (b - 1), h, stage_open[:, NB * (b - 1):NB * b], R)
                        elif follows:
                            gather_v(BATCHES * n - 1, h, final, P)
                pool.wait_ge(moved, n + 1)
                alone(pool)
                g.tensor_copy(final, stage_open[:, NB * (OPEN - 1):NB * OPEN]).then_inc(staged, 1)
                pool.wait_ge(staged, STAGES * n + 2)
                alone(pool)
                with pool.Fori(0, PAIRS) as p:
                    for b in range(PER_PAIR):
                        s, k = divmod(b, PER_PAIR // 2)
                        before, kb = divmod((b - 1) % PER_PAIR, PER_PAIR // 2)
                        batch = BATCHES * n + PER_PAIR * p + (OPEN + b)
                        if k == 0:
                            g.tensor_copy(stage_pair[:, s, :], i_cur[:, bass.ds(PER_PAIR * NB * p + OPEN * NB + half * s, half)])\
                                .then_inc(staged, 1)
                            pool.wait_ge(staged, STAGES * n + 2 * p + (3 + s))
                        for h in range(2):
                            gather_u(batch, b, h, stage_pair[:, s, NB * k:NB * k + NB], R)
                            gather_v(batch - 1, h, stage_pair[:, before, NB * kb:NB * kb + NB], R)

            tile_e(0, follows=False)
            with pool.Fori(1, PTILES) as i:
                tile_e(i)
            tile_e(PTILES, R=SAMPLE)
            for h in range(2):
                gather_v(BATCHES * TILES - 1, h, final, SAMPLE)


def _position_constants():
    slopes = np.exp2(-8.0 * np.arange(1, HEADS + 1, dtype=np.float32) / HEADS).astype(np.float32)
    r, c = np.arange(WINDOW)[:, None], np.arange(2 * WINDOW)[None, :]
    dist = WINDOW + r - c
    valid = (dist >= 0) & (dist <= WINDOW)
    prompt = np.where(valid[:, None, :], -slopes[None, :, None] * dist[:, None, :].astype(np.float32), np.float32(NEG))
    b, g, t = (x.ravel()[:, None] for x in np.meshgrid(np.arange(B), np.arange(GQ), np.arange(T), indexing="ij"))
    sb, st = (x.ravel()[None, :] for x in np.meshgrid(np.arange(B), np.arange(T), indexing="ij"))
    dist = np.concatenate([WINDOW + t - np.arange(WINDOW)[None, :], t - st], 1)
    valid = (dist >= 0) & (dist <= WINDOW) & np.concatenate([np.ones((P, WINDOW), bool), sb == b], 1)
    sample = np.stack([np.where(valid, -slopes[kv * GQ + g] * dist.astype(np.float32), np.float32(NEG))
                       for kv in range(KV)], 1)
    return prompt.astype(np.float32), sample.astype(np.float32)


def kernel(x_prompt, x_sample, cache_swa_k, cache_swa_v, cache_mem_k, cache_mem_v, mem_prompt,
           norm1_g, w_in, b_gate, swa_sinks, chunk_norm_g, chunk_ws, chunk_bs, mem_norm_g, w_mem_kv,
           w_branch_out, w_out, norm2_g, peer_wq, peer_subkeys, peer_u, peer_v, final_norm_g):
    import concourse.bacc as bacc
    from concourse.bass_utils import run_bass_kernel_spmd

    A = np.asarray
    f32 = np.float32

    def on_all(v):
        v = A(v).reshape(1, -1)
        return np.ascontiguousarray(np.broadcast_to(v, (P, v.shape[1])))

    def chunked(w):
        w = A(w)
        return np.ascontiguousarray(w.reshape(-1, P, w.shape[1]).transpose(1, 0, 2))

    def blocks(w):
        w = A(w)
        return w.reshape(-1, P, w.shape[1] // P, P).transpose(2, 1, 0, 3)

    qw = HEADS * HD
    o = np.cumsum([0, qw, KVW, KVW, CW, CW, MW, NBR * D])
    w = A(w_in)[0]
    w_q, w_k, w_v, w_u, w_vc, w_mq, w_g = (w[:, o[n]:o[n + 1]] for n in range(7))
    w_q = w_q.reshape(D, KV, GQ, HD).transpose(0, 2, 1, 3).reshape(D, qw)
    w_b = np.concatenate([blocks(x) for x in (w_q, w_mq, w_k, w_u)], 0)
    br = A(w_branch_out)[0]
    br = np.stack([br[0].reshape(KV, GQ, HD, D).transpose(1, 0, 2, 3).reshape(qw, D), br[1], br[2]], 0)
    gates = np.stack([blocks(w_g[:, j * D:(j + 1) * D]) for j in range(NBR)], 1)
    outs = np.stack([blocks(br[j]) for j in range(NBR)], 1)
    w_d = np.concatenate([gates, outs], 3).reshape(DC * NBR, P, DC + BC, P)
    ws = A(chunk_ws)[0]
    ws_smp = np.zeros((SAMPLE, CG, SAMPLE), f32)
    for b in range(B):
        ws_smp[b * T:(b + 1) * T, :, b * T:(b + 1) * T] = ws[:, :T, :T].transpose(2, 0, 1)
    bs = A(chunk_bs)[0]
    xp = np.zeros((PADDED, D), f32)
    xp[:PROMPT] = A(x_prompt)[0]
    xp[PROMPT:TOKENS] = A(x_sample).reshape(SAMPLE, D)
    sinks = A(swa_sinks)[0]
    kc, vc = A(cache_swa_k)[0].reshape(B, WINDOW, KVW), A(cache_swa_v)[0].reshape(B, WINDOW, KVW)
    mk, mv = A(cache_mem_k)[0], A(cache_mem_v)[0].reshape(B, MT, P, MW)
    prompt_bias, sample_bias = _position_constants()
    arrays = dict(
        x=xp, mem=A(mem_prompt)[0], ident=np.eye(P, dtype=f32), iota16=on_all(np.arange(K, dtype=f32)),
        norm1_col=A(norm1_g)[0].reshape(DC, P).T, mem_norm_col=A(mem_norm_g)[0].reshape(DC, P).T,
        w_vvc=chunked(np.concatenate([w_v, w_vc], 1)), w_mem=chunked(A(w_mem_kv)[0]),
        swa_bias=prompt_bias, smp_bias=sample_bias, chunk_g=on_all(chunk_norm_g),
        chunk_b=on_all(bs).reshape(P, CG, P), chunk_b_smp=on_all(np.tile(bs[:, None, :T], (1, B, 1))).reshape(P, CG, SAMPLE),
        ws_T=ws.transpose(2, 0, 1), ws_T_smp=ws_smp,
        gate_b=A(b_gate)[0].reshape(NBR, DC, P).transpose(2, 1, 0).reshape(P, DC * NBR),
        sinks=on_all(sinks),
        smp_sinks=np.tile(np.repeat(sinks.reshape(KV, GQ), T, axis=1), (1, B)).T,
        k_cache_T=kc.transpose(2, 0, 1), v_cache=vc.transpose(1, 0, 2), k_cache_rows=kc, v_cache_rows=vc,
        mk_cache_T=mk.transpose(0, 3, 2, 1).reshape(B, P, MH * MEM),
        mv_cache=mv.transpose(0, 2, 1, 3).reshape(B, P, MT * MW),
        w_b=w_b, w_d=w_d, w_out=chunked(A(w_out)[0]), w_q=chunked(A(peer_wq)[0]),
        subT=A(peer_subkeys)[0].transpose(2, 0, 1), norm2_g=on_all(norm2_g), final_g=on_all(final_norm_g),
        peer_u=A(peer_u)[0], peer_v=A(peer_v)[0],
    )
    outputs = dict(
        y=(TOKENS, D), k_prompt=(WINDOW, KVW), v_prompt=(WINDOW, KVW), mk_out=(MEM, MW), mv_out=(MEM, MW),
        k_sample_old=(B, WINDOW - T, KVW), v_sample_old=(B, WINDOW - T, KVW),
        k_sample_new=(SAMPLE, KVW), v_sample_new=(SAMPLE, KVW), vc_out=(SAMPLE, CW),
    )
    nc = bacc.Bacc("TRN2", target_bir_lowering=False, num_devices=1)
    tensors = {}
    for name, a in arrays.items():
        arrays[name] = np.ascontiguousarray(a)
        assert a.dtype == f32, name
        tensors[name] = nc.dram_tensor(name, a.shape, F32, kind="ExternalInput").ap()
    for name, shape in outputs.items():
        tensors[name] = nc.dram_tensor(name, shape, F32, kind="ExternalOutput").ap()
    tensors["m_scratch"] = nc.dram_tensor("m_scratch", (DC, P, PADDED), F32, kind="Internal").ap()
    build(nc, tensors)
    r = run_bass_kernel_spmd(nc, [arrays], core_ids=[0]).results[0]

    def rolled(name):
        new = r[f"{name}_sample_new"].reshape(B, T, KVW)
        return np.concatenate([r[f"{name}_sample_old"], new], 1).reshape(1, B, WINDOW, KV, HD)

    return (r["y"][:PROMPT].reshape(1, PROMPT, D), r["y"][PROMPT:].reshape(B, T, D),
            r["k_prompt"].reshape(1, 1, WINDOW, KV, HD), r["v_prompt"].reshape(1, 1, WINDOW, KV, HD),
            r["mk_out"].reshape(1, 1, MEM, MH, P), r["mv_out"].reshape(1, 1, MEM, MH, P),
            rolled("k"), rolled("v"), r["vc_out"].reshape(1, B, T, CG, P))
```

```python
from contextlib import ExitStack, contextmanager

import numpy as np

import concourse.bass as bass
from concourse import mybir

F32, U32, BF16 = mybir.dt.float32, mybir.dt.uint32, mybir.dt.bfloat16
ALU = mybir.AluOpType
ACT = mybir.ActivationFunctionType
AX = mybir.AxisListType

P = 128
D = 1024
DC = D // P
PROMPT = 1024
B, T = 8, 4
SAMPLE = B * T
TOKENS = PROMPT + SAMPLE
PTILES = PROMPT // P
TILES = PTILES + 1
PADDED = TILES * P
THIRD = TOKENS // 3
HD = 64
KV = 2
GQ = 4
HEADS = KV * GQ
KVW = KV * HD
WINDOW = 128
SWA_SCALE = HD ** -0.5
CG = 4
CW = CG * P
MEM = 256
MT = MEM // P
MH = 4
MW = MH * P
MEM_SCALE = P ** -0.5
NBR = 3
BC = 4
EPS = 1e-6
NEG = -1e30
PH = 8
K = 16
NK = 128
EXPERTS = NK * NK
PAIRS = PH // 2
SLOTS = PH * K
NB = 4
OPEN = 8
PER_PAIR = (SLOTS // NB - OPEN) // PAIRS
BATCHES = SLOTS // NB
GROUPS = P // SAMPLE
assert GROUPS * SAMPLE == SLOTS and GROUPS == PAIRS and OPEN * NB == SAMPLE
PACKED = 16 * (GROUPS - 1 + 2 * GROUPS)
LAST = BATCHES * PTILES + OPEN - 1
STAGES = 2 + 2 * PAIRS
RESERVED = 6
ARENA = 52400
LOWEST = -3.0e38

FQ, FM, FK, FU = 0, GQ, GQ + MH, GQ + MH + 1
FEATS = FU + CG


class Steps:

    def __init__(self, eng, sem):
        self.eng, self.sem, self.base, self.n = eng, sem, 0, 0
        self.last = None

    def add(self, ins, signal=None, after=None):
        if signal is not None:
            self.last = (signal, after)
            return ins.then_inc(signal, 1)
        self.last = None
        self.n += 1
        return ins.then_inc(self.sem, 1)

    def settle(self):
        if self.last:
            assert self.last[1] is not None
            self.eng.wait_ge(*self.last)
        elif not isinstance(self.base, int) or self.base + self.n:
            self.eng.wait_ge(self.sem, self.base + self.n)

    @contextmanager
    def loop(self, first, end, per):
        with self.eng.Fori(first, end) as i:
            start, outer = self.n, self.base
            self.base, self.last = outer + i * per - first * per, None
            yield i
            assert self.n - start == per, (self.n - start, per)
            self.base, self.last = outer, None
        self.n = start + (end - first) * per


def build(nc, t):
    ctx = ExitStack()
    with ctx:
        def sem(name):
            return ctx.enter_context(nc.semaphore(name))

        ps = ctx.enter_context(nc.psum_tensor("ps", [P, 8, 512], F32))

        def keep(name, shape, dt=F32):
            return ctx.enter_context(nc.sbuf_tensor(f"{name}_sb", [P, *shape], dt))

        ident = keep("ident", [P])
        idents = keep("idents", [SAMPLE])
        nothing = keep("nothing", [512], BF16)
        norm1_col, mem_norm_col = keep("norm1_col", [DC]), keep("mem_norm_col", [DC])
        eps = keep("eps", [1])
        stat = keep("stat", [16])
        iota16 = keep("iota16", [K])
        arena = keep("arena", [ARENA])

        class Region:

            def __init__(self, at=0):
                self.at = at

            def take(self, *shape, dt=F32):
                n = int(np.prod(shape)) // (2 if dt == BF16 else 1)
                a = arena[:, self.at:self.at + n]
                self.at += n
                assert self.at <= ARENA, self.at
                if dt != F32:
                    a = a.bitcast(dt)
                names = "abcd"[:len(shape)]
                if len(shape) > 1:
                    kw = {names[k]: shape[k] for k in range(1, len(shape))}
                    a = a.rearrange(f"p ({' '.join(names)}) -> p {' '.join(names)}", **kw)
                return a

        r = Region()
        xnT = r.take(DC, PADDED)
        feats_at = r.at
        feats = r.take(FEATS, PADDED)
        spT_at = r.at
        spT = r.take(CG, PADDED)
        v_nat = r.take(TILES, KVW)
        mkT_at = r.at
        mkT = r.take(MH, MEM)
        mv = r.take(MT, MW)
        w_ring_at = r.at
        w_ring = r.take(NBR, DC + BC, P)
        w_ring_end = r.at
        swa_bias_at = r.at
        swa_bias = r.take(HEADS, 2 * P)
        smp_bias = r.take(KV, P + SAMPLE)
        chunk_g = r.take(CW)
        chunk_b = r.take(CG, P)
        chunk_b_smp = r.take(CG, SAMPLE)
        ws_T = r.take(CG, P)
        ws_T_smp = r.take(CG, SAMPLE)
        gate_b = r.take(DC * NBR)
        sinks = r.take(HEADS)
        smp_sinks = r.take(KV)
        knat = r.take(2, KVW)
        row = r.take(8, HEADS)
        temps_at = r.at
        a = Region(feats_at)
        w_vvc = a.take(DC, KVW + CW)
        w_mem = a.take(DC, 2 * MW)
        assert a.at <= feats_at + FEATS * PADDED
        a = Region(temps_at)
        x_t = a.take(D)
        xs = a.take(D)
        squares = a.take(D)
        xn_tile = a.take(DC, P)
        vc_gelu = a.take(CW)
        vc_n = a.take(CW)
        vc_squares = a.take(CW)
        mk_nat = a.take(MT, MW)
        c = Region(temps_at)
        qs = c.take(FK, P)
        ks = c.take(2 * P)
        vs = c.take(2, KVW)
        sc = c.take(2, HEADS, 2 * P)
        scT = c.take(KV, 2, GQ, P)
        msc = c.take(2, MH, MEM)
        mscT = c.take(MH, MT, P)
        s = Region(w_ring_at)
        kcT = s.take(B, P)
        cv = s.take(B, KVW)
        cache_ring = [s.take(MH * MEM) for _ in range(2)]
        assert s.at <= w_ring_end
        s = Region(temps_at)
        cache_ring += [s.take(MH * MEM) for _ in range(2 * B - RESERVED - 2)]
        smp_sT = s.take(KV, P)
        smp_snT = s.take(KV, P)
        smp_s = s.take(KV, P + SAMPLE)
        smp_pT = s.take(KV, P)
        smp_pnT = s.take(KV, P)
        smp_m = s.take(MEM)
        q_step, p_step = P + T, P + MH * T
        q_apart = Region(spT_at).take(B * MH * q_step)
        p_apart = [Region(mkT_at).take(B * p_step)]
        assert mkT_at + B * p_step <= w_ring_at
        s = Region(swa_bias_at)
        p_apart.append(s.take(B * p_step))
        smp_o = s.take(MW)
        assert s.at <= swa_bias_at + HEADS * 2 * P
        d = Region(spT_at)
        sig = d.take(TOKENS)
        prod = d.take(TOKENS)
        merged = d.take(PADDED)
        assert d.at <= w_ring_at
        e = Region(temps_at)
        w_out = e.take(DC, D)
        subT = e.take(2, NK)
        norm2_g, final_g = e.take(D), e.take(D)
        g_next, g_cur = e.take(SLOTS), e.take(SLOTS)
        i_next, i_cur = e.take(SLOTS, dt=U32), e.take(SLOTS, dt=U32)
        e = Region()
        w_q = e.take(DC, PH * 2 * P)
        u_ring = e.take(2, NB, D)
        v_ring = e.take(NB, D)
        m_tile = e.take(DC, P)
        h_next, h_cur = e.take(D), e.take(D)
        n2_next, n2_cur = e.take(D), e.take(D)
        n2T = e.take(DC, P)
        dump, u_dump = e.take(D, dt=BF16), e.take(D)
        y = e.take(D)
        q_nat = e.take(4 * P)
        qT = e.take(4, P)
        rest = e.take(4, NK)
        sv = e.take(4, K)
        si = e.take(4, K, dt=U32)
        sif = e.take(4, K)
        cand = e.take(2, K * K)
        cand2 = rest.rearrange("p (h k) n -> p h (k n)", h=2)
        cv16 = e.take(2, K)
        ci16 = e.take(2, K, dt=U32)
        hilo = e.take(2, 2, K, dt=U32)
        hilof = e.take(2, 2, K)
        match = cand.rearrange("p h (k a) -> p h k a", k=K)
        picked = e.take(2, 2, K)
        shifted = e.take(2, K)
        raised = e.take(2, K)
        i_packed, g_packed = e.take(SAMPLE, dt=U32), e.take(SAMPLE)
        stage_open = e.take(OPEN * NB, dt=U32)
        stage_pair = e.take(2, PER_PAIR // 2 * NB, dt=U32)
        act4, gelu4, c4 = e.take(2, NB), e.take(2, NB), e.take(2, NB)
        diag = e.take(2, NB, P)
        norm = e.take(8)
        assert e.at <= temps_at, e.at

        act_, dve_, pool_ = sem("act_steps"), sem("dve_steps"), sem("pool_steps")
        passed = sem("waits_passed")
        chunk_in, consts_in, cols_in = sem("chunk_in"), sem("consts_in"), sem("cols_in")
        made = sem("made")
        x_in, mean_sq, rstd, scaled, xT_mm, xn_ready, xn_kept = (sem(n) for n in (
            "x_in", "mean_sq", "rstd", "scaled", "xT_mm", "xn_ready", "xn_kept"))
        v_mm, vc_mm, v_out, vc_out, vc_sq, vc_rstd, vc_ready, sp_mm, sp_out = (sem(n) for n in (
            "v_mm", "vc_mm", "v_out", "vc_out", "vc_sq", "vc_rstd", "vc_ready", "sp_mm", "sp_out"))
        w_a_in, w_mem_in, mkv_mm, mkv_out, mkT_mm, mkT_out = (sem(n) for n in (
            "w_a_in", "w_mem_in", "mkv_mm", "mkv_out", "mkT_mm", "mkT_out"))
        wb_in = [sem(f"wb_in{n}") for n in range(2)]
        b_mm, b_out, chunk_out, knat_mm, knat_out = (sem(n) for n in (
            "b_mm", "b_out", "chunk_out", "knat_mm", "knat_out"))
        c_in, cv_in = sem("c_in"), sem("cv_in")
        s_mm, s_taken, m_ready, e_ready, p_ready, pT_mm, pT_out, pv_mm, swa_out = (sem(n) for n in (
            "s_mm", "s_taken", "m_ready", "e_ready", "p_ready", "pT_mm", "pT_out", "pv_mm", "swa_out"))
        ms_mm, mm_ready, me_ready, mp_ready, mpT_mm, mpT_out, mpv_mm, mem_out = (sem(n) for n in (
            "ms_mm", "mm_ready", "me_ready", "mp_ready", "mpT_mm", "mpT_out", "mpv_mm", "mem_out"))
        smp_in, smp_pe, smp_act, smp_dve = sem("smp_in"), sem("smp_pe"), sem("smp_act"), sem("smp_dve")
        smp_kv_in = [sem(f"smp_kv_in{n}") for n in range(len(cache_ring))]
        smp_kv_used, apart = sem("smp_kv_used"), sem("apart")
        wd_in = [sem(f"wd_in{n}") for n in range(NBR)]
        d_mm, d_sig, d_mul, merged_ready, merged_out = (sem(n) for n in (
            "d_mm", "d_sig", "d_mul", "merged_ready", "merged_out"))
        w_out_in = sem("w_out_in")
        w_q_in = [sem(f"w_q_in{p}") for p in range(PAIRS)]
        h0_mm = sem("h0_mm")
        m_in, h_in, h_mm, h_sum, root, n2_ready, n2T_mm, n2T_out = (sem(n) for n in (
            "m_in", "h_in", "h_mm", "h_sum", "root", "n2_ready", "n2T_mm", "n2T_out"))
        q_mm, q_out, qT_mm, qT_out, key_mm, keys_taken, shifted_ready, raised_ready = (sem(n) for n in (
            "q_mm", "q_out", "qT_mm", "qT_out", "key_mm", "keys_taken", "shifted_ready", "raised_ready"))
        packed = sem("packed")
        chosen, moved, h_moved, staged, dots, gelus, c_ready, diags, v_used = (sem(n) for n in (
            "chosen", "moved", "h_moved", "staged", "dots", "gelus", "c_ready", "diags", "v_used"))
        u_in = [[sem(f"u_in{n}{j}") for j in range(NB)] for n in range(2)]
        v_in = [sem(f"v_in{j}") for j in range(NB)]
        acc_mm, acc_taken, y_root, y_ready, y_out = (sem(n) for n in (
            "acc_mm", "acc_taken", "y_root", "y_ready", "y_out"))
        stored, stored_k = sem("stored"), sem("stored_k")

        def cols(n):
            return bass.ds(n * P, P)

        def alone(eng):
            eng.sem_inc(passed, 1)

        def need(eng, sem, value):
            if not isinstance(value, int) or value > 0:
                eng.wait_ge(sem, value)

        def wide(a, *shape):
            return a.unsqueeze(a.ndim).broadcast_to([a.shape[0], *shape])

        FIRST_LOADS = ["chunk_g", "chunk_b", "chunk_b_smp", "ws_T", "ws_T_smp"]
        LOADS = ["swa_bias", "smp_bias", "gate_b", "sinks", "smp_sinks"]
        where = dict(swa_bias=swa_bias, smp_bias=smp_bias, chunk_g=chunk_g, chunk_b=chunk_b,
                     ws_T=ws_T, gate_b=gate_b, sinks=sinks, smp_sinks=smp_sinks,
                     chunk_b_smp=chunk_b_smp, ws_T_smp=ws_T_smp[0:SAMPLE])
        def cache_slot(n):
            return n if n < len(cache_ring) else n - len(cache_ring) + 2

        block = ctx.enter_context(nc.Block())

        @block.sync
        def _(sp):
            def send(out, in_, s):
                return sp.dma_start(out, in_).then_inc(s, 16)

            def load_b(n, slot):
                send(w_ring[:, slot, 0:DC, :], t["w_b"][bass.ds(n, 1)].rearrange("a p c m -> p (a c) m"), wb_in[slot])

            send(x_t[:, :], t["x"][0:P, :], x_in)
            send(ident[:, :], t["ident"], cols_in)
            send(idents[:, :], t["idents"], cols_in)
            send(norm1_col[:, :], t["norm1_col"], cols_in)
            send(mem_norm_col[:, :], t["mem_norm_col"], cols_in)
            send(iota16[:, :], t["iota16"], cols_in)
            send(w_vvc[:, :, :], t["w_vvc"], w_a_in)
            for name in FIRST_LOADS:
                send(where[name], t[name], chunk_in)
            def load_x(n):
                sp.wait_ge(mean_sq, n)
                sp.wait_ge(scaled, n)
                send(x_t[:, :], t["x"][cols(n), :], x_in)

            load_x(1)
            load_x(2)
            send(w_mem[:, :, :], t["w_mem"], w_mem_in)
            for n in range(2):
                load_b(n, n)
            with sp.Fori(3, TILES) as i:
                load_x(i)
            for m in range(MT):
                sp.wait_ge(mean_sq, TILES + m)
                sp.wait_ge(scaled, TILES + m)
                send(x_t[:, :], t["mem"][m * P:(m + 1) * P, :], x_in)
            for name in LOADS:
                send(where[name], t[name], consts_in)
            sp.wait_ge(vc_ready, TILES)
            send(t["vc_out"], vc_n[0:SAMPLE, :], stored)
            sp.wait_ge(v_out, TILES)
            send(t["v_prompt"], v_nat[:, PTILES - 1, :], stored)
            send(t["v_sample_new"], v_nat[0:SAMPLE, PTILES, :], stored)
            for m in range(MT):
                sp.wait_ge(mkv_out, 2 * m + 2)
                send(t["mk_out"][m * P:(m + 1) * P, :], mk_nat[:, m, :], stored)
                send(t["mv_out"][m * P:(m + 1) * P, :], mv[:, m, :], stored)
            for name in ("k", "v"):
                send(t[f"{name}_sample_old"], t[f"{name}_cache_rows"][:, T:WINDOW, :], stored_k)

            with sp.Fori(1, 4) as i:
                for slot in range(2):
                    sp.wait_ge(b_mm, 6 * i + 3 * slot - 3)
                    load_b(2 * i + slot, slot)
            sp.wait_ge(b_mm, 3 * (FK - 1))
            load_b(FK, 0)
            with sp.Fori(0, 2) as i:
                for k in range(2):
                    sp.wait_ge(b_mm, 6 * i + 3 * (FU - 1 + k))
                    load_b(2 * i + FU + k, (FU + k) % 2)
            sp.wait_ge(knat_out, 1)
            send(t["k_prompt"], knat[:, 0, :], stored_k)
            send(t["k_sample_new"], knat[0:SAMPLE, 1, :], stored_k)

            def load_cache(n):
                src = t["mk_cache_T"] if n < B else t["mv_cache"]
                send(cache_ring[cache_slot(n)], src[n % B], smp_kv_in[cache_slot(n)])

            sp.wait_ge(b_mm, 3 * FEATS)
            send(kcT[:, :, :], t["k_cache_T"], smp_in)
            send(cv[:, :, :], t["v_cache"], smp_in)
            load_cache(0)
            load_cache(1)
            sp.wait_ge(mem_out, PTILES)
            sp.wait_ge(swa_out, PTILES)
            sp.wait_ge(mpv_mm, PTILES)
            for n in range(2, len(cache_ring)):
                load_cache(n)
            for n in range(len(cache_ring), 2 * B):
                sp.wait_ge(smp_kv_used, n - len(cache_ring) + 3)
                load_cache(n)

            def load_d(i, j):
                send(w_ring[:, j, :, :], t["w_d"][bass.ds(3 * i + j, 1)].rearrange("a p c m -> p (a c) m"), wd_in[j])

            sp.wait_ge(smp_pe, 4)
            for j in range(NBR):
                load_d(0, j)
            sp.wait_ge(smp_kv_used, 2 * B)
            for name, a in dict(w_out=w_out, subT=subT, norm2_g=norm2_g, final_g=final_g).items():
                send(a, t[name], w_out_in)
            with sp.Fori(1, DC) as i:
                for j in range(NBR):
                    sp.wait_ge(d_mm, 9 * i + (3 * j - 6))
                    load_d(i, j)
                sp.wait_ge(merged_ready, i)
                send(t["m_scratch"][bass.ds(i - 1, 1)].rearrange("a p n -> (a p) n"), merged[:, :], merged_out)
            sp.wait_ge(merged_ready, DC)
            send(t["m_scratch"][DC - 1], merged[:, :], merged_out)

            sp.wait_ge(d_mm, 3 * NBR * DC)
            sp.wait_ge(merged_out, 16 * DC)
            sp.wait_ge(stored, 16 * (3 + 2 * MT))
            sp.wait_ge(stored_k, 16 * 4)

            def load_m(f):
                send(m_tile[:, :, :], t["m_scratch"][:, :, cols(f)].rearrange("c p n -> p c n"), m_in)

            def load_h(f):
                send(h_next[:, :], t["x"][cols(f), :], h_in)

            load_h(0)
            for p in range(PAIRS):
                part = slice(4 * P * p, 4 * P * (p + 1))
                send(w_q[:, :, part], t["w_q"][:, :, part], w_q_in[p])
            load_m(1)
            sp.wait_ge(h_moved, 1)
            load_h(1)
            sp.wait_ge(h_mm, 2)
            load_m(2)
            with sp.Fori(1, PTILES - 1) as i:
                sp.wait_ge(y_ready, i)
                send(t["y"][cols(i - 1), :], y[:, :], y_out)
                sp.wait_ge(h_moved, i + 1)
                load_h(i + 1)
                sp.wait_ge(h_mm, i + 2)
                load_m(i + 2)
            sp.wait_ge(y_ready, PTILES - 1)
            send(t["y"][cols(PTILES - 2), :], y[:, :], y_out)
            sp.wait_ge(h_moved, PTILES)
            load_h(PTILES)
            sp.wait_ge(n2T_mm, TILES)
            for q in range(1, GROUPS):
                send(n2_next[q * SAMPLE:(q + 1) * SAMPLE, :], n2_next[0:SAMPLE, :], packed)
            for q in range(GROUPS):
                sp.wait_ge(chosen, PAIRS * PTILES + q + 1)
                send(i_packed[q * SAMPLE:(q + 1) * SAMPLE, :], i_next[0:SAMPLE, q * SAMPLE:(q + 1) * SAMPLE], packed)
                send(g_packed[q * SAMPLE:(q + 1) * SAMPLE, :], g_next[0:SAMPLE, q * SAMPLE:(q + 1) * SAMPLE], packed)
            sp.wait_ge(y_ready, PTILES)
            send(t["y"][cols(PTILES - 1), :], y[:, :], y_out)
            sp.wait_ge(y_ready, TILES)
            send(t["y"][PROMPT:TOKENS, :], y[0:SAMPLE, :], y_out)
            sp.wait_ge(y_out, 16 * TILES)

        @block.tensor
        def _(pe):
            mm, tr = nc.tensor.matmul, nc.tensor.transpose
            xT = ps[:, 0:2, :].rearrange("p b (c n) -> p (b c) n", n=P)

            def transpose_x(n):
                pe.wait_ge(scaled, n + 1)
                need(pe, xn_ready, n)
                for c in range(DC):
                    last = tr(xT[:, c, :], xs[:, c * P:(c + 1) * P], ident[:, :])
                last.then_inc(xT_mm, 1)

            def tile_a(n, sample=False):
                pe.wait_ge(xn_ready, n + 1)
                need(pe, v_out, n)
                need(pe, vc_out, n)
                for c in range(DC):
                    last = mm(ps[:, 2, 0:KVW], xn_tile[:, c, :], w_vvc[:, c, 0:KVW], start=c == 0, stop=c == DC - 1)
                last.then_inc(v_mm, 1)
                for c in range(DC):
                    last = mm(ps[:, 3, :], xn_tile[:, c, :], w_vvc[:, c, KVW:KVW + CW], start=c == 0, stop=c == DC - 1)
                last.then_inc(vc_mm, 1)
                transpose_x(n + 1)
                pe.wait_ge(made, 2)
                pe.wait_ge(vc_ready, n + 1)
                need(pe, sp_out, n)
                for g in range(CG):
                    if sample:
                        last = mm(ps[:, 4, g * SAMPLE:(g + 1) * SAMPLE], vc_n[0:SAMPLE, g * P:(g + 1) * P],
                                  ws_T_smp[0:SAMPLE, g, :], start=True, stop=True)
                    else:
                        last = mm(ps[:, 4, g * P:(g + 1) * P], vc_n[:, g * P:(g + 1) * P], ws_T[:, g, :],
                                  start=True, stop=True)
                last.then_inc(sp_mm, 1)

            pe.wait_ge(cols_in, 80)
            transpose_x(0)
            pe.wait_ge(w_a_in, 16)
            tile_a(0)
            with pe.Fori(1, PTILES) as i:
                tile_a(i)
            tile_a(PTILES, sample=True)

            pe.wait_ge(w_mem_in, 16)
            for m in range(MT):
                pe.wait_ge(xn_ready, TILES + m + 1)
                need(pe, mkv_out, 2 * m)
                for half in range(2):
                    for c in range(DC):
                        last = mm(ps[:, 5 + half, :], xn_tile[:, c, :], w_mem[:, c, half * MW:(half + 1) * MW],
                                  start=c == 0, stop=c == DC - 1)
                    last.then_inc(mkv_mm, 1)
                if m + 1 < MT:
                    transpose_x(TILES + m + 1)
                pe.wait_ge(mkv_out, 2 * m + 1)
                need(pe, mkT_out, m)
                for h in range(MH):
                    last = tr(ps[:, 7, h * P:(h + 1) * P], mk_nat[:, m, h * P:(h + 1) * P], ident[:, :])
                last.then_inc(mkT_mm, 1)

            def block_b(n, slot, uses, first=False):
                pe.wait_ge(wb_in[slot], 16 * uses)
                for th in range(3):
                    if not first:
                        pe.wait_ge(b_out, 3 * n + (th - 2))
                    for c in range(DC):
                        last = mm(ps[:, 5 + th, 0:THIRD], w_ring[:, slot, c, :], xnT[:, c, th * THIRD:(th + 1) * THIRD],
                                  start=c == 0, stop=c == DC - 1)
                    last.then_inc(b_mm, 1)

            pe.wait_ge(xn_kept, TILES)
            pe.wait_ge(mkT_out, MT)
            pe.wait_ge(mkv_out, 2 * MT)
            block_b(0, 0, 1, first=True)
            block_b(1, 1, 1)
            with pe.Fori(1, 4) as i:
                for slot in range(2):
                    block_b(2 * i + slot, slot, i + 1)
            block_b(FK, 0, 5)
            with pe.Fori(0, 2) as i:
                for k in range(2):
                    slot = (FU + k) % 2
                    block_b(2 * i + FU + k, slot, i + (5 if slot else 6))
            pe.wait_ge(b_out, 3 * FEATS)
            tr(ps[:, 0, 0:KVW], feats[:, FK, PROMPT - P:PROMPT], ident[:, :])
            tr(ps[0:SAMPLE, 1, 0:KVW], feats[:, FK, PROMPT:TOKENS], ident[:, :]).then_inc(knat_mm, 1)
            pe.wait_ge(knat_out, 1)

            def window_scores(n, first=False):
                pe.wait_ge(c_in, 2 * n + 2)
                if not first:
                    pe.wait_ge(me_ready, n)
                    need(pe, swa_out, n - 1)
                keys = slice(P, 2 * P) if first else slice(0, 2 * P)
                for kv in range(KV):
                    part = slice(kv * HD, (kv + 1) * HD)
                    for g in range(GQ):
                        at = (g % 2) * 2 * P
                        last = mm(ps[:, 2 * kv + g // 2, at + keys.start:at + keys.stop], qs[part, FQ + g, :],
                                  ks[part, keys], start=True, stop=True)
                last.then_inc(s_mm, 1)

            def memory_scores(n):
                pe.wait_ge(s_taken, n + 1)
                for h in range(MH):
                    last = mm(ps[:, 1 + h // 2, (h % 2) * MEM:(h % 2 + 1) * MEM], qs[:, FM + h, :], mkT[:, h, :],
                              start=True, stop=True)
                last.then_inc(ms_mm, 1)

            def tile_c(n, slot, first=False, last_tile=False):
                if not last_tile:
                    window_scores(n + 1)
                pe.wait_ge(p_ready, n + 1)
                if not first:
                    pe.wait_ge(mpT_out, n)
                    pe.wait_ge(pT_out, 2 * n)
                    pe.wait_ge(mem_out, n)
                halves = (1,) if first else (0, 1)
                for kv in range(KV):
                    for half in halves:
                        for g in range(GQ):
                            last = tr(ps[:, 4 + 2 * kv + half, g * P:(g + 1) * P],
                                      sc[:, slot, kv * GQ + g, half * P:(half + 1) * P], ident[:, :])
                    last.then_inc(pT_mm, 1)
                if not last_tile:
                    memory_scores(n + 1)
                pe.wait_ge(pT_out, 2 * n + 2)
                pe.wait_ge(cv_in, n + 1)
                for kv in range(KV):
                    part = slice(kv * HD, (kv + 1) * HD)
                    for half in halves:
                        last = mm(ps[part, 0, :], vs[:, half, part], scT[:, kv, half, :, :].rearrange("p g n -> p (g n)"),
                                  start=half == halves[0], stop=half == 1)
                last.then_inc(pv_mm, 1)
                pe.wait_ge(mp_ready, n + 1)
                for h in range(MH):
                    for m in range(MT):
                        k = h * MT + m
                        last = tr(ps[:, 4 + k // 4, (k % 4) * P:(k % 4 + 1) * P], msc[:, slot, h, m * P:(m + 1) * P], ident[:, :])
                last.then_inc(mpT_mm, 1)
                pe.wait_ge(mpT_out, n + 1)
                for h in range(MH):
                    for m in range(MT):
                        last = mm(ps[:, 7, h * P:(h + 1) * P], mv[:, m, h * P:(h + 1) * P], mscT[:, h, m, :],
                                  start=m == 0, stop=m == MT - 1)
                last.then_inc(mpv_mm, 1)

            window_scores(0, first=True)
            memory_scores(0)
            tile_c(0, 0, first=True)
            with pe.Fori(0, PTILES // 2 - 1) as i:
                for k in range(2):
                    tile_c(2 * i + (k + 1), 1 - k)
            tile_c(PTILES - 1, 1, last_tile=True)

            pe.wait_ge(mem_out, PTILES)
            pe.wait_ge(swa_out, PTILES)
            pe.wait_ge(smp_in, 32)
            for kv in range(KV):
                part = slice(kv * HD, (kv + 1) * HD)
                for b in range(B):
                    q = feats[part, FQ:FQ + GQ, PROMPT + b * T:PROMPT + (b + 1) * T]
                    at = slice(b * GQ * T, (b + 1) * GQ * T)
                    mm(ps[:, kv, at], kcT[part, b, :], q, start=True, stop=True)
                    last = mm(ps[0:SAMPLE, 2 + kv, at], feats[part, FK, PROMPT:TOKENS], q, start=True, stop=True)
            last.then_inc(smp_pe, 1)
            pe.wait_ge(smp_act, 1)
            for kv in range(KV):
                at = kv * 2 * P
                tr(ps[:, 4, at:at + P], smp_sT[:, kv, :], ident[:, :])
                last = tr(ps[:, 4, at + P:at + P + SAMPLE], smp_snT[0:SAMPLE, kv, :], ident[0:SAMPLE, 0:SAMPLE])
            last.then_inc(smp_pe, 1)
            pe.wait_ge(apart, 2)
            for b in range(B):
                pe.wait_ge(smp_kv_in[cache_slot(b)], 16)
                km = cache_ring[cache_slot(b)].rearrange("p (h m) -> p h m", h=MH)
                for h in range(MH):
                    k = b * MH + h
                    last = mm(ps[:, 1, 0:MEM], q_apart[:, k * P:(k + 1) * P], km[:, h, :],
                              start=k == 0, stop=k == B * MH - 1)
                last.then_inc(smp_kv_used, 1)
            pe.wait_ge(smp_dve, 2)
            for kv in range(KV):
                tr(ps[:, 6, kv * P:(kv + 1) * P], smp_s[:, kv, 0:P], ident[:, :])
                last = tr(ps[0:SAMPLE, 7, kv * P:(kv + 1) * P], smp_s[:, kv, P:P + SAMPLE], ident[:, :])
            last.then_inc(smp_pe, 1)
            pe.wait_ge(smp_act, 3)
            for kv in range(KV):
                part = slice(kv * HD, (kv + 1) * HD)
                for b in range(B):
                    at = slice(b * GQ * T, (b + 1) * GQ * T)
                    mm(ps[part, 0, at], cv[:, b, part], smp_pT[:, kv, at], start=True, stop=False)
                    last = mm(ps[part, 0, at], v_nat[0:SAMPLE, PTILES, part], smp_pnT[0:SAMPLE, kv, at],
                              start=False, stop=True)
            last.then_inc(smp_pe, 1)
            pe.wait_ge(smp_dve, 5)
            for m in range(MT):
                last = tr(ps[:, 2, m * P:(m + 1) * P], smp_m[:, m * P:(m + 1) * P], ident[:, :])
            last.then_inc(smp_pe, 1)
            pe.wait_ge(smp_act, 5)
            for b in range(B):
                pe.wait_ge(smp_kv_in[cache_slot(B + b)], 16 * (1 + (B + b >= len(cache_ring))))
                vm = cache_ring[cache_slot(B + b)].rearrange("p (m w) -> p m w", m=MT)
                for m in range(MT):
                    last = mm(ps[:, 3, :], p_apart[m][:, b * P:(b + 1) * P], vm[:, m, :],
                              start=b == m == 0, stop=b == B - 1 and m == MT - 1)
                last.then_inc(smp_kv_used, 1)
            pe.wait_ge(smp_act, 6)
            for h in range(MH):
                last = tr(ps[:, 5, h * P:(h + 1) * P], smp_o[:, h * P:(h + 1) * P], ident[:, :])
            last.then_inc(smp_pe, 1)

            def unit(i, j, first=False):
                pe.wait_ge(wd_in[j], 16 * (i + 1))
                branch = feats[:, (FQ, FU, FM)[j]:(FQ, FU, FM)[j] + BC, :]
                for th in range(3):
                    part = slice(th * THIRD, (th + 1) * THIRD)
                    if not first:
                        pe.wait_ge(d_sig, 9 * i + (3 * j + th - 2))
                        pe.wait_ge(d_mul, 9 * i + (3 * j + th - 2))
                    for c in range(DC):
                        mm(ps[:, th, 0:THIRD], w_ring[:, j, c, :], xnT[:, c, part], start=c == 0, stop=c == DC - 1)
                    for c in range(BC):
                        last = mm(ps[:, 3 + th, 0:THIRD], w_ring[:, j, DC + c, :], branch[:, c, part],
                                  start=c == 0, stop=c == BC - 1)
                    last.then_inc(d_mm, 1)
                    if j == 0 and th == 0 and not first:
                        add_h0(i - 1)

            def add_h0(i):
                pe.wait_ge(merged_ready, i + 1)
                for half in range(2):
                    last = mm(ps[:, 6 + half:7 + half, :], merged[:, 0:P], w_out[:, bass.ds(i, 1), half * 512:(half + 1) * 512],
                              start=False, stop=False, skip_group_check=True)
                last.then_inc(h0_mm, 1)

            def empty_sums(a, b, **flags):
                for bank in (a, b):
                    last = mm(ps[:, bank, :], nothing[:, 0:P], nothing[:, :], skip_group_check=True, **flags)
                return last

            pe.wait_ge(smp_dve, 6)
            pe.wait_ge(chunk_out, CG)
            for j in range(NBR):
                unit(0, j, first=j == 0)
            empty_sums(6, 7, start=True, stop=False)
            pe.wait_ge(w_out_in, 16 * 4)
            with pe.Fori(1, DC) as i:
                for j in range(NBR):
                    unit(i, j)
            add_h0(DC - 1)
            empty_sums(6, 7, start=False, stop=True).then_inc(h_mm, 1)

            h_ps = ps[:, 4:6, :]
            n2T_ps = h_ps.rearrange("p b (c n) -> p (b c) n", n=P)

            def front_h(f, part):
                half, at = divmod(part, 2)
                if part == 0:
                    pe.wait_ge(m_in, 16 * f)
                    pe.wait_ge(n2T_out, f)
                for c in range(DC // 2 * at, DC // 2 * (at + 1)):
                    last = mm(h_ps[:, half, :], m_tile[:, c, :], w_out[:, c, half * 512:(half + 1) * 512],
                              start=c == 0, stop=c == DC - 1)
                if part == 3:
                    last.then_inc(h_mm, 1)

            def front_n2T(f):
                pe.wait_ge(n2_ready, f + 1)
                for c in range(DC):
                    last = tr(n2T_ps[:, c, :], n2_next[:, c * P:(c + 1) * P], ident[:, :])
                last.then_inc(n2T_mm, 1)

            def front_q(f, p, part):
                if part == 0:
                    need(pe, keys_taken, PAIRS * f + p)
                    pe.wait_ge(n2T_out, f + 1)
                for c in range(DC // 4 * part, DC // 4 * (part + 1)):
                    last = mm(ps[:, 6:7, :], n2T[:, c, :], w_q[:, c:c + 1, bass.ds(p * 4 * P, 4 * P)],
                              start=c == 0, stop=c == DC - 1)
                if part == 3:
                    last.then_inc(q_mm, 1)

            def front_qT(g):
                pe.wait_ge(q_out, g + 1)
                for k in range(4):
                    last = tr(ps[:, 7, k * P:(k + 1) * P], q_nat[:, k * P:(k + 1) * P], ident[:, :])
                last.then_inc(qT_mm, 1)

            def front_keys(g):
                pe.wait_ge(qT_out, g + 1)
                for k in range(4):
                    last = mm(ps[:, 6, k * NK:(k + 1) * NK], qT[:, k, :], subT[:, k % 2, :], start=True, stop=True)
                last.then_inc(key_mm, 1)

            def open_acc(n):
                need(pe, acc_taken, n)
                empty_sums(0, 1, start=True, stop=False)

            def add_v(batch, b, slots=range(NB), M=P):
                for j in slots:
                    pe.wait_ge(v_in[j], 16 * batch + 16)
                    pe.wait_ge(diags, 4 * batch + (j + 1))
                    for half in range(2):
                        last = mm(ps[0:M, half, :], diag[:, b % 2, j, 0:M], v_ring[:, j, half * 512:(half + 1) * 512],
                                  start=False, stop=False, skip_group_check=True)
                    last.then_inc(v_used, 1)

            def close_acc(batch, M=P):
                add_v(batch, BATCHES - 1, M=M)
                empty_sums(0, 1, start=False, stop=True).then_inc(acc_mm, 1)

            def tile_e(n, f, follows=True, M=P):
                for b in range(OPEN):
                    if b == 0 and follows:
                        close_acc(BATCHES * n - 1)
                    if b == 1:
                        open_acc(n)
                    if b:
                        add_v(BATCHES * n + (b - 1), b - 1, (0, 1), M)
                    if not follows:
                        first_front(b, 0)
                    if b:
                        add_v(BATCHES * n + (b - 1), b - 1, (2, 3), M)
                    if not follows:
                        first_front(b, 1)
                    elif f is not None:
                        if b < 4:
                            front_h(f, b)
                        elif b == 6:
                            front_n2T(f)
                if f is None:
                    return
                with pe.Fori(0, PAIRS) as p:
                    for b in range(PER_PAIR):
                        add_v(BATCHES * n + PER_PAIR * p + (OPEN + b - 1), (b - 1) % 2, (0, 1))
                        if b < 2:
                            front_q(f, p, 2 * b)
                        elif b == 2:
                            front_qT(PAIRS * f + p)
                        elif b == 3:
                            front_keys(PAIRS * f + p)
                        add_v(BATCHES * n + PER_PAIR * p + (OPEN + b - 1), (b - 1) % 2, (2, 3))
                        if b < 2:
                            front_q(f, p, 2 * b + 1)

            def first_keys(p):
                pe.wait_ge(w_q_in[p], 16)
                for part in range(4):
                    front_q(0, p, part)
                front_qT(p)
                front_keys(p)

            def first_front(b, h):
                if b in (0, 3):
                    p = 2 if b == 0 else 3
                    pe.wait_ge(w_q_in[p], 16)
                    front_q(0, p, 2 * h)
                    front_q(0, p, 2 * h + 1)
                    if h:
                        front_qT(p)
                elif b in (1, 4):
                    if h == 0:
                        front_keys(2 if b == 1 else 3)
                    else:
                        for part in (0, 1) if b == 1 else (2, 3):
                            front_h(1, part)
                if b == OPEN - 1 and h:
                    front_n2T(1)

            pe.wait_ge(d_sig, 3 * NBR * DC)
            pe.wait_ge(d_mul, 3 * NBR * DC)
            front_n2T(0)
            for p in range(2):
                first_keys(p)
            tile_e(0, 1, follows=False)
            with pe.Fori(1, PTILES) as i:
                tile_e(i, i + 1)
            tile_e(PTILES, None, M=SAMPLE)
            close_acc(LAST, SAMPLE)

        @block.scalar
        def _(act):
            fn = nc.scalar.activation

            def mean_square(n):
                act.wait_ge(x_in, 16 * n + 16)
                need(act, rstd, n)
                fn(squares[:, :], x_t[:, :], ACT.Square, scale=D ** -0.5, accum_out=stat[:, 0:1]).then_inc(mean_sq, 1)
                act.wait_ge(mean_sq, n + 1)

            def tile_a(n):
                mean_square(n + 1)
                act.wait_ge(v_mm, n + 1)
                alone(act)
                fn(v_nat[:, bass.ds(n, 1), :], ps[:, 2:3, 0:KVW], ACT.Copy).then_inc(v_out, 1)
                act.wait_ge(vc_mm, n + 1)
                need(act, vc_ready, n)
                fn(vc_gelu[:, :], ps[:, 3, :], ACT.Gelu).then_inc(vc_out, 1)
                act.wait_ge(vc_out, n + 1)
                need(act, vc_rstd, n)
                fn(vc_squares[:, :], vc_gelu[:, :], ACT.Square, accum_out=stat[:, 4:5]).then_inc(vc_sq, 1)
                act.wait_ge(vc_sq, n + 1)

            mean_square(0)
            tile_a(0)
            with act.Fori(1, TILES) as i:
                tile_a(i)
            for m in range(MT):
                if m + 1 < MT:
                    mean_square(TILES + m + 1)
                act.wait_ge(mkv_mm, 2 * m + 1)
                fn(mk_nat[:, m, :], ps[:, 5, :], ACT.Copy).then_inc(mkv_out, 1)
                act.wait_ge(mkv_mm, 2 * m + 2)
                fn(mv[:, m, :], ps[:, 6, :], ACT.Copy).then_inc(mkv_out, 1)

            def block_b(n, func):
                for th in range(3):
                    act.wait_ge(b_mm, 3 * n + (th + 1))
                    alone(act)
                    fn(feats[:, bass.ds(n, 1), th * THIRD:(th + 1) * THIRD], ps[:, 5 + th:6 + th, 0:THIRD], func)\
                        .then_inc(b_out, 1)

            with act.Fori(0, FU) as i:
                block_b(i, ACT.Copy)
            with act.Fori(0, CG) as i:
                block_b(i + FU, ACT.Gelu)

            act.wait_ge(xn_ready, TILES + MT)

            def window_exp(n, slot, first=False):
                keys = slice(P, 2 * P) if first else slice(0, 2 * P)
                act.wait_ge(m_ready, n + 1)
                for h in range(HEADS):
                    fn(sc[:, slot, h, keys], sc[:, slot, h, keys], ACT.Exp, bias=row[:, 1, h:h + 1], accum_out=row[:, 3, h:h + 1])
                fn(row[:, 4, :], row[:, 2, :], ACT.Exp).then_inc(e_ready, 1)

            def memory_exp(n, slot):
                act.wait_ge(mm_ready, n + 1)
                need(act, mpT_mm, n - 1)
                for h in range(MH):
                    last = fn(msc[:, slot, h, :], ps[:, 1 + h // 2, (h % 2) * MEM:(h % 2 + 1) * MEM], ACT.Exp,
                              bias=row[:, 5, h:h + 1], scale=MEM_SCALE, accum_out=row[:, 6, h:h + 1])
                last.then_inc(me_ready, 1)

            def tile_c(n, slot, first=False, last_tile=False):
                for kv in range(KV):
                    act.wait_ge(pT_mm, 2 * n + (kv + 1))
                    if not first:
                        act.wait_ge(pv_mm, n)
                    lo = 1 if first else 0
                    fn(scT[:, kv, lo:2, :, :].rearrange("p a g n -> p a (g n)"), ps[:, 4 + 2 * kv + lo:6 + 2 * kv, :],
                       ACT.Copy).then_inc(pT_out, 1)
                if not last_tile:
                    window_exp(n + 1, 1 - slot)
                if not last_tile:
                    memory_exp(n + 1, 1 - slot)

            window_exp(0, 0, first=True)
            memory_exp(0, 0)
            tile_c(0, 0, first=True)
            with act.Fori(0, PTILES // 2 - 1) as i:
                for k in range(2):
                    tile_c(2 * i + (k + 1), 1 - k)
            tile_c(PTILES - 1, 1, last_tile=True)

            act.wait_ge(mpv_mm, PTILES)
            act.wait_ge(smp_pe, 1)
            fn(smp_sT[:, :, :], ps[:, 0:2, 0:P], ACT.Copy)
            fn(smp_snT[0:SAMPLE, :, :], ps[0:SAMPLE, 2:4, 0:P], ACT.Copy).then_inc(smp_act, 1)
            act.wait_ge(smp_dve, 1)
            for kv in range(KV):
                fn(smp_s[:, kv, :], smp_s[:, kv, :], ACT.Exp, bias=row[:, 1, kv:kv + 1], accum_out=row[:, 3, kv:kv + 1])
            fn(row[:, 4, 0:KV], row[:, 2, 0:KV], ACT.Exp).then_inc(smp_act, 1)
            act.wait_ge(smp_pe, 3)
            fn(smp_pT[:, :, :].rearrange("p a n -> p (a n)"), ps[:, 6, 0:KV * P], ACT.Copy)
            fn(smp_pnT[0:SAMPLE, :, :].rearrange("p a n -> p (a n)"), ps[0:SAMPLE, 7, 0:KV * P], ACT.Copy)\
                .then_inc(smp_act, 1)
            act.wait_ge(smp_dve, 4)
            fn(smp_m[:, :], ps[:, 1, 0:MEM], ACT.Exp, bias=row[:, 5, 0:1], scale=MEM_SCALE,
               accum_out=row[:, 6, 0:1]).then_inc(smp_act, 1)
            act.wait_ge(smp_pe, 5)
            act.wait_ge(apart, 4)
            for m in range(MT):
                last = fn(p_apart[m].rearrange("p (b n) -> p b n", b=B)[:, :, 0:MH * T],
                          ps[:, 2, m * P:(m + 1) * P].rearrange("p (b n) -> p b n", b=B), ACT.Copy)
            last.then_inc(smp_act, 1)
            act.wait_ge(smp_kv_used, 2 * B)
            fn(smp_o[:, :], ps[:, 3, :], ACT.Copy).then_inc(smp_act, 1)

            def unit(i, j, first=False):
                for th in range(3):
                    act.wait_ge(d_mm, 9 * i + (3 * j + th + 1))
                    if not first:
                        act.wait_ge(d_mul, 9 * i + (3 * j + th - 2))
                    alone(act)
                    fn(sig[:, th * THIRD:(th + 1) * THIRD], ps[:, th, 0:THIRD], ACT.Sigmoid,
                       bias=gate_b[:, bass.ds(3 * i + j, 1)]).then_inc(d_sig, 1)

            act.wait_ge(smp_kv_used, 2 * B)
            for j in range(NBR):
                unit(0, j, first=j == 0)
            with act.Fori(1, DC) as i:
                for j in range(NBR):
                    unit(i, j)

            A = Steps(act, act_)

            def square_root(a, R, signal):
                A.add(fn(dump[0:R, :], a[0:R, :], ACT.Square, scale=D ** -0.5, accum_out=norm[0:R, 0:1]))
                A.settle()
                A.add(fn(norm[0:R, 1:2], norm[0:R, 0:1], ACT.Sqrt, bias=eps[0:R, 0:1]), signal)

            def front_norm(f):
                act.wait_ge(h_sum, f + 1)
                square_root(h_next, P, root)

            def front_n2T(f):
                act.wait_ge(n2T_mm, f + 1)
                A.add(fn(n2T[:, :, :].rearrange("p c n -> p (c n)"), ps[:, 4:6, :].rearrange("p a n -> p (a n)"),
                         ACT.Copy), n2T_out)

            def front_q(g):
                act.wait_ge(q_mm, g + 1)
                A.add(fn(q_nat[:, :], ps[:, 6, :], ACT.Copy), q_out)

            def front_qT(g):
                act.wait_ge(qT_mm, g + 1)
                A.add(fn(qT[:, :, :].rearrange("p k n -> p (k n)"), ps[:, 7, :], ACT.Copy), qT_out)

            def front_exp(g):
                act.wait_ge(shifted_ready, g + 1)
                A.add(fn(raised[:, :, :].rearrange("p h k -> p (h k)"), shifted[:, :, :].rearrange("p h k -> p (h k)"),
                         ACT.Exp), raised_ready)

            def gelu(batch, b):
                act.wait_ge(dots, 4 * batch + 4)
                A.add(fn(gelu4[:, b % 2, :], act4[:, b % 2, :], ACT.Gelu), gelus)

            def make_diag(batch, b, M=P):
                act.wait_ge(c_ready, batch + 1)
                need(act, v_used, 4 * batch - 4)
                for j in range(NB):
                    A.add(fn(diag[:, b % 2, j, 0:M], (ident if M == P else idents)[:, :], ACT.Copy, scale=c4[:, b % 2, j:j + 1]), diags)

            def final_root(n, R=P):
                act.wait_ge(acc_taken, n + 1)
                square_root(h_cur, R, y_root)

            def tile_e(n, f, follows=True, M=P):
                for b in range(OPEN):
                    if b:
                        make_diag(BATCHES * n + (b - 1), b - 1, M)
                    elif follows:
                        make_diag(BATCHES * n - 1, BATCHES - 1)
                    if b == 1 and follows:
                        final_root(n - 1)
                    if not follows and b in (1, 4, 6):
                        front_exp((1, 4, 6).index(b) + 1)
                    gelu(BATCHES * n + b, b)
                    if not follows:
                        if b in (0, 3):
                            front_q(2 if b == 0 else 3)
                            front_qT(2 if b == 0 else 3)
                        elif b == OPEN - 2:
                            front_norm(f)
                        elif b == OPEN - 1:
                            front_n2T(f)
                    elif f is not None:
                        if b == 4:
                            front_norm(f)
                        elif b == 6:
                            front_n2T(f)
                if f is None:
                    return
                with act.Fori(0, PAIRS) as p:
                    for b in range(PER_PAIR):
                        if b == 2:
                            front_q(PAIRS * f + p)
                        elif b == 5:
                            front_exp(PAIRS * f + p)
                        make_diag(BATCHES * n + PER_PAIR * p + (OPEN + b - 1), (b - 1) % 2)
                        gelu(BATCHES * n + PER_PAIR * p + (OPEN + b), b)
                        if b == 2:
                            front_qT(PAIRS * f + p)

            front_norm(0)
            front_n2T(0)
            for p in range(2):
                front_q(p)
                front_qT(p)
                if p == 0:
                    front_exp(p)
            tile_e(0, 1, follows=False)
            with A.loop(1, PTILES, 2) as i:
                tile_e(i, i + 1)
            tile_e(PTILES, None, M=SAMPLE)
            make_diag(LAST, BATCHES - 1, SAMPLE)
            final_root(PTILES, SAMPLE)

        @block.vector
        def _(dve):
            V = Steps(dve, dve_)
            v = nc.vector

            V.add(v.memset(nothing[:, :], 0.0))
            V.add(v.memset(eps[:, :], EPS))
            dve.wait_ge(cols_in, 80)

            def scale_x(n):
                dve.wait_ge(rstd, n + 1)
                need(dve, xT_mm, n)
                v.tensor_scalar(xs[:, :], x_t[:, :], stat[:, 2:3], None, ALU.mult).then_inc(scaled, 1)

            def xn(n, col, kept):
                dve.wait_ge(xT_mm, n + 1)
                need(dve, xn_kept, kept)
                xT = ps[:, 0:2, :].rearrange("p b (c n) -> p (b c) n", n=P)
                v.tensor_tensor(xn_tile[:, :, :], xT, wide(col[:, :], DC, P), ALU.mult).then_inc(xn_ready, 1)

            def tile_a(n, sample=False):
                scale_x(n + 1)
                dve.wait_ge(vc_mm, n + 1)
                xn(n + 1, mem_norm_col if sample else norm1_col, n + 1)
                dve.wait_ge(vc_rstd, n + 1)
                need(dve, sp_mm, n)
                v.scalar_tensor_tensor(vc_n[:, :], vc_gelu[:, :], stat[:, 6:7], chunk_g, ALU.mult, ALU.mult)\
                    .then_inc(vc_ready, 1)
                dve.wait_ge(sp_mm, n + 1)
                if sample:
                    v.tensor_tensor(spT[:, :, PROMPT:TOKENS], ps[:, 4, 0:CG * SAMPLE].rearrange("p (g n) -> p g n", g=CG),
                                    chunk_b_smp[:, :, :], ALU.add).then_inc(sp_out, 1)
                else:
                    v.tensor_tensor(spT[:, :, cols(n)], ps[:, 4, :].rearrange("p (g n) -> p g n", g=CG),
                                    chunk_b[:, :, :], ALU.add).then_inc(sp_out, 1)

            scale_x(0)
            xn(0, norm1_col, 0)
            dve.wait_ge(chunk_in, 16 * len(FIRST_LOADS))
            tile_a(0)
            with dve.Fori(1, PTILES) as i:
                tile_a(i)
            tile_a(PTILES, sample=True)
            for m in range(MT):
                if m + 1 < MT:
                    scale_x(TILES + m + 1)
                    dve.wait_ge(mkv_mm, 2 * m + 2)
                    xn(TILES + m + 1, mem_norm_col, TILES)
                dve.wait_ge(mkT_mm, m + 1)
                v.tensor_copy(mkT[:, :, m * P:(m + 1) * P], ps[:, 7, :].rearrange("p (h n) -> p h n", h=MH))\
                    .then_inc(mkT_out, 1)

            dve.wait_ge(consts_in, 16 * len(LOADS))

            dve.wait_ge(sp_out, TILES)
            with dve.Fori(0, CG) as i:
                dve.wait_ge(b_out, 3 * i + 3 * (FU + 1))
                v.tensor_tensor(feats[:, bass.ds(i + FU, 1), 0:TOKENS], feats[:, bass.ds(i + FU, 1), 0:TOKENS],
                                spT[:, bass.ds(i, 1), 0:TOKENS], ALU.mult).then_inc(chunk_out, 1)
            dve.wait_ge(knat_mm, 1)
            v.tensor_copy(knat[:, 0, :], ps[:, 0, 0:KVW])
            v.tensor_copy(knat[0:SAMPLE, 1, :], ps[0:SAMPLE, 1, 0:KVW]).then_inc(knat_out, 1)

            def maxima(n, slot, first=False):
                keys = slice(P, 2 * P) if first else slice(0, 2 * P)
                read = ps[:, 0:4, :].rearrange("p b (g n) -> p (b g) n", g=2)[:, :, keys]
                dve.wait_ge(s_mm, n + 1)
                need(dve, pT_mm, 2 * n - 2)
                V.add(v.scalar_tensor_tensor(sc[:, slot, :, keys], read, SWA_SCALE, swa_bias[:, :, keys], ALU.mult, ALU.add), s_taken, n + 1)
                V.settle()
                V.add(v.tensor_reduce(row[:, 0, :], sc[:, slot, :, keys], AX.X, ALU.max))
                V.settle()
                V.add(v.tensor_tensor(row[:, 0, :], row[:, 0, :], sinks, ALU.max))
                V.settle()
                V.add(v.tensor_scalar(row[:, 1, :], row[:, 0, :], -1.0, None, ALU.mult))
                V.add(v.tensor_tensor(row[:, 2, :], sinks, row[:, 0, :], ALU.subtract), m_ready)

            def memory_maxima(n):
                dve.wait_ge(ms_mm, n + 1)
                V.add(v.tensor_reduce(row[:, 7, 0:MH], ps[:, 1:3, :].rearrange("p b (g n) -> p (b g) n", g=2), AX.X, ALU.max))
                V.settle()
                V.add(v.tensor_scalar(row[:, 5, 0:MH], row[:, 7, 0:MH], -MEM_SCALE, None, ALU.mult), mm_ready)

            def divide(n, slot, first=False):
                keys = slice(P, 2 * P) if first else slice(0, 2 * P)
                nk = P if first else 2 * P
                dve.wait_ge(e_ready, n + 1)
                V.add(v.tensor_tensor(row[:, 3, :], row[:, 3, :], row[:, 4, :], ALU.add))
                V.settle()
                V.add(v.reciprocal(row[:, 4, :], row[:, 3, :]))
                V.settle()
                V.add(v.tensor_tensor(sc[:, slot, :, keys], sc[:, slot, :, keys], wide(row[:, 4, :], HEADS, nk), ALU.mult), p_ready)

            def memory_divide(n, slot):
                dve.wait_ge(me_ready, n + 1)
                V.add(v.reciprocal(row[:, 7, 0:MH], row[:, 6, 0:MH]))
                V.settle()
                V.add(v.tensor_tensor(msc[:, slot, :, :], msc[:, slot, :, :], wide(row[:, 7, 0:MH], MH, MEM), ALU.mult), mp_ready, n + 1)

            def tile_c(n, slot, last_tile=False):
                if not last_tile:
                    maxima(n + 1, 1 - slot)
                    memory_maxima(n + 1)
                dve.wait_ge(pv_mm, n + 1)
                V.add(v.tensor_copy(feats[:, FQ:FQ + GQ, cols(n)], ps[:, 0, :].rearrange("p (g n) -> p g n", g=GQ)), swa_out)
                dve.wait_ge(mpT_mm, n + 1)
                need(dve, mpv_mm, n)
                V.add(v.tensor_copy(mscT[:, :, :, :].rearrange("p h m n -> p (h m n)"),
                                    ps[:, 4:6, :].rearrange("p a n -> p (a n)")), mpT_out)
                if not last_tile:
                    divide(n + 1, 1 - slot)
                dve.wait_ge(mpv_mm, n + 1)
                V.add(v.tensor_copy(feats[:, FM:FM + MH, cols(n)], ps[:, 7, :].rearrange("p (h n) -> p h n", h=MH)), mem_out, n + 1)
                if not last_tile:
                    memory_divide(n + 1, 1 - slot)

            maxima(0, 0, first=True)
            memory_maxima(0)
            divide(0, 0, first=True)
            memory_divide(0, 0)
            tile_c(0, 0)
            with V.loop(0, PTILES // 2 - 1, 2 * 7) as i:
                for k in range(2):
                    tile_c(2 * i + (k + 1), 1 - k)
            tile_c(PTILES - 1, 1, last_tile=True)

            V.settle()
            dve.wait_ge(smp_pe, 2)
            V.add(v.scalar_tensor_tensor(smp_s[:, :, :], ps[:, 4, :].rearrange("p (k n) -> p k n", k=KV)[:, :, 0:P + SAMPLE],
                                         SWA_SCALE, smp_bias[:, :, :], ALU.mult, ALU.add))
            V.settle()
            V.add(v.tensor_reduce(row[:, 0, 0:KV], smp_s[:, :, :], AX.X, ALU.max))
            V.settle()
            V.add(v.tensor_tensor(row[:, 0, 0:KV], row[:, 0, 0:KV], smp_sinks, ALU.max))
            V.settle()
            V.add(v.tensor_scalar(row[:, 1, 0:KV], row[:, 0, 0:KV], -1.0, None, ALU.mult))
            V.add(v.tensor_tensor(row[:, 2, 0:KV], smp_sinks, row[:, 0, 0:KV], ALU.subtract), smp_dve)
            dve.wait_ge(smp_act, 2)
            V.add(v.tensor_tensor(row[:, 3, 0:KV], row[:, 3, 0:KV], row[:, 4, 0:KV], ALU.add))
            V.settle()
            V.add(v.reciprocal(row[:, 4, 0:KV], row[:, 3, 0:KV]))
            V.settle()
            V.add(v.tensor_tensor(smp_s[:, :, :], smp_s[:, :, :], wide(row[:, 4, 0:KV], KV, P + SAMPLE), ALU.mult), smp_dve)
            dve.wait_ge(smp_pe, 4)
            for g in range(GQ):
                V.add(v.tensor_copy(
                    feats[:, FQ + g, PROMPT:TOKENS].rearrange("p (b t) -> p b t", b=B),
                    ps[:, 0, 0:P].rearrange("p (b g t) -> p b g t", b=B, g=GQ)[:, :, g, :]),
                    smp_dve if g == GQ - 1 else None)
            dve.wait_ge(smp_kv_used, B)
            V.add(v.tensor_reduce(row[:, 7, 0:1], ps[:, 1, 0:MEM], AX.X, ALU.max))
            V.settle()
            V.add(v.tensor_scalar(row[:, 5, 0:1], row[:, 7, 0:1], -MEM_SCALE, None, ALU.mult), smp_dve)
            dve.wait_ge(smp_act, 4)
            V.add(v.reciprocal(row[:, 7, 0:1], row[:, 6, 0:1]))
            V.settle()
            V.add(v.tensor_scalar(smp_m[:, :], smp_m[:, :], row[:, 7, 0:1], None, ALU.mult), smp_dve)
            dve.wait_ge(smp_pe, 6)
            for h in range(MH):
                V.add(v.tensor_copy(
                    feats[:, FM + h, PROMPT:TOKENS].rearrange("p (b t) -> p b t", b=B),
                    ps[:, 5, h * P:(h + 1) * P].rearrange("p (b h t) -> p b h t", b=B, h=MH)[:, :, h, :]),
                    smp_dve if h == MH - 1 else None, 6)

            V.settle()
            V.add(v.memset(merged[:, TOKENS:PADDED], 0.0))
            V.settle()

            def unit(i, j, first=False):
                for th in range(3):
                    part = slice(th * THIRD, (th + 1) * THIRD)
                    dve.wait_ge(d_sig, 9 * i + (3 * j + th + 1))
                    if j == 0:
                        if th == 0 and not first:
                            dve.wait_ge(merged_out, 16 * i)
                            dve.wait_ge(h0_mm, i)
                        V.add(v.tensor_tensor(merged[:, part], ps[:, 3 + th, 0:THIRD], sig[:, part], ALU.mult), d_mul, 9 * i + (3 * j + th + 1))
                    else:
                        V.settle()
                        V.add(v.tensor_tensor(prod[:, part], ps[:, 3 + th, 0:THIRD], sig[:, part], ALU.mult), d_mul, 9 * i + (3 * j + th + 1))
                        V.settle()
                        V.add(v.tensor_tensor(merged[:, part], merged[:, part], prod[:, part], ALU.add),
                              merged_ready if j == NBR - 1 and th == 2 else None, i + 1)

            for j in range(NBR):
                unit(0, j, first=True)
            with V.loop(1, DC, 5) as i:
                for j in range(NBR):
                    unit(i, j)

            V.settle()
            dve.wait_ge(w_out_in, 16 * 4)

            def hold():
                V.settle()
                alone(dve)

            def inverse_root(R, scr):
                V.add(v.reciprocal(scr[0:R, 2:3], scr[0:R, 1:2]))
                V.add(v.tensor_scalar(scr[0:R, 3:4], scr[0:R, 0:1], EPS, None, ALU.add))
                V.settle()
                V.add(v.scalar_tensor_tensor(scr[0:R, 4:5], scr[0:R, 2:3], scr[0:R, 3:4], scr[0:R, 2:3], ALU.mult, ALU.mult))
                V.settle()
                V.add(v.tensor_scalar(scr[0:R, 5:6], scr[0:R, 4:5], -0.5, 1.5, ALU.mult, ALU.add))
                V.settle()
                V.add(v.tensor_tensor(scr[0:R, 6:7], scr[0:R, 2:3], scr[0:R, 5:6], ALU.mult))
                V.settle()

            def front_sum(f, bank=4):
                dve.wait_ge(h_mm, f + 1)
                dve.wait_ge(h_in, 16 * f + 16)
                V.add(v.tensor_tensor(h_next[:, :], h_next[:, :], ps[:, bank:bank + 2, :].rearrange("p a n -> p (a n)"), ALU.add), h_sum, f + 1)

            def front_norm(f):
                dve.wait_ge(root, f + 1)
                inverse_root(P, norm)
                V.add(v.scalar_tensor_tensor(n2_next[:, :], h_next[:, :], norm[:, 6:7], norm2_g, ALU.mult, ALU.mult), n2_ready, f + 1)

            def keys_first(g):
                dve.wait_ge(key_mm, g + 1)
                hold()
                s4 = ps[:, 6, :].rearrange("p (k n) -> p k n", k=4)
                for k in range(4):
                    V.add(v.max(sv[:, k, 0:8], s4[:, k, :]))
                hold()
                for k in range(4):
                    V.add(v.max_index(si[:, k, 0:8], sv[:, k, 0:8], s4[:, k, :]))
                for k in range(4):
                    V.add(v.match_replace(rest[:, k, :], sv[:, k, 0:8], s4[:, k, :], LOWEST),
                          keys_taken if k == 3 else None, g + 1)

            def keys_second(g):
                hold()
                for k in range(4):
                    V.add(v.max(sv[:, k, 8:16], rest[:, k, :]))
                hold()
                for k in range(4):
                    V.add(v.max_index(si[:, k, 8:16], sv[:, k, 8:16], rest[:, k, :]))
                for h in range(2):
                    V.add(v.tensor_tensor(cand[:, h, :].rearrange("p (a b) -> p a b", a=K), wide(sv[:, 2 * h, :], K, K),
                                          sv[:, 2 * h + 1, :].unsqueeze(1).broadcast_to([P, K, K]), ALU.add))
                V.settle()
                V.add(v.tensor_copy(sif[:, :, :], si[:, :, :]))

            def pairs_best(g):
                hold()
                for h in range(2):
                    V.add(v.max(cv16[:, h, 0:8], cand[:, h, :]))
                hold()
                for h in range(2):
                    V.add(v.max_index(ci16[:, h, 0:8], cv16[:, h, 0:8], cand[:, h, :]))
                for h in range(2):
                    V.add(v.match_replace(cand2[:, h, :], cv16[:, h, 0:8], cand[:, h, :], LOWEST))
                hold()
                for h in range(2):
                    V.add(v.max(cv16[:, h, 8:16], cand2[:, h, :]))
                hold()
                for h in range(2):
                    V.add(v.max_index(ci16[:, h, 8:16], cv16[:, h, 8:16], cand2[:, h, :]))
                V.add(v.tensor_tensor(shifted[:, :, :], cv16[:, :, :], cv16[:, :, 0:1].broadcast_to([P, 2, K]), ALU.subtract), shifted_ready, g + 1)

            flat = "p h k -> p (h k)"

            def key_numbers(half):
                V.settle()
                V.add(v.tensor_tensor(match[:, :, :, :].rearrange("p h k a -> p (h k) a"),
                                      wide(hilof[:, half].rearrange(flat), 2 * K, K),
                                      iota16[:, :].unsqueeze(1).broadcast_to([P, 2 * K, K]), ALU.is_equal))
                V.settle()
                number = sif[:, half:4:2, :]
                V.add(v.tensor_tensor(match[:, :, :, :], match[:, :, :, :],
                                      number.unsqueeze(2).broadcast_to([P, 2, K, K]), ALU.mult))
                V.settle()
                V.add(v.tensor_reduce(picked[:, half].rearrange(flat), match[:, :, :, :].rearrange("p h k a -> p (h k) a"),
                                      AX.X, ALU.add))

            def rows_found():
                V.settle()
                V.add(v.tensor_scalar(hilo[:, 0], ci16[:, :, :], 4, None, ALU.logical_shift_right))
                V.add(v.tensor_scalar(hilo[:, 1], ci16[:, :, :], 15, None, ALU.bitwise_and))
                V.settle()
                V.add(v.tensor_copy(hilof[:, :, :, :], hilo[:, :, :, :]))
                key_numbers(0)

            def experts(f, p):
                g = PAIRS * f + p
                key_numbers(1)
                V.settle()
                need(dve, staged, STAGES * (f - 1) + 1)
                V.add(v.scalar_tensor_tensor(i_next[:, bass.ds(2 * K * p, 2 * K)], picked[:, 0].rearrange(flat), float(NK),
                                             picked[:, 1].rearrange(flat), ALU.mult, ALU.add))
                dve.wait_ge(raised_ready, g + 1)
                V.add(v.tensor_reduce(stat[:, 8:10], raised[:, :, :], AX.X, ALU.add))
                V.settle()
                V.add(v.reciprocal(stat[:, 10:12], stat[:, 8:10]))
                V.settle()
                V.add(v.tensor_tensor(g_next[:, bass.ds(2 * K * p, 2 * K)].rearrange("p (h k) -> p h k", h=2), raised[:, :, :],
                                      wide(stat[:, 10:12], 2, K), ALU.mult), chosen, g + 1)

            def move_n2():
                V.settle()
                V.add(v.tensor_copy(n2_cur, n2_next))
                V.settle()

            def move_choice(n):
                V.settle()
                need(dve, staged, STAGES * n)
                V.add(v.tensor_copy(i_cur, i_next))
                V.add(v.tensor_copy(g_cur, g_next), moved, n + 1)

            def move_h(n):
                V.add(v.tensor_copy(h_cur, h_next), h_moved, n + 1)

            def dot(batch, b, slots):
                for j in slots:
                    dve.wait_ge(u_in[b % 2][j], 8 * batch + 16 - 8 * (b % 2))
                    need(dve, dots, 4 * batch + (j - 1))
                    V.add(v.scalar_tensor_tensor(product[j % 2], u_ring[:, b % 2, j, :], 1.0, n2_cur[:, :],
                                                 ALU.mult, ALU.mult, accum_out=act4[:, b % 2, j:j + 1]), dots, 4 * batch + (j + 1))

            product = [u_dump, ps[:, 2:4, :].rearrange("p a n -> p (a n)")]

            def weigh(batch, at, b, weights=g_cur):
                dve.wait_ge(gelus, batch + 1)
                need(dve, diags, 4 * batch - 4)
                V.add(v.tensor_tensor(c4[:, b % 2, :], gelu4[:, b % 2, :], weights[:, bass.ds(at, NB)], ALU.mult), c_ready, batch + 1)

            def take_acc(n, R=P):
                dve.wait_ge(acc_mm, n + 1)
                dve.wait_ge(h_moved, n + 1)
                V.add(v.tensor_tensor(h_cur[0:R, :], h_cur[0:R, :], ps[0:R, 0:2, :].rearrange("p a n -> p (a n)"), ALU.add), acc_taken, n + 1)

            def final_norm(n, R=P):
                dve.wait_ge(y_root, n + 1)
                inverse_root(R, norm)
                need(dve, y_out, 16 * n)
                V.add(v.scalar_tensor_tensor(y[0:R, :], h_cur[0:R, :], norm[0:R, 6:7], final_g[0:R, :], ALU.mult, ALU.mult),
                      y_ready, n + 1)
                V.settle()

            def tile_e(n, f, follows=True, weights=g_cur):
                if f is None:
                    weigh(BATCHES * n - 1, NB * (BATCHES - 1), BATCHES - 1)
                    dve.wait_ge(packed, PACKED)
                move_n2()
                for b in range(OPEN):
                    dot(BATCHES * n + b, b, (0, 1))
                    if b:
                        weigh(BATCHES * n + (b - 1), NB * (b - 1), b - 1, weights)
                    elif follows and f is not None:
                        weigh(BATCHES * n - 1, NB * (BATCHES - 1), BATCHES - 1)
                        move_choice(n)
                    if b == 1 and follows:
                        take_acc(n - 1)
                    if not follows:
                        first_front(b, 0)
                    dot(BATCHES * n + b, b, (2, 3))
                    if b == 2 and follows:
                        final_norm(n - 1)
                        move_h(n)
                    if not follows:
                        first_front(b, 1)
                    elif f is not None:
                        if b == 4:
                            front_sum(f)
                        elif b == 5:
                            front_norm(f)
                if f is None:
                    return
                with V.loop(0, PAIRS, PAIR_STEPS) as p:
                    for b in range(PER_PAIR):
                        dot(BATCHES * n + PER_PAIR * p + (OPEN + b), b, (0, 1))
                        weigh(BATCHES * n + PER_PAIR * p + (OPEN + b - 1), NB * PER_PAIR * p + NB * (OPEN + b - 1), (b - 1) % 2)
                        if b == 4:
                            keys_second(PAIRS * f + p)
                        elif b == 5:
                            rows_found()
                        dot(BATCHES * n + PER_PAIR * p + (OPEN + b), b, (2, 3))
                        if b == 3:
                            keys_first(PAIRS * f + p)
                        elif b == 4:
                            pairs_best(PAIRS * f + p)
                        elif b == 5:
                            experts(f, p)

            def first_front(b, h):
                if b == 0 and h:
                    move_h(0)
                at = 2 * b + h
                p, stage = divmod(at, 5)
                p += 1
                if p < PAIRS:
                    if stage < 3:
                        (keys_first, keys_second, pairs_best)[stage](p)
                    elif stage == 3:
                        rows_found()
                    else:
                        experts(0, p)
                if at == 2 * OPEN - 2:
                    move_choice(0)
                elif at == 2 * OPEN - 4:
                    front_sum(1)
                elif at == 2 * OPEN - 1:
                    front_norm(1)

            PAIR_STEPS = 11 + 11 + 10 + 12
            front_sum(0, bank=6)
            front_norm(0)
            keys_first(0)
            keys_second(0)
            pairs_best(0)
            rows_found()
            experts(0, 0)
            tile_e(0, 1, follows=False, weights=g_next)
            tile_steps = 2 + 5 + 5 + PAIRS * PAIR_STEPS
            with V.loop(1, PTILES, tile_steps) as i:
                tile_e(i, i + 1)
            tile_e(PTILES, None, weights=g_packed)
            weigh(LAST, NB * (OPEN - 1), BATCHES - 1, g_packed)
            take_acc(PTILES, SAMPLE)
            final_norm(PTILES, SAMPLE)

        @block.gpsimd
        def _(pool):
            G = Steps(pool, pool_)
            g = nc.gpsimd

            G.add(g.memset(stat[:, 3:4], -0.5))
            G.settle()

            def inverse_root(signal, taken, n, at, scale):
                pool.wait_ge(signal, n + 1)
                need(pool, taken, n)
                alone(pool)
                G.add(g.tensor_scalar(stat[:, at + 1:at + 2], stat[:, at:at + 1], scale, EPS, ALU.mult, ALU.add))
                G.settle()

            def rstd_x(n):
                inverse_root(mean_sq, scaled, n, 0, 1.0)
                g.tensor_tensor(stat[:, 2:3], stat[:, 1:2], stat[:, 3:4], ALU.pow).then_inc(rstd, 1)

            def tile_a(n):
                pool.wait_ge(xn_ready, n + 1)
                g.tensor_copy(xnT[:, :, cols(n)], xn_tile[:, :, :]).then_inc(xn_kept, 1)
                rstd_x(n + 1)
                inverse_root(vc_sq, vc_ready, n, 4, 1.0 / CW)
                g.tensor_tensor(stat[:, 6:7], stat[:, 5:6], stat[:, 3:4], ALU.pow).then_inc(vc_rstd, 1)

            rstd_x(0)
            pool.wait_ge(chunk_in, 16 * len(FIRST_LOADS))
            g.affine_select(out=ws_T[:, :, :], in_=ws_T[:, :, :], compare_op=ALU.is_ge, fill=0.0, base=0,
                            pattern=[[0, CG], [1, P]], channel_multiplier=-1).then_inc(made, 1)
            small = ws_T_smp[0:SAMPLE, :, :]
            g.affine_select(out=small, in_=small, compare_op=ALU.is_ge, fill=0.0, base=0,
                            pattern=[[0, CG], [1, SAMPLE]], channel_multiplier=-1).then_inc(made, 1)
            tile_a(0)
            with G.loop(1, TILES, 2) as i:
                tile_a(i)
            for m in range(1, MT):
                rstd_x(TILES + m)

            pool.wait_ge(b_out, 3 * FU)
            pool.wait_ge(v_out, TILES)
            pool.wait_ge(xn_ready, TILES + MT)
            pool.wait_ge(mkT_mm, MT)
            pool.wait_ge(stored, 16 * (3 + 2 * MT))
            g.tensor_copy(qs[:, :, :], feats[:, 0:FK, 0:P]).then_inc(c_in, 1)
            g.tensor_copy(ks[:, P:2 * P], feats[:, FK, 0:P]).then_inc(c_in, 1)
            g.tensor_copy(vs[:, 1, :], v_nat[:, 0, :]).then_inc(cv_in, 1)
            with pool.Fori(1, PTILES) as i:
                pool.wait_ge(ms_mm, i)
                g.tensor_copy(qs[:, :, :], feats[:, 0:FK, cols(i)]).then_inc(c_in, 1)
                g.tensor_copy(ks.unsqueeze(1), feats[:, FK:FK + 1, bass.ds(i * P - P, 2 * P)]).then_inc(c_in, 1)
                pool.wait_ge(pv_mm, i)
                g.tensor_copy(vs[:, :, :], v_nat[:, bass.ds(i - 1, 2), :]).then_inc(cv_in, 1)

            pool.wait_ge(chunk_out, CG)
            g.memset(q_apart, 0.0).then_inc(apart, 1)
            pool.wait_ge(apart, 1)
            g.tensor_copy(q_apart.rearrange("p (b h n) -> p b h n", b=B, h=MH)[:, :, :, 0:T],
                          feats[:, FM:FM + MH, PROMPT:TOKENS].rearrange("p h (b t) -> p b h t", b=B)).then_inc(apart, 1)
            pool.wait_ge(mpv_mm, PTILES)
            for m in range(MT):
                g.memset(p_apart[m], 0.0).then_inc(apart, 1)

            def rows(ring, table, index, s):
                g.indirect_dma_start(ring, None, t[table], bass.IndirectOffsetOnAxis(index, 0)).then_inc(s, 16)

            def gather_u(batch, b, h, index):
                need(pool, dots, 4 * batch + (2 * h - 6))
                alone(pool)
                for j in (2 * h, 2 * h + 1):
                    rows(u_ring[:, b % 2, j, :], "peer_u", index[:, j:j + 1], u_in[b % 2][j])

            def gather_v(batch, h, index):
                need(pool, v_used, 4 * batch + (2 * h - 2))
                alone(pool)
                for j in (2 * h, 2 * h + 1):
                    rows(v_ring[:, j, :], "peer_v", index[:, j:j + 1], v_in[j])

            half = PER_PAIR // 2 * NB
            final = stage_pair[:, 1, half - NB:half]

            def opening(n, index, follows=True):
                for b in range(OPEN):
                    for h in range(2):
                        gather_u(BATCHES * n + b, b, h, index[:, NB * b:NB * b + NB])
                        if b:
                            gather_v(BATCHES * n + (b - 1), h, index[:, NB * (b - 1):NB * b])
                        elif follows:
                            gather_v(BATCHES * n - 1, h, final)

            def tile_e(n, follows=True):
                pool.wait_ge(chosen, PAIRS * n + 1)
                alone(pool)
                g.tensor_copy(stage_open, i_next[:, 0:OPEN * NB]).then_inc(staged, 1)
                pool.wait_ge(staged, STAGES * n + 1)
                opening(n, stage_open, follows)
                pool.wait_ge(moved, n + 1)
                alone(pool)
                g.tensor_copy(final, stage_open[:, NB * (OPEN - 1):NB * OPEN]).then_inc(staged, 1)
                pool.wait_ge(staged, STAGES * n + 2)
                alone(pool)
                with pool.Fori(0, PAIRS) as p:
                    for b in range(PER_PAIR):
                        s, k = divmod(b, PER_PAIR // 2)
                        before, kb = divmod((b - 1) % PER_PAIR, PER_PAIR // 2)
                        batch = BATCHES * n + PER_PAIR * p + (OPEN + b)
                        if k == 0:
                            g.tensor_copy(stage_pair[:, s, :], i_cur[:, bass.ds(PER_PAIR * NB * p + OPEN * NB + half * s, half)])\
                                .then_inc(staged, 1)
                            pool.wait_ge(staged, STAGES * n + 2 * p + (3 + s))
                        for h in range(2):
                            gather_u(batch, b, h, stage_pair[:, s, NB * k:NB * k + NB])
                            gather_v(batch - 1, h, stage_pair[:, before, NB * kb:NB * kb + NB])

            tile_e(0, follows=False)
            with pool.Fori(1, PTILES) as i:
                tile_e(i)
            for h in range(2):
                gather_v(BATCHES * PTILES - 1, h, final)
            pool.wait_ge(packed, PACKED)
            opening(PTILES, i_packed, follows=False)
            for h in range(2):
                gather_v(LAST, h, i_packed[:, NB * (OPEN - 1):NB * OPEN])


def _position_constants():
    slopes = np.exp2(-8.0 * np.arange(1, HEADS + 1, dtype=np.float32) / HEADS).astype(np.float32)
    r, c = np.arange(WINDOW)[:, None], np.arange(2 * WINDOW)[None, :]
    dist = WINDOW + r - c
    valid = (dist >= 0) & (dist <= WINDOW)
    prompt = np.where(valid[:, None, :], -slopes[None, :, None] * dist[:, None, :].astype(np.float32), np.float32(NEG))
    b, g, t = (x.ravel()[:, None] for x in np.meshgrid(np.arange(B), np.arange(GQ), np.arange(T), indexing="ij"))
    sb, st = (x.ravel()[None, :] for x in np.meshgrid(np.arange(B), np.arange(T), indexing="ij"))
    dist = np.concatenate([WINDOW + t - np.arange(WINDOW)[None, :], t - st], 1)
    valid = (dist >= 0) & (dist <= WINDOW) & np.concatenate([np.ones((P, WINDOW), bool), sb == b], 1)
    sample = np.stack([np.where(valid, -slopes[kv * GQ + g] * dist.astype(np.float32), np.float32(NEG))
                       for kv in range(KV)], 1)
    return prompt.astype(np.float32), sample.astype(np.float32)


def kernel(x_prompt, x_sample, cache_swa_k, cache_swa_v, cache_mem_k, cache_mem_v, mem_prompt,
           norm1_g, w_in, b_gate, swa_sinks, chunk_norm_g, chunk_ws, chunk_bs, mem_norm_g, w_mem_kv,
           w_branch_out, w_out, norm2_g, peer_wq, peer_subkeys, peer_u, peer_v, final_norm_g):
    import concourse.bacc as bacc
    from concourse.bass_utils import run_bass_kernel_spmd

    A = np.asarray
    f32 = np.float32

    def on_all(v):
        v = A(v).reshape(1, -1)
        return np.ascontiguousarray(np.broadcast_to(v, (P, v.shape[1])))

    def chunked(w):
        w = A(w)
        return np.ascontiguousarray(w.reshape(-1, P, w.shape[1]).transpose(1, 0, 2))

    def blocks(w):
        w = A(w)
        return w.reshape(-1, P, w.shape[1] // P, P).transpose(2, 1, 0, 3)

    qw = HEADS * HD
    o = np.cumsum([0, qw, KVW, KVW, CW, CW, MW, NBR * D])
    w = A(w_in)[0]
    w_q, w_k, w_v, w_u, w_vc, w_mq, w_g = (w[:, o[n]:o[n + 1]] for n in range(7))
    w_q = w_q.reshape(D, KV, GQ, HD).transpose(0, 2, 1, 3).reshape(D, qw)
    w_b = np.concatenate([blocks(x) for x in (w_q, w_mq, w_k, w_u)], 0)
    br = A(w_branch_out)[0]
    br = np.stack([br[0].reshape(KV, GQ, HD, D).transpose(1, 0, 2, 3).reshape(qw, D), br[1], br[2]], 0)
    gates = np.stack([blocks(w_g[:, j * D:(j + 1) * D]) for j in range(NBR)], 1)
    outs = np.stack([blocks(br[j]) for j in range(NBR)], 1)
    w_d = np.concatenate([gates, outs], 3).reshape(DC * NBR, P, DC + BC, P)
    ws = A(chunk_ws)[0]
    ws_smp = np.zeros((SAMPLE, CG, SAMPLE), f32)
    for b in range(B):
        ws_smp[b * T:(b + 1) * T, :, b * T:(b + 1) * T] = ws[:, :T, :T].transpose(2, 0, 1)
    bs = A(chunk_bs)[0]
    xp = np.zeros((PADDED, D), f32)
    xp[:PROMPT] = A(x_prompt)[0]
    xp[PROMPT:TOKENS] = A(x_sample).reshape(SAMPLE, D)
    sinks = A(swa_sinks)[0]
    kc, vc = A(cache_swa_k)[0].reshape(B, WINDOW, KVW), A(cache_swa_v)[0].reshape(B, WINDOW, KVW)
    mk, mv = A(cache_mem_k)[0], A(cache_mem_v)[0].reshape(B, MT, P, MW)
    prompt_bias, sample_bias = _position_constants()
    arrays = dict(
        x=xp, mem=A(mem_prompt)[0], ident=np.eye(P, dtype=f32),
        idents=np.tile(np.eye(SAMPLE, dtype=f32), (P // SAMPLE, 1)), iota16=on_all(np.arange(K, dtype=f32)),
        norm1_col=A(norm1_g)[0].reshape(DC, P).T, mem_norm_col=A(mem_norm_g)[0].reshape(DC, P).T,
        w_vvc=chunked(np.concatenate([w_v, w_vc], 1)), w_mem=chunked(A(w_mem_kv)[0]),
        swa_bias=prompt_bias, smp_bias=sample_bias, chunk_g=on_all(chunk_norm_g),
        chunk_b=on_all(bs).reshape(P, CG, P), chunk_b_smp=on_all(np.tile(bs[:, None, :T], (1, B, 1))).reshape(P, CG, SAMPLE),
        ws_T=ws.transpose(2, 0, 1), ws_T_smp=ws_smp,
        gate_b=A(b_gate)[0].reshape(NBR, DC, P).transpose(2, 1, 0).reshape(P, DC * NBR),
        sinks=on_all(sinks),
        smp_sinks=np.tile(np.repeat(sinks.reshape(KV, GQ), T, axis=1), (1, B)).T,
        k_cache_T=kc.transpose(2, 0, 1), v_cache=vc.transpose(1, 0, 2), k_cache_rows=kc, v_cache_rows=vc,
        mk_cache_T=mk.transpose(0, 3, 2, 1).reshape(B, P, MH * MEM),
        mv_cache=mv.transpose(0, 2, 1, 3).reshape(B, P, MT * MW),
        w_b=w_b, w_d=w_d, w_out=chunked(A(w_out)[0]), w_q=chunked(A(peer_wq)[0]),
        subT=A(peer_subkeys)[0].transpose(2, 0, 1), norm2_g=on_all(norm2_g), final_g=on_all(final_norm_g),
        peer_u=A(peer_u)[0], peer_v=A(peer_v)[0],
    )
    outputs = dict(
        y=(TOKENS, D), k_prompt=(WINDOW, KVW), v_prompt=(WINDOW, KVW), mk_out=(MEM, MW), mv_out=(MEM, MW),
        k_sample_old=(B, WINDOW - T, KVW), v_sample_old=(B, WINDOW - T, KVW),
        k_sample_new=(SAMPLE, KVW), v_sample_new=(SAMPLE, KVW), vc_out=(SAMPLE, CW),
    )
    nc = bacc.Bacc("TRN2", target_bir_lowering=False, num_devices=1)
    tensors = {}
    for name, a in arrays.items():
        arrays[name] = np.ascontiguousarray(a)
        assert a.dtype == f32, name
        tensors[name] = nc.dram_tensor(name, a.shape, F32, kind="ExternalInput").ap()
    for name, shape in outputs.items():
        tensors[name] = nc.dram_tensor(name, shape, F32, kind="ExternalOutput").ap()
    tensors["m_scratch"] = nc.dram_tensor("m_scratch", (DC, P, PADDED), F32, kind="Internal").ap()
    build(nc, tensors)
    r = run_bass_kernel_spmd(nc, [arrays], core_ids=[0]).results[0]

    def rolled(name):
        new = r[f"{name}_sample_new"].reshape(B, T, KVW)
        return np.concatenate([r[f"{name}_sample_old"], new], 1).reshape(1, B, WINDOW, KV, HD)

    return (r["y"][:PROMPT].reshape(1, PROMPT, D), r["y"][PROMPT:].reshape(B, T, D),
            r["k_prompt"].reshape(1, 1, WINDOW, KV, HD), r["v_prompt"].reshape(1, 1, WINDOW, KV, HD),
            r["mk_out"].reshape(1, 1, MEM, MH, P), r["mv_out"].reshape(1, 1, MEM, MH, P),
            rolled("k"), rolled("v"), r["vc_out"].reshape(1, B, T, CG, P))
```
